# Optimizing a Trainium2 kernel written in Bass

```python
import jax, jax.numpy as jnp
from jax import lax
import numpy as np

D_MODEL = 1024
BATCH = 1
SEQ = 512
DEPTH = 1
DEC_BATCH = 8
DEC_SEQ = 1
PAST_LEN = 2048
PAGE_SIZE = 128

MIX_WIDTH = D_MODEL
HEAD_DIM = 64
ATTN_WIDTH = MIX_WIDTH // 2
N_Q_HEADS = ATTN_WIDTH // HEAD_DIM
N_KV_HEADS = 2
GQA_GROUP = N_Q_HEADS // N_KV_HEADS
KV_WIDTH = N_KV_HEADS * HEAD_DIM
WINDOW = 128
GM_WIDTH = MIX_WIDTH - ATTN_WIDTH
GM_GROUPS = 4
GM_DIM = GM_WIDTH // GM_GROUPS
CHUNK = 128
D_FF = 2816
PLE_DIM = 256
IN_COLS = ATTN_WIDTH + 2 * KV_WIDTH + 2 * GM_WIDTH
SPLITS = (ATTN_WIDTH, ATTN_WIDTH + KV_WIDTH, ATTN_WIDTH + 2 * KV_WIDTH,
          ATTN_WIDTH + 2 * KV_WIDTH + GM_WIDTH)
RMS_EPS = 1e-6
LN_EPS = 1e-5
ATTN_SCALE = HEAD_DIM ** -0.5

kernel_name = "hymba_swa_sink_gmlp_macaron_step"

def rms_norm(x, g):
    xf = x.astype(jnp.float32)
    y = xf * lax.rsqrt(jnp.mean(xf * xf, axis=-1, keepdims=True) + RMS_EPS)
    return (y * g.astype(jnp.float32)).astype(x.dtype)

def layer_norm(x, g, b):
    xf = x.astype(jnp.float32)
    mu = jnp.mean(xf, axis=-1, keepdims=True)
    xc = xf - mu
    y = xc * lax.rsqrt(jnp.mean(xc * xc, axis=-1, keepdims=True) + LN_EPS)
    return (y * g.astype(jnp.float32) + b.astype(jnp.float32)).astype(x.dtype)

def swiglu(x, w1, w3, w2):
    return (jax.nn.silu(x @ w1) * (x @ w3)) @ w2

def sink_softmax(scores, mask, sinks):
    s = jnp.where(mask, scores, -jnp.inf)
    sink = sinks.astype(jnp.float32).reshape(N_KV_HEADS, GQA_GROUP, 1, 1)
    m = jnp.maximum(jnp.max(s, axis=-1, keepdims=True), sink)
    e = jnp.exp(s - m)
    return e / (jnp.sum(e, axis=-1, keepdims=True) + jnp.exp(sink - m))

def window_attn_prompt(q, k, v, sinks):
    B, S = q.shape[:2]
    nb = -(-S // WINDOW)
    pad = nb * WINDOW - S
    qb = jnp.pad(q, ((0, 0), (0, pad), (0, 0), (0, 0), (0, 0))).reshape(
        B, nb, WINDOW, N_KV_HEADS, GQA_GROUP, HEAD_DIM)
    kp = jnp.pad(k, ((0, 0), (WINDOW, pad), (0, 0), (0, 0))).reshape(B, nb + 1, WINDOW, N_KV_HEADS, HEAD_DIM)
    vp = jnp.pad(v, ((0, 0), (WINDOW, pad), (0, 0), (0, 0))).reshape(B, nb + 1, WINDOW, N_KV_HEADS, HEAD_DIM)
    kb = jnp.concatenate([kp[:, :-1], kp[:, 1:]], axis=2)
    vb = jnp.concatenate([vp[:, :-1], vp[:, 1:]], axis=2)
    scores = jnp.einsum('bnqhgd,bnshd->bnhgqs', qb, kb,
                        preferred_element_type=jnp.float32) * ATTN_SCALE
    qi = jnp.arange(WINDOW)[:, None]
    kj = jnp.arange(2 * WINDOW)[None, :]
    rel = kj - WINDOW - qi
    band = (rel <= 0) & (rel >= -WINDOW)
    kpos = (jnp.arange(nb)[:, None] - 1) * WINDOW + jnp.arange(2 * WINDOW)[None, :]
    mask = band[None] & (kpos >= 0)[:, None, :]
    probs = sink_softmax(scores, mask[None, :, None, None], sinks)
    out = jnp.einsum('bnhgqs,bnshd->bnqhgd', probs.astype(v.dtype), vb)
    return out.reshape(B, nb * WINDOW, ATTN_WIDTH)[:, :S]

def window_attn_sample(q, k_new, v_new, k_buf, v_buf, sinks):
    Bd, T = q.shape[:2]
    k_all = jnp.concatenate([k_buf, k_new], axis=1)
    v_all = jnp.concatenate([v_buf, v_new], axis=1)
    scores = jnp.einsum('bqhgd,bshd->bhgqs', q, k_all,
                        preferred_element_type=jnp.float32) * ATTN_SCALE
    j = jnp.arange(T)[:, None]
    c = jnp.arange(WINDOW + T)[None, :]
    rel = c - WINDOW - j
    mask = (rel <= 0) & (rel >= -WINDOW)
    probs = sink_softmax(scores, mask, sinks)
    out = jnp.einsum('bhgqs,bshd->bqhgd', probs.astype(v_all.dtype), v_all)
    return out.reshape(Bd, T, ATTN_WIDTH), k_all[:, T:], v_all[:, T:]

def chunk_spatial_mix(v, w_s, b_s):
    B, S = v.shape[:2]
    nc = -(-S // CHUNK)
    pad = nc * CHUNK - S
    vc = jnp.pad(v, ((0, 0), (0, pad), (0, 0), (0, 0))).reshape(B, nc, CHUNK, GM_GROUPS, GM_DIM)
    w = w_s * jnp.tril(jnp.ones((CHUNK, CHUNK), w_s.dtype))
    out = jnp.einsum('gts,bnsgc->bntgc', w, vc) + jnp.transpose(b_s)[:, :, None]
    return out.reshape(B, nc * CHUNK, GM_GROUPS, GM_DIM)[:, :S]

def decoder_layer(x, ple, attend, g_ffn1, w1_ffn1, w3_ffn1, w2_ffn1, g_mix, w_in, b_in,
                  gm_ln_g, gm_ln_b, gm_w_s, gm_b_s, w_out, b_out,
                  g_ffn2, w1_ffn2, w3_ffn2, w2_ffn2, g_ple, w_ple_gate, w_ple_proj):
    B, S = x.shape[:2]
    x = x + 0.5 * swiglu(rms_norm(x, g_ffn1), w1_ffn1, w3_ffn1, w2_ffn1)
    z = rms_norm(x, g_mix) @ w_in + b_in
    q, k, v, u, vg = jnp.split(z, SPLITS, axis=-1)
    q = q.reshape(B, S, N_KV_HEADS, GQA_GROUP, HEAD_DIM)
    k = k.reshape(B, S, N_KV_HEADS, HEAD_DIM)
    v = v.reshape(B, S, N_KV_HEADS, HEAD_DIM)
    attn_out, k_state, v_state = attend(q, k, v)
    vg = layer_norm(jax.nn.gelu(vg), gm_ln_g, gm_ln_b)
    gm_out = jax.nn.gelu(u) * chunk_spatial_mix(
        vg.reshape(B, S, GM_GROUPS, GM_DIM), gm_w_s, gm_b_s).reshape(B, S, GM_WIDTH)
    x = x + jnp.concatenate([attn_out, gm_out], axis=-1) @ w_out + b_out
    x = x + 0.5 * swiglu(rms_norm(x, g_ffn2), w1_ffn2, w3_ffn2, w2_ffn2)
    gate = jax.nn.sigmoid(rms_norm(x, g_ple) @ w_ple_gate)
    x = x + gate * (ple @ w_ple_proj)
    return x, k_state, v_state, vg

def setup_inputs(seed: int = 0) -> dict:
    key = jax.random.key(seed)
    ks = iter(jax.random.split(key, 40))
    f32 = jnp.float32
    L, D, F = DEPTH, D_MODEL, D_FF

    def nrm(shape, scale):
        return jax.random.normal(next(ks), shape, f32) * scale

    def gain(shape):
        return 1.0 + nrm(shape, 0.05)

    return {
        "x_prompt": nrm((BATCH, SEQ, D), 1.0),
        "x_sample": nrm((DEC_BATCH, DEC_SEQ, D), 1.0),
        "cache_k_win": nrm((L, DEC_BATCH, WINDOW, N_KV_HEADS, HEAD_DIM), 1.0),
        "cache_v_win": nrm((L, DEC_BATCH, WINDOW, N_KV_HEADS, HEAD_DIM), 1.0),
        "p_prompt": nrm((L, BATCH, SEQ, PLE_DIM), 1.0),
        "p_sample": nrm((L, DEC_BATCH, DEC_SEQ, PLE_DIM), 1.0),
        "g_ffn1": gain((L, D)),
        "w1_ffn1": nrm((L, D, F), D ** -0.5),
        "w3_ffn1": nrm((L, D, F), D ** -0.5),
        "w2_ffn1": nrm((L, F, D), F ** -0.5),
        "g_mix": gain((L, D)),
        "w_in": nrm((L, D, IN_COLS), D ** -0.5),
        "b_in": nrm((L, IN_COLS), 0.02),
        "attn_sinks": nrm((L, N_Q_HEADS), 0.5),
        "gm_ln_g": gain((L, GM_WIDTH)),
        "gm_ln_b": nrm((L, GM_WIDTH), 0.02),
        "gm_w_s": nrm((L, GM_GROUPS, CHUNK, CHUNK), CHUNK ** -0.5),
        "gm_b_s": 1.0 + nrm((L, GM_GROUPS, CHUNK), 0.1),
        "w_out": nrm((L, MIX_WIDTH, D), MIX_WIDTH ** -0.5),
        "b_out": nrm((L, D), 0.02),
        "g_ffn2": gain((L, D)),
        "w1_ffn2": nrm((L, D, F), D ** -0.5),
        "w3_ffn2": nrm((L, D, F), D ** -0.5),
        "w2_ffn2": nrm((L, F, D), F ** -0.5),
        "g_ple": gain((L, D)),
        "w_ple_gate": nrm((L, D, D), D ** -0.5),
        "w_ple_proj": nrm((L, PLE_DIM, D), PLE_DIM ** -0.5),
        "g_final": gain((D,)),
    }

def reference(x_prompt, x_sample, cache_k_win, cache_v_win, p_prompt, p_sample,
              g_ffn1, w1_ffn1, w3_ffn1, w2_ffn1, g_mix, w_in, b_in, attn_sinks,
              gm_ln_g, gm_ln_b, gm_w_s, gm_b_s, w_out, b_out,
              g_ffn2, w1_ffn2, w3_ffn2, w2_ffn2, g_ple, w_ple_gate, w_ple_proj, g_final):
    xp, xs = x_prompt, x_sample
    kp_list, vp_list, ks_list, vs_list, gp_list, gs_list = [], [], [], [], [], []
    last_chunk_start = ((SEQ - 1) // CHUNK) * CHUNK
    for i in range(DEPTH):
        w = (g_ffn1[i], w1_ffn1[i], w3_ffn1[i], w2_ffn1[i], g_mix[i], w_in[i], b_in[i],
             gm_ln_g[i], gm_ln_b[i], gm_w_s[i], gm_b_s[i], w_out[i], b_out[i],
             g_ffn2[i], w1_ffn2[i], w3_ffn2[i], w2_ffn2[i], g_ple[i], w_ple_gate[i], w_ple_proj[i])
        sinks = attn_sinks[i]
        kb, vb = cache_k_win[i], cache_v_win[i]

        def attend_prompt(q, k, v, sinks=sinks):
            return window_attn_prompt(q, k, v, sinks), k[:, -WINDOW:], v[:, -WINDOW:]

        def attend_sample(q, k, v, sinks=sinks, kb=kb, vb=vb):
            return window_attn_sample(q, k, v, kb, vb, sinks)

        xp, kp_new, vp_new, gvp = decoder_layer(xp, p_prompt[i], attend_prompt, *w)
        xs, ks_new, vs_new, gvs = decoder_layer(xs, p_sample[i], attend_sample, *w)
        kp_list.append(kp_new)
        vp_list.append(vp_new)
        ks_list.append(ks_new)
        vs_list.append(vs_new)
        gp_list.append(gvp[:, last_chunk_start:])
        gs_list.append(gvs)
    y_prompt = rms_norm(xp, g_final)
    y_sample = rms_norm(xs, g_final)
    k_win_prompt = jnp.stack(kp_list)
    v_win_prompt = jnp.stack(vp_list)
    k_win_sample = jnp.stack(ks_list)
    v_win_sample = jnp.stack(vs_list)
    gm_v_prompt = jnp.stack(gp_list)
    gm_v_sample = jnp.stack(gs_list)
    return (y_prompt, y_sample, k_win_prompt, v_win_prompt, k_win_sample, v_win_sample, gm_v_prompt, gm_v_sample)


_drawn_inputs = setup_inputs


def setup_inputs(seed=0):
    import zlib

    import numpy as np

    out = dict(_drawn_inputs(seed))
    spreads = {}
    factors = {'attn_sinks': 8.0, 'gm_ln_b': 2.855, 'b_out': 3.337, 'g_ffn2': 3.458, 'g_ple': 169.957}
    for name, (base, spread) in spreads.items():
        noise = np.random.default_rng([zlib.crc32(name.encode()), seed]).standard_normal(out[name].shape)
        drawn = base * np.exp(spread * noise) if base else spread * noise
        out[name] = __import__('jax').numpy.asarray(drawn.astype(out[name].dtype))
    for name, factor in factors.items():
        out[name] = (out[name] * factor).astype(out[name].dtype)
    return out
```

```python
from contextlib import ExitStack

import concourse.bass as bass
from concourse import mybir

F32 = mybir.dt.float32
F32R = mybir.dt.float32r
I32 = mybir.dt.int32
ALU = mybir.AluOpType
ACT = mybir.ActivationFunctionType
AX_X = mybir.AxisListType.X

P = 128
D, FF, PLE = 1024, 2816, 256
TP, TS = 512, 8
T = TP + TS
HALF = T // 2
NB = TP // P
KD, KF, KP = D // P, FF // P, PLE // P
HD, NQ, NKV, GQ = 64, 8, 2, 4
GM, GG = 512, 4
W = 128
RMS_EPS, LN_EPS = 1e-6, 1e-5
SCALE = HD ** -0.5
NEG = -1.0e30
GELU_C = 0.7978845608028654
RSQRT_SEED = 1597463007.0

RING = 3
UP1 = 0
DOWN1 = UP1 + 2 * KF
IN = DOWN1 + 3 * KD
OUT = IN + 14
UP2 = OUT + KD
DOWN2 = UP2 + 2 * KF
LAST = DOWN2 + 3 * KD
END = LAST + KD + 2
DOWN_K = (8, 8, 6)

IN_ORDER = ("g0", "g1", "k", "v", "q0", "g2", "q1", "g3", "q2", "q3", "u0", "u1", "u2", "u3")
IN_PAIR = (0, 1, 2, 0, 1, 0, 1, 0, 1, 0, 1, 0, 1, 0)
C_BOUT, C_Q, C_K, C_V, C_U, C_G, N_COLS = 32, 40, 44, 45, 46, 50, 54


def mixer_steps():
    extra = {
        (0, 8): [("stat_sum",)],
        (1, 2): [("cache_turn",)],
        (1, 8): [("stat_spread",), ("evac", 0)],
        (2, 3): [("ws_turn",)],
        (2, 7): [("g_turn", 0), ("evac", 1)],
        (3, 6): [("g_turn", 1)],
        (4, 6): [("kv_turn",)],
        (6, 6): [("g_turn", 2)],
        (8, 6): [("g_turn", 3)],
        (9, 6): [("norm_stats",)],
        (10, 3): [("norm", 0), ("norm", 1)],
        (10, 7): [("norm", 2), ("norm", 3), ("norm", 4)],
        (11, 4): [("s_scores",)],
        (11, 6): [("s_softmax",)],
        (12, 2): [("s_probs",)],
        (12, 4): [("s_values",)],
        (11, 5): [("spatial", 0), ("gm", 0)],
        (12, 6): [("spatial", 1), ("gm", 1)],
        (13, 2): [("spatial", 2), ("gm", 2)],
        (13, 5): [("spatial", 3)],
    }
    for i in range(8):
        extra.setdefault((5 + i, 0), []).insert(0, ("scores", i))
        extra.setdefault((6 + i, 1), []).insert(0, ("p_turn", i, 0))
        extra.setdefault((6 + i, 3), []).insert(0, ("p_turn", i, 1))
        extra.setdefault((6 + i, 5), []).insert(0, ("values", i))
        extra.setdefault((6 + i, 7), []).insert(0, ("o_turn", i))
    steps = []
    for u in range(14):
        for k in range(KD):
            steps += extra.pop((u, k), [])
            steps.append(("gemm", u, k))
        steps += extra.pop((u, KD), [])
        if u > 1:
            steps.append(("evac", u))
    assert not extra, extra
    return steps + [("gm", 3)]


def hybrid_decoder_layer(nc, a, o):
    steps = mixer_steps()
    with ExitStack() as ctx:
        def sb(name, shape, dt=F32, scope=ctx):
            return scope.enter_context(nc.sbuf_tensor(name, shape, dt))

        def sem(name):
            return ctx.enter_context(nc.semaphore(name))

        x = sb("x", [P, KD, T])
        xg_hi = sb("xg_hi", [P, KD, T], F32R)
        xg_lo = sb("xg_lo", [P, KD, T], F32R)
        w_raw = sb("w_raw", [P, RING, KD * P])
        w_hi = sb("w_hi", [P, RING, KD * P], F32R)
        w_lo = sb("w_lo", [P, RING, KD * P], F32R)
        ta = sb("ta", [P, T])
        tb = sb("tb", [P, T])
        tq = sb("tq", [P, T])
        rstd = sb("rstd", [P, T])
        sq = sb("sq", [P, T])
        ssq = sb("ssq", [P, T])
        diag = sb("diag", [P, T])
        ident = sb("ident", [P, P])
        ones = sb("ones", [P, P])
        p_t = sb("p_t", [P, KP, T])
        cols = sb("cols", [P, 64])
        var = sb("var", [P, 8])
        rs = sb("rs", [P, 8])
        rs_i = sb("rs_i", [P, 8], I32)
        rs_t = sb("rs_t", [P, 8])

        with ExitStack() as s:
            x_rows = sb("x_rows", [P, NB, D], scope=s)
            xs_rows = sb("xs_rows", [P, D], scope=s)
            rows = sb("rows", [64, P], scope=s)
        with ExitStack() as s:
            h1 = sb("h1_hi", [P, KF, T], F32R, s), sb("h1_lo", [P, KF, T], F32R, s)
            p_rows = sb("p_rows", [P, NB, PLE], scope=s)
            ps_rows = sb("ps_rows", [P, PLE], scope=s)
        with ExitStack() as s:
            mix_hi = sb("mix_hi", [P, 8, T], F32R, s)
            mix_lo = sb("mix_lo", [P, 8, T], F32R, s)
            q_t = sb("q_t", [P, GQ, T], scope=s)
            k_t = sb("k_t", [P, T], scope=s)
            v_t = sb("v_t", [P, T], scope=s)
            g_rows = sb("g_rows", [P, NB + 1, GM], scope=s)
            v_rows = sb("v_rows", [P, NB + 1, P], scope=s)
            k_rows = sb("k_rows", [P, 2, P], scope=s)
            ws_t = sb("ws_t", [P, GG, P], scope=s)
            bs_all = sb("bs_all", [P, GG, P], scope=s)
            lng = sb("lng", [P, GM], scope=s)
            lnb = sb("lnb", [P, GM], scope=s)
            probs = sb("probs", [P, 2, NKV, 2, 2 * W], scope=s)
            probs_t = sb("probs_t", [P, 2, NKV, 2, P], scope=s)
            o_rows = sb("o_rows", [P, 2, NKV, HD], scope=s)
            mask = sb("mask", [P, 2, 2 * W], scope=s)
            cache_k_t = sb("cache_k_t", [P, TS, W], scope=s)
            cache_v = sb("cache_v", [P, TS, W], scope=s)
            neg_sink = sb("neg_sink", [P, NQ], scope=s)
            sink = sb("sink", [P, NQ], scope=s)
            st = sb("st", [P, 32], scope=s)
            bn = sb("bn", [P, NB + 1, 6], scope=s)
            mv = sb("mv", [P, NB + 1, 2], scope=s)
            w00 = sb("w00", [TS, GG], scope=s)
            w00_diag = sb("w00_diag", [TS, GG, TS], scope=s)
            s_sink = sb("s_sink", [64, 1], scope=s)
            s_st = sb("s_st", [64, 8], scope=s)
            q_diag = sb("q_diag", [P, TS, NQ], scope=s)
            qk_new = sb("qk_new", [P, TS, NQ], scope=s)
            s_keys = sb("s_keys", [P, 64], scope=s)
            s_p = sb("s_p", [64, W + 1], scope=s)
            s_new = sb("s_new", [64, 64], scope=s)
            s_pt = sb("s_pt", [P, 64], scope=s)
            s_pv = sb("s_pv", [P, TS, NQ], scope=s)
            s_o = sb("s_o", [P, TS, NQ], scope=s)
            with ExitStack() as early:
                cache_k = sb("cache_k", [P, TS, W], scope=early)
                ws_rows = sb("ws_rows", [P, GG, P], scope=early)
                g_t = sb("g_t", [P, T], scope=early)
            gu = sb("gu", [P, 2, T], scope=s)
            sp = sb("sp", [P, T], scope=s)
        with ExitStack() as s:
            h2 = sb("h2_hi", [P, KF, T], F32R, s), sb("h2_lo", [P, KF, T], F32R, s)
        with ExitStack() as s:
            p_hi = sb("p_hi", [P, KP, T], F32R, s)
            p_lo = sb("p_lo", [P, KP, T], F32R, s)
            pp = sb("pp", [P, KD, T], scope=s)
            g_fin = sb("g_fin", [P, D], scope=s)
            y = sb("y", [P, NB + 1, D], scope=s)

        ps = ctx.enter_context(nc.psum_tensor("ps", [P, 8, 512], F32))

        raw_in = [sem(f"raw_in{i}") for i in range(RING)]
        w_hi_ready, w_lo_ready = sem("w_hi_ready"), sem("w_lo_ready")
        unit_done = sem("unit_done")
        x_in = [sem(f"x_in{i}") for i in range(NB + 1)]
        p_in, ps_in = sem("p_in"), sem("ps_in")
        rows_in = sem("rows_in")
        consts_ready = sem("consts_ready")
        cols_turned, cols_ready = sem("cols_turned"), sem("cols_ready")
        x_turned = sem("x_turned")
        x_ready = sem("x_ready")
        xg_hi_ready, xg_lo_ready = sem("xg_hi_ready"), sem("xg_lo_ready")
        p_turned, p_ready = sem("p_turned"), sem("p_ready")
        sq_cleared, sq_made, sq_added = sem("sq_cleared"), sem("sq_made"), sem("sq_added")
        stat_summed, diag_ready = sem("stat_summed"), sem("diag_ready")
        stat_spread, rstd_ready = sem("stat_spread"), sem("rstd_ready")
        dve_step = sem("dve_step")
        a_ready, tanh_ready = sem("a_ready"), sem("tanh_ready")
        ab_ready, ab_scaled = sem("ab_ready"), sem("ab_scaled")
        h_ready, h_hi_ready, h_lo_ready = sem("h_ready"), sem("h_hi_ready"), sem("h_lo_ready")
        mix_in = sem("mix_in")
        cache_in, ws_in = sem("cache_in"), sem("ws_in")
        mask_ready = sem("mask_ready")
        z_scaled, z_done = sem("z_scaled"), sem("z_done")
        gelu_sq, gelu_arg, gelu_tanh = sem("gelu_sq"), sem("gelu_arg"), sem("gelu_tanh")
        gelu_done = sem("gelu_done")
        cache_turned, cache_taken = sem("cache_turned"), sem("cache_taken")
        ws_turned, ws_taken, ws_ready = sem("ws_turned"), sem("ws_taken"), sem("ws_ready")
        g_turned, g_taken = sem("g_turned"), sem("g_taken")
        kv_turned, kv_taken = sem("kv_turned"), sem("kv_taken")
        g_normed = sem("g_normed")
        scored, masked, max_ready = sem("scored"), sem("masked"), sem("max_ready")
        exp_done, sum_ready = sem("exp_done"), sem("sum_ready")
        probs_turned = sem("probs_turned")
        probs_taken = sem("probs_taken0"), sem("probs_taken1")
        o_made, o_taken = sem("o_made"), sem("o_taken")
        o_turned, o_hi, o_lo = sem("o_turned"), sem("o_hi"), sem("o_lo")
        spatial_made, spatial_taken = sem("spatial_made"), sem("spatial_taken")
        gm_ready, gm_hi, gm_lo = sem("gm_ready"), sem("gm_hi"), sem("gm_lo")
        w00_ready = sem("w00_ready")
        s_built, s_scored, s_taken = sem("s_built"), sem("s_scored"), sem("s_taken")
        s_turned, s_max, s_exp, s_normed = sem("s_turned"), sem("s_max"), sem("s_exp"), sem("s_normed")
        s_diag_clear = sem("s_diag_clear")
        s_p_turned, s_p_taken = sem("s_p_turned"), sem("s_p_taken")
        s_valued, s_out, s_hi, s_lo = sem("s_valued"), sem("s_out"), sem("s_hi"), sem("s_lo")
        pple_hi, pple_lo, pp_made, pp_ready = sem("pple_hi"), sem("pple_lo"), sem("pp_made"), sem("pp_ready")
        z_ready, gate_ready, gated = sem("z_ready"), sem("gate_ready"), sem("gated")
        g_fin_in = sem("g_fin_in")
        y_turned, y_ready = sem("y_turned"), sem("y_ready")
        out_done = sem("out_done")

        def pair(i, width=HALF):
            return ps[:, 2 * i:2 * i + 2, 0:width]

        def halves(ap):
            return ap.rearrange("p (h t) -> p h t", h=2)

        def at(n, step, it):
            return n if it is None else it * step + n

        def tile_of(t, m, step, it):
            if it is None:
                return t[:, m, :]
            return t[:, bass.ds(it * step + m, 1), :].rearrange("p a t -> p (a t)")

        def col(c, step=0, it=None):
            return cols[:, c:c + 1] if it is None else cols[:, bass.ds(it * step + c, 1)]

        w_dram = {n: a[n][0].rearrange("(k p) c -> p k c", p=P)
                  for n in ("w1_ffn1", "w3_ffn1", "w2_ffn1", "w_in", "w_out", "w1_ffn2", "w3_ffn2",
                            "w2_ffn2", "w_ple_gate", "w_ple_proj")}
        mix_loads = 6 + TS

        block = ctx.enter_context(nc.Block())

        @block.sync
        def _(sp_):
            def load(n, step, it, src, width=KD * P):
                if n >= RING:
                    sp_.wait_ge(w_lo_ready, at(n - RING + 1, step, it))
                dst = w_raw[:, n % RING, 0:width]
                dst = dst.rearrange("p (k c) -> p k c", k=src.shape[1])
                sp_.dma_start(dst, src).then_inc(raw_in[n % RING], 16)

            def up_step(base, ws, f, it):
                for i, w in enumerate(ws):
                    c = bass.ds(at(f * P, 3 * P, it), P) if it is not None else slice(f * P, f * P + P)
                    load(base + 2 * f + i, 6, it, w_dram[w][:, :, c])

            def down_step(base, w, m, it):
                c = bass.ds(at(m * P, 2 * P, it), P)
                for i, kn in enumerate(DOWN_K):
                    load(base + 3 * m + i, 6, it, w_dram[w][:, 8 * i:8 * i + kn, c], kn * P)

            def ffn(up, down, w1, w3, w2, first=0):
                for f in range(1 if first else 0, 4):
                    up_step(up, (w1, w3), f, None)
                with sp_.Fori(0, (KF - 4) // 3) as it:
                    for r in range(3):
                        up_step(up, (w1, w3), 4 + r, it)
                if first:
                    sp_.wait_ge(x_turned, KD)
                    sp_.dma_start(p_rows[:], a["p_prompt"][0, 0].rearrange("(b p) c -> p b c", p=P)).then_inc(p_in, 16)
                    sp_.dma_start(ps_rows[0:TS, :], a["p_sample"][0].rearrange("b t c -> (b t) c")).then_inc(ps_in, 16)
                with sp_.Fori(0, KD // 2) as it:
                    for r in range(2):
                        down_step(down, w2, r, it)

            r0 = 0
            for name in ("g_ffn1", "g_mix", "g_ffn2", "g_ple", "b_out"):
                sp_.dma_start(rows[r0:r0 + 8, :], a[name][0].rearrange("(k p) -> k p", p=P)).then_inc(rows_in, 16)
                r0 += 8
            b_in = a["b_in"][0]
            for c in range(NKV):
                sp_.dma_start(rows[C_Q:C_Q + GQ, c * HD:(c + 1) * HD],
                              b_in[c * GQ * HD:(c + 1) * GQ * HD].rearrange("(j d) -> j d", d=HD)).then_inc(rows_in, 16)
            sp_.dma_start(rows[C_K:N_COLS, :], b_in[512:1792].rearrange("(k p) -> k p", p=P)).then_inc(rows_in, 16)
            for b in range(NB):
                sp_.dma_start(x_rows[:, b, :], a["x_prompt"][0, b * P:(b + 1) * P, :]).then_inc(x_in[b], 16)
            sp_.dma_start(xs_rows[0:TS, :], a["x_sample"].rearrange("b t d -> (b t) d")).then_inc(x_in[NB], 16)
            up_step(UP1, ("w1_ffn1", "w3_ffn1"), 0, None)
            ffn(UP1, DOWN1, "w1_ffn1", "w3_ffn1", "w2_ffn1", first=1)

            offset = {"q": 0, "k": 512, "v": 640, "u": 768, "g": 1280}
            for u, name in enumerate(IN_ORDER):
                c0 = offset[name[0]] + (int(name[1]) * P if name[0] in "ug" else 0)
                if name[0] == "q":
                    n, j = IN + u, int(name[1])
                    sp_.wait_ge(w_lo_ready, n - RING + 1)
                    for c in range(NKV):
                        src = w_dram["w_in"][:, :, c * 256 + j * HD:c * 256 + (j + 1) * HD]
                        dst = w_raw[:, n % RING, :].rearrange("p (k c d) -> p k c d", k=KD, c=NKV)[:, :, c, :]
                        sp_.dma_start(dst, src).then_inc(raw_in[n % RING], 16)
                else:
                    load(IN + u, 0, None, w_dram["w_in"][:, :, c0:c0 + P])
            wo = a["w_out"][0]
            for m in range(KD):
                n = OUT + m
                sp_.wait_ge(w_lo_ready, n - RING + 1)
                dst = w_raw[:, n % RING, :].rearrange("p (k c) -> p k c", k=KD)
                for c in range(NKV):
                    sp_.dma_start(dst[c * HD:(c + 1) * HD, 0:4, :],
                                  wo[c * 256:(c + 1) * 256, m * P:(m + 1) * P].rearrange("(j d) c -> d j c", d=HD)
                                  ).then_inc(raw_in[n % RING], 16)
                sp_.dma_start(dst[:, 4:8, :], wo[512:1024, m * P:(m + 1) * P].rearrange("(j d) c -> d j c", d=P)
                              ).then_inc(raw_in[n % RING], 16)

            ffn(UP2, DOWN2, "w1_ffn2", "w3_ffn2", "w2_ffn2")

            load(LAST, 0, None, w_dram["w_ple_gate"][:, :, 0:P])
            for i in range(2):
                load(LAST + 1 + i, 0, None, w_dram["w_ple_proj"][:, :, 512 * i:512 * (i + 1)])
            for m in range(1, KD):
                load(LAST + 2 + m, 0, None, w_dram["w_ple_gate"][:, :, m * P:(m + 1) * P])

            for b in range(NB):
                sp_.wait_ge(y_ready, b + 1)
                sp_.dma_start(o["y_prompt"][0, b * P:(b + 1) * P, :], y[:, b, :]).then_inc(out_done, 16)
            sp_.wait_ge(y_ready, NB + 1)
            sp_.dma_start(o["y_sample"].rearrange("b t d -> (b t) d"), y[0:TS, NB, :]).then_inc(out_done, 16)
            sp_.wait_ge(out_done, 16 * 13)

        def parts(n):
            if IN <= n < OUT and IN_ORDER[n - IN][0] == "q":
                return NKV
            return 3 if OUT <= n < UP2 else 1

        def arrived(n):
            return 16 * sum(parts(m) for m in range(n % RING, n + 1, RING))

        @block.scalar
        def _(act):
            def split_hi(n, step=0, it=None):
                if n >= END:
                    return
                act.wait_ge(raw_in[n % RING], at(arrived(n), 16 * step // RING, it))
                if n >= RING:
                    act.wait_ge(unit_done, at(n - RING + 1, step, it))
                nc.scalar.activation(w_hi[:, n % RING, :], w_raw[:, n % RING, :], ACT.Copy).then_inc(w_hi_ready, 1)

            def x_hi(stat, m, step=0, it=None):
                act.wait_ge(x_ready, at(8 * stat + m + 1, step, it))
                nc.scalar.activation(tile_of(xg_hi, m, step, it), tile_of(x, m, step, it), ACT.Copy,
                                     scale=col(8 * stat + m, step, it)).then_inc(xg_hi_ready, 1)

            def spread(stat):
                act.wait_ge(stat_spread, stat + 1)
                nc.scalar.activation(rstd[:, 0:TP], ps[:, 6, :], ACT.Copy).then_inc(rstd_ready, 1)
                nc.scalar.activation(rstd[:, TP:T], ps[:, 7, 8:8 + TS], ACT.Copy).then_inc(rstd_ready, 1)

            def up_step(base, f0, h, f, it):
                split_hi(base + 2 * f + 3, 6, it)
                if f0 + f:
                    act.wait_ge(h_ready, at(f0 + f, 3, it))
                act.wait_ge(a_ready, at(f0 + f + 1, 3, it))
                nc.scalar.activation(tb[:], ta[:], ACT.Tanh, scale=0.5).then_inc(tanh_ready, 1)
                split_hi(base + 2 * f + 4, 6, it)
                act.wait_ge(h_ready, at(f0 + f + 1, 3, it))
                nc.scalar.activation(tile_of(h[0], f, 3, it), tq[:], ACT.Copy).then_inc(h_hi_ready, 1)

            def ffn(up, down, f0, h, stat):
                spread(stat)
                up_step(up, f0, h, 0, None)
                with act.Fori(0, (KF - 1) // 3) as it:
                    for r in range(3):
                        up_step(up, f0, h, 1 + r, it)
                with act.Fori(0, KD // 2) as it:
                    for m in range(2):
                        for c in range(3):
                            split_hi(down + 3 * m + 3 + c, 6, it)
                        x_hi(stat + 1, m, 2, it)

            for n in range(RING):
                split_hi(n)
            act.wait_ge(cols_ready, 1)
            for m in range(KD):
                x_hi(0, m)
            ffn(UP1, DOWN1, 0, h1, 0)

            act.wait_ge(unit_done, IN)
            act.dma_start(cache_k[:], a["cache_k_win"][0].rearrange("b w h d -> w b (h d)")).then_inc(cache_in, 16)
            act.dma_start(ws_rows[:], a["gm_w_s"][0].rearrange("g t s -> t g s")).then_inc(ws_in, 16)
            for dst, src in (
                (sink[:], a["attn_sinks"][0].partition_broadcast(P)),
                (cache_v[:], a["cache_v_win"][0].rearrange("b w h d -> w b (h d)")),
                (bs_all[:], a["gm_b_s"][0].partition_broadcast(P)),
                (lng[:], a["gm_ln_g"][0].partition_broadcast(P)),
                (lnb[:], a["gm_ln_b"][0].partition_broadcast(P)),
            ):
                act.dma_start(dst, src).then_inc(mix_in, 16)
            act.dma_start(w00[:], a["gm_w_s"][0, :, 0, 0].partition_broadcast(TS),
                          allow_slow_non_contiguous=True).then_inc(mix_in, 16)
            for r in range(TS):
                act.dma_start(s_sink[r * NQ:(r + 1) * NQ, :],
                              a["attn_sinks"][0].rearrange("(h o) -> h o", o=1)).then_inc(mix_in, 16)
            for dst, src in ((o["k_win_sample"], a["cache_k_win"]), (o["v_win_sample"], a["cache_v_win"])):
                act.dma_start(dst[0, :, 0:W - 1].rearrange("b w h d -> b (w h d)"),
                              src[0, :, 1:W].rearrange("b w h d -> b (w h d)")).then_inc(out_done, 16)

            n_gelu = 0
            for kind, *arg in steps:
                if kind == "gemm" and arg[1] == 0 and arg[0] > 0:
                    split_hi(IN + arg[0] + 2)
                elif kind == "stat_spread":
                    spread(1)
                elif kind == "cache_turn":
                    act.wait_ge(cache_turned, 1)
                    nc.scalar.activation(cache_k_t[:], ps[:, 4:6, :].rearrange("p a (b w) -> p (a b) w", w=W),
                                         ACT.Copy).then_inc(cache_taken, 1)
                elif kind == "ws_turn":
                    act.wait_ge(ws_turned, 1)
                    nc.scalar.activation(ws_t[:], ps[:, 6, :].rearrange("p (g s) -> p g s", g=GG),
                                         ACT.Copy).then_inc(ws_taken, 1)
                elif kind == "evac":
                    u, name = arg[0], IN_ORDER[arg[0]]
                    j = int(name[1:] or 0)
                    bias = col({"q": C_Q, "k": C_K, "v": C_V, "u": C_U, "g": C_G}[name[0]] + j)
                    act.wait_ge(z_scaled, u + 1)
                    if name[0] in "ug":
                        if n_gelu:
                            act.wait_ge(gelu_done, n_gelu)
                        n_gelu += 1
                        nc.scalar.activation(tb[:], ta[:], ACT.Square, bias=bias).then_inc(gelu_sq, 1)
                        nc.scalar.activation(tq[:], ta[:], ACT.Identity, bias=bias).then_inc(z_done, 1)
                        act.wait_ge(gelu_arg, n_gelu)
                        nc.scalar.activation(tb[:], tb[:], ACT.Tanh).then_inc(gelu_tanh, 1)
                    else:
                        dst = {"q": q_t[:, j, :], "k": k_t[:], "v": v_t[:]}[name[0]]
                        nc.scalar.activation(dst, ta[:], ACT.Identity, bias=bias).then_inc(z_done, 1)
                elif kind == "g_turn":
                    g = arg[0]
                    bank = 4 if g else 6
                    act.wait_ge(g_turned, g + 1)
                    nc.scalar.activation(g_rows[:, 0:NB, g * P:(g + 1) * P],
                                         ps[:, bank, :].rearrange("p (b c) -> p b c", c=P), ACT.Copy)
                    nc.scalar.activation(g_rows[0:TS, NB, g * P:(g + 1) * P], ps[0:TS, bank + 1, 0:P],
                                         ACT.Copy).then_inc(g_taken, 1)
                elif kind == "kv_turn":
                    act.wait_ge(kv_turned, 1)
                    nc.scalar.activation(v_rows[:, 0:NB, :], ps[:, 6, :].rearrange("p (b c) -> p b c", c=P),
                                         ACT.Copy).then_inc(kv_taken, 1)
                    nc.scalar.activation(v_rows[0:TS, NB, :], ps[0:TS, 7, 0:P], ACT.Copy).then_inc(kv_taken, 1)
                    nc.scalar.activation(k_rows[:, 0, :], ps[:, 7, P:2 * P], ACT.Copy).then_inc(kv_taken, 1)
                    nc.scalar.activation(k_rows[0:TS, 1, :], ps[0:TS, 7, 2 * P:3 * P], ACT.Copy).then_inc(kv_taken, 1)
                    act.wait_ge(kv_taken, 4)
                    act.dma_start(o["v_win_prompt"][0, 0].rearrange("w h d -> w (h d)"), v_rows[:, NB - 1, :]
                                  ).then_inc(out_done, 16)
                    act.dma_start(o["k_win_prompt"][0, 0].rearrange("w h d -> w (h d)"), k_rows[:, 0, :]
                                  ).then_inc(out_done, 16)
                    act.dma_start(o["v_win_sample"][0, :, W - 1].rearrange("b h d -> b (h d)"), v_rows[0:TS, NB, :]
                                  ).then_inc(out_done, 16)
                    act.dma_start(o["k_win_sample"][0, :, W - 1].rearrange("b h d -> b (h d)"), k_rows[0:TS, 1, :]
                                  ).then_inc(out_done, 16)
                elif kind == "scores":
                    i = arg[0]
                    c0 = 16 * (i % 2)
                    act.wait_ge(max_ready, i + 1)
                    for c in range(4):
                        item = probs[:, i % 2, c // 2, c % 2, :]
                        nc.scalar.activation(item, item, ACT.Exp, bias=st[:, c0 + c:c0 + c + 1],
                                             accum_out=st[:, c0 + 8 + c:c0 + 9 + c]).then_inc(exp_done, 1)
                    nc.scalar.activation(st[:, c0 + 4:c0 + 8], st[:, c0 + 4:c0 + 8], ACT.Exp).then_inc(exp_done, 1)
                elif kind == "p_turn" and arg[1] == 1:
                    i = arg[0]
                    act.wait_ge(probs_turned, 2 * i + 2)
                    nc.scalar.activation(probs_t[:, 1].rearrange("p c k q -> p (c k q)"), ps[:, 6, :],
                                         ACT.Copy).then_inc(probs_taken[1], 1)
                elif kind == "o_turn":
                    i = arg[0]
                    act.wait_ge(o_turned, i + 1)
                    nc.scalar.activation(mix_hi[:, i // 2, 256 * (i % 2):256 * (i % 2) + 256], ps[:, 7, 256:512],
                                         ACT.Copy).then_inc(o_hi, 1)
                elif kind == "norm" and arg[0] >= NB - 1:
                    b = arg[0]
                    act.wait_ge(g_normed, b + 1)
                    if b == NB - 1:
                        act.dma_start(o["gm_v_prompt"][0, 0], g_rows[:, b, :]).then_inc(out_done, 16)
                    else:
                        act.dma_start(o["gm_v_sample"][0].rearrange("b t c -> (b t) c"), g_rows[0:TS, b, :]
                                      ).then_inc(out_done, 16)
                elif kind == "gm":
                    g = arg[0]
                    act.wait_ge(gm_ready, g + 1)
                    nc.scalar.activation(mix_hi[:, 4 + g, :], sp[:], ACT.Copy, scale=0.5).then_inc(gm_hi, 1)
                elif kind == "s_softmax":
                    act.wait_ge(s_max, 1)
                    nc.scalar.activation(s_p[:], s_p[:], ACT.Exp, bias=s_st[:, 0:1],
                                         accum_out=s_st[:, 2:3]).then_inc(s_exp, 1)
                    nc.scalar.activation(s_st[:, 1:2], s_st[:, 1:2], ACT.Exp).then_inc(s_exp, 1)
                elif kind == "s_values":
                    act.wait_ge(s_out, 1)
                    for c in range(NKV):
                        part = slice(c * HD, (c + 1) * HD)
                        nc.scalar.activation(mix_hi[part, 0:4, TP:T],
                                             s_o[part, :, c * GQ:(c + 1) * GQ].rearrange("p s j -> p j s"),
                                             ACT.Copy).then_inc(s_hi, 1)

            split_hi(OUT + 2)
            for m in range(KD):
                split_hi(OUT + m + 3)
                x_hi(2, m)
            act.wait_ge(out_done, 16 * 8)
            ffn(UP2, DOWN2, KF, h2, 2)

            act.wait_ge(unit_done, LAST)
            act.dma_start(g_fin[:], a["g_final"].partition_broadcast(P)).then_inc(g_fin_in, 16)
            nc.scalar.activation(p_hi[:], p_t[:], ACT.Copy).then_inc(pple_hi, 1)
            split_hi(LAST + 3)
            split_hi(LAST + 4)
            spread(3)
            split_hi(LAST + 5)
            for m in range(KD):
                if m:
                    split_hi(LAST + 5 + m)
                    act.wait_ge(gated, m)
                act.wait_ge(z_ready, m + 1)
                nc.scalar.activation(tb[:], ta[:], ACT.Tanh, scale=0.5).then_inc(gate_ready, 1)

        @block.gpsimd
        def _(pool):
            def split_lo(n, step=0, it=None):
                if n >= END:
                    return
                pool.wait_ge(w_hi_ready, at(n + 1, step, it))
                nc.gpsimd.tensor_tensor(w_lo[:, n % RING, :], w_raw[:, n % RING, :],
                                        w_hi[:, n % RING, :].bitcast(F32), ALU.subtract).then_inc(w_lo_ready, 1)

            def clear_ssq(stat):
                if stat:
                    pool.wait_ge(stat_summed, stat)
                nc.gpsimd.memset(ssq[:], 0.0).then_inc(sq_cleared, 1)

            def add_square(stat, m, step=0, it=None):
                if 8 * stat + m == 0:
                    pool.wait_ge(sq_cleared, 1)
                else:
                    pool.wait_ge(sq_cleared, stat + 1)
                    pool.wait_ge(sq_added, at(8 * stat + m, step, it))
                pool.wait_ge(x_ready, at(8 * stat + m + 1, step, it))
                nc.gpsimd.tensor_tensor(sq[:], tile_of(x, m, step, it), tile_of(x, m, step, it),
                                        ALU.mult).then_inc(sq_made, 1)
                pool.wait_ge(sq_made, at(8 * stat + m + 1, step, it))
                nc.gpsimd.tensor_tensor(ssq[:], ssq[:], sq[:], ALU.add).then_inc(sq_added, 1)

            def ffn(up, down, stat):
                split_lo(up + 3)
                split_lo(up + 4)
                with pool.Fori(0, (KF - 1) // 3) as it:
                    for r in range(3):
                        split_lo(up + 2 * (1 + r) + 3, 6, it)
                        split_lo(up + 2 * (1 + r) + 4, 6, it)
                clear_ssq(stat + 1)
                with pool.Fori(0, KD // 2) as it:
                    for m in range(2):
                        for c in range(3):
                            split_lo(down + 3 * m + 3 + c, 6, it)
                        add_square(stat + 1, m, 2, it)

            nc.gpsimd.memset(ident[:], 0.0).then_inc(consts_ready, 1)
            nc.gpsimd.memset(ones[:], 1.0).then_inc(consts_ready, 1)
            nc.gpsimd.memset(var[:], 1.0).then_inc(consts_ready, 1)
            clear_ssq(0)
            pool.wait_ge(consts_ready, 3)
            nc.gpsimd.affine_select(out=ident[:], in_=ident[:], compare_op=ALU.not_equal, fill=1.0, base=0,
                                    pattern=[[-1, P]], channel_multiplier=1).then_inc(consts_ready, 1)
            for n in range(RING):
                split_lo(n)
            for m in range(KD):
                add_square(0, m)
            ffn(UP1, DOWN1, 0)

            clear_ssq(2)
            pool.wait_ge(unit_done, IN)
            nc.gpsimd.memset(mask[:], 0.0).then_inc(mask_ready, 1)
            nc.gpsimd.memset(q_diag[:], 0.0).then_inc(s_diag_clear, 1)
            pool.wait_ge(mask_ready, 1)
            nc.gpsimd.affine_select(out=mask[:, 0, :], in_=mask[:, 0, :], compare_op=ALU.is_ge, fill=NEG, base=0,
                                    pattern=[[-1, 2 * W]], channel_multiplier=1).then_inc(mask_ready, 1)
            nc.gpsimd.affine_select(out=mask[:, 1, :], in_=mask[:, 1, :], compare_op=ALU.is_ge, fill=NEG, base=W,
                                    pattern=[[-1, 2 * W]], channel_multiplier=1).then_inc(mask_ready, 1)
            pool.wait_ge(mask_ready, 3)
            nc.gpsimd.affine_select(out=mask[:, 1, :], in_=mask[:, 1, :], compare_op=ALU.is_ge, fill=NEG, base=0,
                                    pattern=[[1, 2 * W]], channel_multiplier=-1).then_inc(mask_ready, 1)
            for kind, *arg in steps:
                if kind == "gemm" and arg[1] == 0 and arg[0] > 0:
                    split_lo(IN + arg[0] + 2)
                elif kind == "ws_turn":
                    pool.wait_ge(ws_taken, 1)
                    nc.gpsimd.affine_select(out=ws_t[:], in_=ws_t[:], compare_op=ALU.is_ge, fill=0.0, base=0,
                                            pattern=[[0, GG], [1, P]], channel_multiplier=-1).then_inc(ws_ready, 1)

            split_lo(OUT + 2)
            for m in range(KD):
                split_lo(OUT + m + 3)
                add_square(2, m)
            ffn(UP2, DOWN2, 2)
            clear_ssq(4)
            for n in range(LAST + 3, LAST + 6):
                split_lo(n)
            for m in range(KD):
                if m:
                    split_lo(LAST + 5 + m)
                add_square(4, m)

        @block.vector
        def _(dve):
            chain = [0]

            def link(ins):
                chain[0] += 1
                ins.then_inc(dve_step, 1)
                dve.wait_ge(dve_step, chain[0])

            def rsqrt():
                link(nc.vector.tensor_scalar(rs_i[:], var[:].bitcast(I32), 1, None, ALU.logical_shift_right))
                link(nc.vector.tensor_scalar(rs[:].bitcast(I32), rs_i[:], -1.0, RSQRT_SEED, ALU.mult, ALU.add))
                for _ in range(3):
                    link(nc.vector.tensor_tensor(rs_t[:], rs[:], rs[:], ALU.mult))
                    link(nc.vector.tensor_tensor(rs_t[:], rs_t[:], var[:], ALU.mult))
                    link(nc.vector.tensor_scalar(rs_t[:], rs_t[:], -0.5, 1.5, ALU.mult, ALU.add))
                    link(nc.vector.tensor_tensor(rs[:], rs[:], rs_t[:], ALU.mult))

            def stat_rsqrt(stat):
                dve.wait_ge(stat_summed, stat + 1)
                link(nc.vector.tensor_scalar(var[:, 0:NB], ps[:, 7, 0:NB], 1.0 / D, RMS_EPS, ALU.mult, ALU.add))
                link(nc.vector.tensor_scalar(var[0:TS, NB:NB + 1], ps[0:TS, 7, NB:NB + 1], 1.0 / D, RMS_EPS,
                                             ALU.mult, ALU.add))
                rsqrt()

            def stat_diag(stat):
                stat_rsqrt(stat)
                nc.vector.tensor_tensor(diag[:, 0:TP].rearrange("p (b t) -> p b t", t=P),
                                        ident[:].unsqueeze(1).broadcast_to([P, NB, P]),
                                        rs[:, 0:NB].unsqueeze(2).broadcast_to([P, NB, P]),
                                        ALU.mult).then_inc(diag_ready, 1)
                nc.vector.tensor_scalar(diag[0:TS, TP:T], ident[0:TS, 0:TS], rs[0:TS, NB:NB + 1], None,
                                        ALU.mult).then_inc(diag_ready, 1)

            def x_lo(stat, m, step=0, it=None):
                dve.wait_ge(xg_hi_ready, at(8 * stat + m + 1, step, it))
                nc.vector.scalar_tensor_tensor(out=tile_of(xg_lo, m, step, it), in0=tile_of(x, m, step, it),
                                               scalar=col(8 * stat + m, step, it),
                                               in1=tile_of(xg_hi, m, step, it).bitcast(F32),
                                               op0=ALU.mult, op1=ALU.subtract).then_inc(xg_lo_ready, 1)

            def take_turned(dst, p):
                nc.vector.tensor_copy(dst[:, 0:TP], ps[:, 2 * p, :])
                return nc.vector.tensor_copy(dst[:, TP:T], ps[:, 2 * p + 1, 0:TS])

            def up_step(base, f0, h, f, it):
                if f0 + f:
                    dve.wait_ge(tanh_ready, at(f0 + f, 3, it))
                dve.wait_ge(unit_done, at(base + 2 * f + 1, 6, it))
                nc.vector.tensor_tensor(halves(ta[:]), pair(2 * f % 3), halves(rstd[:]), ALU.mult).then_inc(a_ready, 1)
                if f0 + f:
                    dve.wait_ge(h_lo_ready, at(f0 + f, 3, it))
                dve.wait_ge(a_ready, at(f0 + f + 1, 3, it))
                dve.wait_ge(unit_done, at(base + 2 * f + 2, 6, it))
                nc.vector.tensor_tensor(halves(tq[:]), pair((2 * f + 1) % 3), halves(ta[:]),
                                        ALU.mult).then_inc(ab_ready, 1)
                dve.wait_ge(ab_ready, at(f0 + f + 1, 3, it))
                nc.vector.tensor_tensor(tq[:], tq[:], rstd[:], ALU.mult).then_inc(ab_scaled, 1)
                dve.wait_ge(tanh_ready, at(f0 + f + 1, 3, it))
                dve.wait_ge(ab_scaled, at(f0 + f + 1, 3, it))
                nc.vector.scalar_tensor_tensor(out=tq[:], in0=tb[:], scalar=1.0, in1=tq[:], op0=ALU.add,
                                               op1=ALU.mult).then_inc(h_ready, 1)
                dve.wait_ge(h_hi_ready, at(f0 + f + 1, 3, it))
                nc.vector.tensor_tensor(tile_of(h[1], f, 3, it), tq[:], tile_of(h[0], f, 3, it).bitcast(F32),
                                        ALU.subtract).then_inc(h_lo_ready, 1)

            def down_step(base, stat, m, it):
                dve.wait_ge(unit_done, at(base + 3 * m + 3, 6, it))
                nc.vector.scalar_tensor_tensor(out=halves(tile_of(x, m, 2, it)), in0=pair(m % 2), scalar=0.25,
                                               in1=halves(tile_of(x, m, 2, it)), op0=ALU.mult,
                                               op1=ALU.add).then_inc(x_ready, 1)
                x_lo(stat, m, 2, it)

            def ffn(up, down, f0, h, stat):
                dve.wait_ge(rstd_ready, 2 * (stat + 1))
                up_step(up, f0, h, 0, None)
                with dve.Fori(0, (KF - 1) // 3) as it:
                    for r in range(3):
                        up_step(up, f0, h, 1 + r, it)
                if stat == 0:
                    for k in range(KP):
                        dve.wait_ge(p_turned, k + 1)
                        take_turned(p_t[:, k, :], 3 - k).then_inc(p_ready, 1)
                with dve.Fori(0, KD // 2) as it:
                    for m in range(2):
                        down_step(down, stat + 1, m, it)

            dve.wait_ge(cols_turned, 1)
            nc.vector.tensor_copy(cols[:, 0:N_COLS], ps[:, 6, 0:N_COLS]).then_inc(cols_ready, 1)
            dve.wait_ge(cols_ready, 1)
            for m in range(KD):
                dve.wait_ge(x_turned, m + 1)
                take_turned(x[:, m, :], m % 3).then_inc(x_ready, 1)
                x_lo(0, m)
            stat_diag(0)
            ffn(UP1, DOWN1, 0, h1, 0)

            n_gelu = 0
            for kind, *arg in steps:
                if kind == "stat_sum":
                    stat_diag(1)
                elif kind == "evac":
                    u, name = arg[0], IN_ORDER[arg[0]]
                    if u == 0:
                        dve.wait_ge(rstd_ready, 4)
                    else:
                        dve.wait_ge(z_done, u)
                    dve.wait_ge(unit_done, IN + u + 1)
                    nc.vector.tensor_tensor(halves(ta[:]), pair(IN_PAIR[u]), halves(rstd[:]),
                                            ALU.mult).then_inc(z_scaled, 1)
                    if name[0] in "ug":
                        n_gelu += 1
                        g = int(name[1])
                        dst = g_t[:] if name[0] == "g" else gu[:, g % 2, :]
                        dve.wait_ge(gelu_sq, n_gelu)
                        link(nc.vector.tensor_scalar(tb[:], tb[:], 0.044715 * GELU_C, GELU_C, ALU.mult, ALU.add))
                        dve.wait_ge(z_done, u + 1)
                        nc.vector.tensor_tensor(tb[:], tb[:], tq[:], ALU.mult).then_inc(gelu_arg, 1)
                        if name[0] == "g" and g:
                            dve.wait_ge(g_turned, g)
                        dve.wait_ge(gelu_tanh, n_gelu)
                        nc.vector.scalar_tensor_tensor(out=dst, in0=tb[:], scalar=1.0, in1=tq[:], op0=ALU.add,
                                                       op1=ALU.mult).then_inc(gelu_done, 1)
                    if name == "k":
                        dve.wait_ge(mix_in, 16 * mix_loads)
                        link(nc.vector.tensor_scalar(neg_sink[:], sink[:], -1.0, None, ALU.mult))
                        nc.vector.tensor_tensor(w00_diag[:], ident[0:TS, 0:TS].unsqueeze(1).broadcast_to([TS, GG, TS]),
                                                w00[:].unsqueeze(2).broadcast_to([TS, GG, TS]),
                                                ALU.mult).then_inc(w00_ready, 1)
                elif kind == "scores":
                    i = arg[0]
                    j, bp, c0 = i // 2, i % 2, 16 * (i % 2)
                    dst = probs[:, bp]
                    dve.wait_ge(scored, i + 1)
                    if i == 0:
                        dve.wait_ge(mask_ready, 4)
                    if i >= 2:
                        dve.wait_ge(probs_turned, 2 * (i - 1))
                    for c in range(NKV):
                        m_ = (mask[:, 0:2, :] if bp == 0 else mask[:, 1:2, :].broadcast_to([P, 2, 2 * W]))
                        last = nc.vector.scalar_tensor_tensor(
                            out=dst[:, c], in0=ps[:, 4 + c, :].rearrange("p (b s) -> p b s", b=2), scalar=SCALE,
                            in1=m_, op0=ALU.mult, op1=ALU.add)
                    last.then_inc(masked, 1)
                    dve.wait_ge(masked, i + 1)
                    link(nc.vector.tensor_reduce(st[:, c0 + 12:c0 + 16], dst.rearrange("p c b s -> p (c b) s"),
                                                 AX_X, ALU.max))
                    by_head = lambda t: (t[:].rearrange("p (c j) -> p c j", c=NKV)[:, :, j:j + 1]
                                         .broadcast_to([P, NKV, 2]))
                    link(nc.vector.scalar_tensor_tensor(
                        out=st[:, c0:c0 + 4].rearrange("p (c b) -> p c b", c=NKV),
                        in0=st[:, c0 + 12:c0 + 16].rearrange("p (c b) -> p c b", c=NKV), scalar=-1.0,
                        in1=by_head(neg_sink), op0=ALU.mult, op1=ALU.min))
                    nc.vector.tensor_tensor(st[:, c0 + 4:c0 + 8].rearrange("p (c b) -> p c b", c=NKV),
                                            st[:, c0:c0 + 4].rearrange("p (c b) -> p c b", c=NKV),
                                            by_head(sink), ALU.add).then_inc(max_ready, 1)
                elif kind == "p_turn" and arg[1] == 0:
                    i = arg[0]
                    c0 = 16 * (i % 2)
                    dve.wait_ge(probs_turned, 2 * i + 1)
                    nc.vector.tensor_copy(probs_t[:, 0].rearrange("p c k q -> p (c k q)"),
                                          ps[:, 6, :]).then_inc(probs_taken[0], 1)
                    dve.wait_ge(exp_done, 5 * (i + 1))
                    link(nc.vector.tensor_tensor(st[:, c0 + 12:c0 + 16], st[:, c0 + 8:c0 + 12], st[:, c0 + 4:c0 + 8],
                                                 ALU.add))
                    link(nc.vector.reciprocal(st[:, c0 + 12:c0 + 16], st[:, c0 + 12:c0 + 16]))
                elif kind == "values":
                    i = arg[0]
                    c0 = 16 * (i % 2)
                    dve.wait_ge(o_made, i + 1)
                    if i:
                        dve.wait_ge(o_turned, i)
                    nc.vector.tensor_tensor(
                        o_rows[:], ps[:, 7, 0:256].rearrange("p (b c d) -> p b c d", b=2, c=NKV),
                        st[:, c0 + 12:c0 + 16].rearrange("p (c b) -> p b c", c=NKV).unsqueeze(3)
                        .broadcast_to([P, 2, NKV, HD]), ALU.mult).then_inc(o_taken, 1)
                elif kind == "o_turn":
                    i = arg[0]
                    part = slice(256 * (i % 2), 256 * (i % 2) + 256)
                    dve.wait_ge(o_hi, i + 1)
                    nc.vector.tensor_tensor(mix_lo[:, i // 2, part], ps[:, 7, 256:512],
                                            mix_hi[:, i // 2, part].bitcast(F32), ALU.subtract).then_inc(o_lo, 1)
                elif kind == "norm_stats":
                    dve.wait_ge(g_taken, GG)
                    for b in range(NB + 1):
                        n = P if b < NB else TS
                        link(nc.vector.bn_stats(bn[0:n, b, :], g_rows[0:n, b, :]))
                        link(nc.vector.bn_aggr(mv[0:n, b, :], bn[0:n, b, :]))
                        link(nc.vector.tensor_scalar(var[0:n, b:b + 1], mv[0:n, b, 1:2], 4 * LN_EPS, None, ALU.add))
                    rsqrt()
                elif kind == "norm":
                    b = arg[0]
                    n = P if b < NB else TS
                    v = g_rows[0:n, b, :]
                    link(nc.vector.tensor_scalar(v, v, mv[0:n, b, 0:1], rs[0:n, b:b + 1], ALU.subtract, ALU.mult))
                    link(nc.vector.tensor_tensor(v, v, lng[0:n, :], ALU.mult))
                    nc.vector.tensor_tensor(v, v, lnb[0:n, :], ALU.add).then_inc(g_normed, 1)
                elif kind == "spatial":
                    g = arg[0]
                    dve.wait_ge(spatial_made, g + 1)
                    if g:
                        dve.wait_ge(gm_lo, g)
                    nc.vector.tensor_tensor(sp[:, 0:TP].rearrange("p (b t) -> p b t", t=P),
                                            ps[:, 4, :].rearrange("p (b t) -> p b t", t=P),
                                            bs_all[:, g:g + 1, :].broadcast_to([P, NB, P]), ALU.add)
                    nc.vector.tensor_scalar(sp[:, TP:T], ps[:, 5, 384:384 + TS], bs_all[:, g, 0:1], None,
                                            ALU.add).then_inc(spatial_taken, 1)
                elif kind == "gm":
                    g = arg[0]
                    dve.wait_ge(spatial_taken, g + 1)
                    dve.wait_ge(gelu_done, GG + g + 1)
                    nc.vector.tensor_tensor(sp[:], sp[:], gu[:, g % 2, :], ALU.mult).then_inc(gm_ready, 1)
                    dve.wait_ge(gm_hi, g + 1)
                    nc.vector.scalar_tensor_tensor(out=mix_lo[:, 4 + g, :], in0=sp[:], scalar=0.5,
                                                   in1=mix_hi[:, 4 + g, :].bitcast(F32), op0=ALU.mult,
                                                   op1=ALU.subtract).then_inc(gm_lo, 1)
                elif kind == "s_scores":
                    dve.wait_ge(s_diag_clear, 1)
                    dve.wait_ge(z_done, IN_ORDER.index("q3") + 1)
                    for c in range(NKV):
                        part = slice(c * HD, (c + 1) * HD)
                        link(nc.vector.tensor_copy(q_diag[part, :, c * GQ:(c + 1) * GQ],
                                                   q_t[part, :, TP:T].rearrange("p j s -> p s j")))
                    nc.vector.tensor_tensor(qk_new[:], q_diag[:], k_t[:, TP:T].unsqueeze(2).broadcast_to([P, TS, NQ]),
                                            ALU.mult).then_inc(s_built, 1)
                    dve.wait_ge(s_scored, 1)
                    nc.vector.tensor_copy(s_keys[:], ps[:, 5, 0:64]).then_inc(s_taken, 1)
                elif kind == "s_softmax":
                    dve.wait_ge(s_turned, 1)
                    link(nc.vector.tensor_scalar(s_p[:, 0:W], ps[0:64, 5, 128:256], SCALE, None, ALU.mult))
                    link(nc.vector.tensor_scalar(s_p[:, W:W + 1], ps[0:64, 5, 64:65], SCALE, None, ALU.mult))
                    link(nc.vector.tensor_reduce(s_st[:, 3:4], s_p[:], AX_X, ALU.max))
                    link(nc.vector.tensor_tensor(s_st[:, 3:4], s_st[:, 3:4], s_sink[:], ALU.max))
                    link(nc.vector.tensor_scalar(s_st[:, 0:1], s_st[:, 3:4], -1.0, None, ALU.mult))
                    nc.vector.tensor_tensor(s_st[:, 1:2], s_st[:, 0:1], s_sink[:], ALU.add).then_inc(s_max, 1)
                    dve.wait_ge(s_exp, 2)
                    link(nc.vector.tensor_tensor(s_st[:, 4:5], s_st[:, 1:2], s_st[:, 2:3], ALU.add))
                    link(nc.vector.reciprocal(s_st[:, 5:6], s_st[:, 4:5]))
                    link(nc.vector.tensor_scalar(s_p[:], s_p[:], s_st[:, 5:6], None, ALU.mult))
                    nc.vector.tensor_scalar(s_new[:], ident[0:64, 0:64], s_p[:, W:W + 1], None,
                                            ALU.mult).then_inc(s_normed, 1)
                elif kind == "s_probs":
                    dve.wait_ge(s_p_turned, 1)
                    nc.vector.tensor_copy(s_pt[:], ps[:, 5, 0:64]).then_inc(s_p_taken, 1)
                    nc.vector.tensor_tensor(s_pv[:], ps[:, 5, 64:128].rearrange("p (s h) -> p s h", s=TS),
                                            v_t[:, TP:T].unsqueeze(2).broadcast_to([P, TS, NQ]),
                                            ALU.mult).then_inc(s_p_taken, 1)
                elif kind == "s_values":
                    dve.wait_ge(s_valued, 1)
                    dve.wait_ge(s_p_taken, 2)
                    nc.vector.tensor_tensor(s_o[:], ps[:, 5, 256:320].rearrange("p (s h) -> p s h", s=TS), s_pv[:],
                                            ALU.add).then_inc(s_out, 1)
                    for c in range(NKV):
                        part = slice(c * HD, (c + 1) * HD)
                        dve.wait_ge(s_hi, c + 1)
                        nc.vector.tensor_tensor(mix_lo[part, 0:4, TP:T],
                                                s_o[part, :, c * GQ:(c + 1) * GQ].rearrange("p s j -> p j s"),
                                                mix_hi[part, 0:4, TP:T].bitcast(F32), ALU.subtract).then_inc(s_lo, 1)

            for m in range(KD):
                dve.wait_ge(unit_done, OUT + m + 1)
                nc.vector.scalar_tensor_tensor(out=halves(x[:, m, :]), in0=pair(m % 3), scalar=col(C_BOUT + m),
                                               in1=halves(x[:, m, :]), op0=ALU.add,
                                               op1=ALU.add).then_inc(x_ready, 1)
                x_lo(2, m)
            stat_diag(2)
            ffn(UP2, DOWN2, KF, h2, 2)

            dve.wait_ge(pple_hi, 1)
            nc.vector.tensor_tensor(p_lo[:], p_t[:], p_hi[:].bitcast(F32), ALU.subtract).then_inc(pple_lo, 1)
            stat_diag(3)
            for m in range(KD):
                if m % 4 == 3:
                    dve.wait_ge(unit_done, LAST + 2 + m // 4)
                else:
                    dve.wait_ge(pp_made, 3 * (m // 4) + m % 4 + 1)
                nc.vector.tensor_copy(halves(pp[:, m, :]), pair(1 + m % 2)).then_inc(pp_ready, 1)
            for m in range(KD):
                if m == 0:
                    dve.wait_ge(rstd_ready, 8)
                else:
                    dve.wait_ge(gate_ready, m)
                dve.wait_ge(unit_done, LAST + 1 if m == 0 else LAST + 3 + m)
                nc.vector.tensor_tensor(halves(ta[:]), pair(m % 3), halves(rstd[:]), ALU.mult).then_inc(z_ready, 1)
                dve.wait_ge(gate_ready, m + 1)
                nc.vector.scalar_tensor_tensor(out=tq[:], in0=tb[:], scalar=1.0, in1=pp[:, m, :], op0=ALU.add,
                                               op1=ALU.mult).then_inc(gated, 1)
                dve.wait_ge(gated, m + 1)
                nc.vector.scalar_tensor_tensor(out=x[:, m, :], in0=tq[:], scalar=0.5, in1=x[:, m, :], op0=ALU.mult,
                                               op1=ALU.add).then_inc(x_ready, 1)

            stat_rsqrt(4)
            dve.wait_ge(g_fin_in, 16)
            for b in range(NB + 1):
                n = P if b < NB else TS
                dve.wait_ge(y_turned, b + 1)
                nc.vector.scalar_tensor_tensor(out=y[0:n, b, :].rearrange("p (a c) -> p a c", a=2),
                                               in0=ps[0:n, 2 * (b % 4):2 * (b % 4) + 2, :], scalar=rs[0:n, b:b + 1],
                                               in1=g_fin[0:n, :].rearrange("p (a c) -> p a c", a=2), op0=ALU.mult,
                                               op1=ALU.mult).then_inc(y_ready, 1)

        @block.tensor
        def _(pe):
            def k_step(n, k, src, sk, p, first, last):
                for i, (w, m_) in enumerate(((w_hi, src[0]), (w_hi, src[1]), (w_lo, src[0]))):
                    for h in range(2):
                        ins = pe.matmul(ps[:, 2 * p + h, 0:HALF], w[:, n % RING, k * P:(k + 1) * P],
                                        m_[:, sk, h * HALF:(h + 1) * HALF],
                                        start=(first and i == 0), stop=(last and i == 2))
                return ins

            def unit(n, src, p, sk0=0, kn=KD, first=True, last=True, step=0, it=None, ready=None):
                pe.wait_ge(w_lo_ready, at(n + 1, step, it))
                for k in range(kn):
                    if ready:
                        pe.wait_ge(ready[0], ready[1] + k + 1)
                    ins = k_step(n, k, src, sk0 + k, p, first and k == 0, last and k == kn - 1)
                ins.then_inc(unit_done, 1)

            def stat_sum(stat):
                pe.wait_ge(sq_added, 8 * (stat + 1))
                for b in range(NB + 1):
                    n = P if b < NB else TS
                    ins = pe.matmul(ps[0:n, 7, b:b + 1], ssq[:, b * P:b * P + n], ones[:, 0:1], start=True, stop=True)
                ins.then_inc(stat_summed, 1)

            def stat_out(stat):
                pe.wait_ge(diag_ready, 2 * (stat + 1))
                pe.matmul(ps[:, 6, :], ones[:], diag[:, 0:TP], start=True, stop=True)
                pe.matmul(ps[:, 7, 8:8 + TS], ones[0:TS, :], diag[0:TS, TP:T], start=True,
                          stop=True).then_inc(stat_spread, 1)

            def turn(dst, src, n=P):
                return pe.transpose(dst, src, ident[0:n, 0:n])

            def turn_tile(rows_, s_rows, c, p):
                for b in range(NB):
                    turn(ps[:, 2 * p, b * P:(b + 1) * P], rows_[:, b, c * P:(c + 1) * P])
                return turn(ps[:, 2 * p + 1, 0:TS], s_rows[0:TS, c * P:(c + 1) * P], TS)

            def up_step(base, f0, f, it, src):
                pe.wait_ge(a_ready, at(f0 + f, 3, it))
                unit(base + 2 * f, src, 2 * f % 3, step=6, it=it)
                unit(base + 2 * f + 1, src, (2 * f + 1) % 3, step=6, it=it)

            def down_step(base, f0, stat, h, m, it):
                pe.wait_ge(x_ready, at(8 * stat + m - 1, 2, it))
                for c, kn in enumerate(DOWN_K):
                    pe.wait_ge(h_lo_ready, f0 + 8 * c + kn)
                    unit(base + 3 * m + c, h, m % 2, 8 * c, kn, c == 0, c == 2, 6, it)

            def ffn(up, down, f0, h, stat, src):
                with pe.Fori(0, (KF - 1) // 3) as it:
                    for r in range(3):
                        up_step(up, f0, 1 + r, it, src)
                if stat == 0:
                    pe.wait_ge(p_in, 16)
                    pe.wait_ge(ps_in, 16)
                    turn_tile(p_rows, ps_rows, 0, 3).then_inc(p_turned, 1)
                    pe.wait_ge(a_ready, KF)
                    turn_tile(p_rows, ps_rows, 1, 2).then_inc(p_turned, 1)
                pe.wait_ge(a_ready, f0 + KF)
                with pe.Fori(0, KD // 2) as it:
                    for m in range(2):
                        down_step(down, f0, stat + 1, h, m, it)

            xg = xg_hi, xg_lo

            pe.wait_ge(consts_ready, 4)
            pe.wait_ge(rows_in, 16 * 8)
            pe.transpose(ps[:, 6, 0:N_COLS], rows[0:N_COLS, :], ident[0:N_COLS, 0:N_COLS]).then_inc(cols_turned, 1)
            for s_ in x_in:
                pe.wait_ge(s_, 16)
            for m in range(KD):
                if m >= 3:
                    pe.wait_ge(x_ready, m - 2)
                turn_tile(x_rows, xs_rows, m, m % 3).then_inc(x_turned, 1)

            pe.wait_ge(x_ready, KD)
            unit(UP1, xg, 0, ready=(xg_lo_ready, 0))
            stat_sum(0)
            unit(UP1 + 1, xg, 1)
            stat_out(0)
            ffn(UP1, DOWN1, 0, h1, 0, xg)

            for kind, *arg in steps:
                if kind == "gemm":
                    u, k = arg
                    n = IN + u
                    if k == 0:
                        if u == 0:
                            pe.wait_ge(x_ready, 15)
                        if u == 1:
                            pe.wait_ge(x_ready, 16)
                        if u == 2:
                            pe.wait_ge(cache_taken, 1)
                        if u >= 3:
                            pe.wait_ge(z_scaled, u - 1 if u > 3 else 1)
                        pe.wait_ge(w_lo_ready, n + 1)
                    if u == 0:
                        pe.wait_ge(xg_lo_ready, 8 + k + 1)
                    ins = k_step(n, k, xg, k, IN_PAIR[u], k == 0, k == KD - 1)
                    if k == KD - 1:
                        ins.then_inc(unit_done, 1)
                elif kind == "stat_sum":
                    stat_sum(1)
                elif kind == "stat_spread":
                    stat_out(1)
                elif kind == "cache_turn":
                    pe.wait_ge(cache_in, 16)
                    for b in range(TS):
                        ins = turn(ps[:, 4 + b // 4, (b % 4) * W:(b % 4 + 1) * W], cache_k[:, b, :])
                    ins.then_inc(cache_turned, 1)
                elif kind == "ws_turn":
                    pe.wait_ge(ws_in, 16)
                    pe.wait_ge(rstd_ready, 4)
                    for g in range(GG):
                        ins = turn(ps[:, 6, g * P:(g + 1) * P], ws_rows[:, g, :])
                    ins.then_inc(ws_turned, 1)
                elif kind == "g_turn":
                    g = arg[0]
                    bank = 4 if g else 6
                    pe.wait_ge(gelu_done, g + 1)
                    if g == 0:
                        pe.wait_ge(ws_taken, 1)
                    elif g == 1:
                        pe.wait_ge(z_scaled, 3)
                    else:
                        pe.wait_ge(masked, 2 * g - 2)
                    for b in range(NB):
                        turn(ps[:, bank, b * P:(b + 1) * P], g_t[:, b * P:(b + 1) * P])
                    pe.transpose(ps[0:TS, bank + 1, 0:P], g_t[:, TP:T], ident[:]).then_inc(g_turned, 1)
                elif kind == "kv_turn":
                    pe.wait_ge(z_done, 4)
                    pe.wait_ge(g_taken, 1)
                    for b in range(NB):
                        turn(ps[:, 6, b * P:(b + 1) * P], v_t[:, b * P:(b + 1) * P])
                    pe.transpose(ps[0:TS, 7, 0:P], v_t[:, TP:T], ident[:])
                    turn(ps[:, 7, P:2 * P], k_t[:, TP - P:TP])
                    pe.transpose(ps[0:TS, 7, 2 * P:3 * P], k_t[:, TP:T], ident[:]).then_inc(kv_turned, 1)
                elif kind == "scores":
                    i = arg[0]
                    j, bp = i // 2, i % 2
                    pe.wait_ge(z_done, IN_ORDER.index(f"q{j}") + 1)
                    pe.wait_ge(g_taken, sum(1 for g, u in enumerate((0, 3, 6, 8)) if u < 5 + i))
                    if i:
                        pe.wait_ge(masked, i)
                    if i == 7:
                        pe.wait_ge(spatial_taken, 1)
                        pe.wait_ge(s_max, 1)
                    for c in range(NKV):
                        part = slice(c * HD, (c + 1) * HD)
                        for r in range(2):
                            b = 2 * bp + r
                            k0 = max(b - 1, 0) * W
                            ins = pe.matmul(ps[:, 4 + c, r * 2 * W:(r + 1) * 2 * W], q_t[part, j, b * P:(b + 1) * P],
                                            k_t[part, k0:k0 + 2 * W], start=True, stop=True)
                    ins.then_inc(scored, 1)
                elif kind == "p_turn":
                    i, r = arg
                    pe.wait_ge(exp_done, 5 * (i + 1))
                    if r == 1:
                        pe.wait_ge(probs_taken[0], i + 1)
                    elif i == 0:
                        pe.wait_ge(kv_taken, 4)
                    else:
                        pe.wait_ge(probs_taken[1], i)
                    for c in range(NKV):
                        for k in range(2):
                            ins = turn(ps[:, 6, (2 * c + k) * P:(2 * c + k + 1) * P],
                                       probs[:, i % 2, c, r, k * W:(k + 1) * W])
                    ins.then_inc(probs_turned, 1)
                elif kind == "values":
                    i = arg[0]
                    bp = i % 2
                    pe.wait_ge(probs_taken[0], i + 1)
                    pe.wait_ge(probs_taken[1], i + 1)
                    if i:
                        pe.wait_ge(o_lo, i)
                    for r in range(2):
                        b = 2 * bp + r
                        ks = (0,) if b == 0 else (0, 1)
                        for c in range(NKV):
                            for k in ks:
                                ins = pe.matmul(ps[:, 7, r * P + c * HD:r * P + (c + 1) * HD], probs_t[:, r, c, k, :],
                                                v_rows[:, max(b - 1, 0) + k, c * HD:(c + 1) * HD],
                                                start=(k == 0), stop=(k == ks[-1]))
                    ins.then_inc(o_made, 1)
                elif kind == "o_turn":
                    i = arg[0]
                    pe.wait_ge(o_taken, i + 1)
                    for r in range(2):
                        ins = turn(ps[:, 7, (2 + r) * P:(3 + r) * P], o_rows[:, r].rearrange("p c d -> p (c d)"))
                    ins.then_inc(o_turned, 1)
                elif kind == "spatial":
                    g = arg[0]
                    pe.wait_ge(g_normed, NB + 1)
                    pe.wait_ge(ws_ready, 1)
                    pe.wait_ge(w00_ready, 1)
                    if g:
                        pe.wait_ge(spatial_taken, g)
                    if g == 0:
                        pe.wait_ge(s_taken, 1)
                    else:
                        pe.wait_ge(s_out, 1)
                    pe.wait_ge(masked, 7 if g == 0 else 8)
                    for b in range(NB):
                        pe.matmul(ps[:, 4, b * P:(b + 1) * P], g_rows[:, b, g * P:(g + 1) * P], ws_t[:, g, :],
                                  start=True, stop=True)
                    pe.matmul(ps[:, 5, 384:384 + TS], g_rows[0:TS, NB, g * P:(g + 1) * P], w00_diag[:, g, :],
                              start=True, stop=True).then_inc(spatial_made, 1)
                elif kind == "s_scores":
                    pe.wait_ge(s_built, 1)
                    pe.wait_ge(masked, 7)
                    for b in range(TS):
                        pe.matmul(ps[:, 5, b * NQ:(b + 1) * NQ], cache_k_t[:, b, :], q_diag[:, b, :],
                                  start=True, stop=True)
                    pe.matmul(ps[0:64, 5, 64:65], qk_new[:].rearrange("p s h -> p (s h)"), ones[:, 0:1],
                              start=True, stop=True).then_inc(s_scored, 1)
                elif kind == "s_softmax":
                    pe.wait_ge(s_taken, 1)
                    pe.wait_ge(spatial_taken, 1)
                    pe.transpose(ps[0:64, 5, 128:256], s_keys[:], ident[:]).then_inc(s_turned, 1)
                elif kind == "s_probs":
                    pe.wait_ge(s_normed, 1)
                    pe.wait_ge(masked, 8)
                    pe.transpose(ps[:, 5, 0:64], s_p[:, 0:W], ident[0:64, 0:64])
                    pe.matmul(ps[:, 5, 64:128], ones[0:64, :], s_new[:], start=True, stop=True).then_inc(s_p_turned, 1)
                elif kind == "s_values":
                    pe.wait_ge(s_p_taken, 2)
                    for b in range(TS):
                        ins = pe.matmul(ps[:, 5, 256 + b * NQ:256 + (b + 1) * NQ], cache_v[:, b, :],
                                        s_pt[:, b * NQ:(b + 1) * NQ], start=True, stop=True)
                    ins.then_inc(s_valued, 1)

            for m in range(KD):
                n = OUT + m
                pe.wait_ge(w_lo_ready, n + 1)
                if m == 0:
                    pe.wait_ge(z_scaled, 14)
                    pe.wait_ge(o_lo, 8)
                    pe.wait_ge(s_lo, 2)
                elif m == 2:
                    pe.wait_ge(spatial_taken, GG)
                elif m >= 3:
                    pe.wait_ge(x_ready, 16 + m - 2)
                for k in range(KD):
                    if m == 0 and k >= 4:
                        pe.wait_ge(gm_lo, k - 3)
                    ins = k_step(n, k, (mix_hi, mix_lo), k, m % 3, k == 0, k == KD - 1)
                ins.then_inc(unit_done, 1)

            pe.wait_ge(x_ready, 16 + 7)
            unit(UP2, xg, 0, ready=(xg_lo_ready, 16))
            stat_sum(2)
            pe.wait_ge(x_ready, 16 + 8)
            unit(UP2 + 1, xg, 1)
            stat_out(2)
            ffn(UP2, DOWN2, KF, h2, 2, xg)

            pe.wait_ge(x_ready, 24 + 7)
            unit(LAST, xg, 0, ready=(xg_lo_ready, 24))
            stat_sum(3)
            pe.wait_ge(pple_lo, 1)
            for i in range(2):
                n = LAST + 1 + i
                pe.wait_ge(w_lo_ready, n + 1)
                for q in range(4):
                    m = 4 * i + q
                    if m >= 2:
                        pe.wait_ge(pp_ready, m - 1)
                    for k in range(KP):
                        ins = k_step(n, 4 * k + q, (p_hi, p_lo), k, 1 + m % 2, k == 0, k == KP - 1)
                    ins.then_inc(unit_done if q == 3 else pp_made, 1)
                if i == 0:
                    stat_out(3)
            for m in range(1, KD):
                pe.wait_ge(pp_ready, KD)
                if m >= 3:
                    pe.wait_ge(z_ready, m - 2)
                unit(LAST + 2 + m, xg, m % 3)

            pe.wait_ge(x_ready, 40)
            def turn_back(b):
                n = P if b < NB else TS
                for k in range(KD):
                    ins = pe.transpose(ps[0:n, 2 * (b % 4) + k // 4, (k % 4) * P:(k % 4 + 1) * P],
                                       x[:, k, b * P:b * P + n], ident[:])
                ins.then_inc(y_turned, 1)

            for b in range(NB - 1):
                turn_back(b)
            stat_sum(4)
            pe.wait_ge(y_ready, 1)
            turn_back(NB - 1)
            turn_back(NB)


_INS = ["x_prompt", "x_sample", "cache_k_win", "cache_v_win", "p_prompt", "p_sample", "g_ffn1", "w1_ffn1", "w3_ffn1",
        "w2_ffn1", "g_mix", "w_in", "b_in", "attn_sinks", "gm_ln_g", "gm_ln_b", "gm_w_s", "gm_b_s", "w_out", "b_out",
        "g_ffn2", "w1_ffn2", "w3_ffn2", "w2_ffn2", "g_ple", "w_ple_gate", "w_ple_proj", "g_final"]
_OUTS = [("y_prompt", (1, TP, D)), ("y_sample", (TS, 1, D)), ("k_win_prompt", (1, 1, W, NKV, HD)),
         ("v_win_prompt", (1, 1, W, NKV, HD)), ("k_win_sample", (1, TS, W, NKV, HD)),
         ("v_win_sample", (1, TS, W, NKV, HD)), ("gm_v_prompt", (1, 1, W, GM)), ("gm_v_sample", (1, TS, 1, GM))]


def kernel(**inputs):
    import numpy as _np
    import concourse.bacc as _bacc
    from concourse import mybir as _mybir
    from concourse.bass_utils import run_bass_kernel_spmd as _run

    nc = _bacc.Bacc("TRN2", target_bir_lowering=False, num_devices=1)
    arrays, ins, outs = {}, {}, {}
    for name in _INS:
        arr = _np.ascontiguousarray(inputs[name])
        arrays[f"in_{name}_dram"] = arr
        ins[name] = nc.dram_tensor(f"in_{name}_dram", arr.shape, _mybir.dt.from_np(arr.dtype),
                                   kind="ExternalInput").ap()
    for name, shape in _OUTS:
        outs[name] = nc.dram_tensor(f"out_{name}_dram", shape, _mybir.dt.float32, kind="ExternalOutput").ap()
    hybrid_decoder_layer(nc, ins, outs)
    r = _run(nc, [arrays], core_ids=[0])
    return tuple(r.results[0][f"out_{name}_dram"] for name, _ in _OUTS)
```

```python
from contextlib import ExitStack

import concourse.bass as bass
from concourse import mybir

F32 = mybir.dt.float32
F32R = mybir.dt.float32r
I32 = mybir.dt.int32
ALU = mybir.AluOpType
ACT = mybir.ActivationFunctionType
AX_X = mybir.AxisListType.X

P = 128
D, FF, PLE = 1024, 2816, 256
TP, TS = 512, 8
T = TP + TS
HALF = T // 2
NB = TP // P
KD, KF, KP = D // P, FF // P, PLE // P
HD, NQ, NKV, GQ = 64, 8, 2, 4
GM, GG = 512, 4
W = 128
RMS_EPS, LN_EPS = 1e-6, 1e-5
SCALE = HD ** -0.5
NEG = -1.0e30
GELU_C = 0.7978845608028654
GELU_K = 0.044715 ** 0.5
RSQRT_SEED = 1597463007.0

RING = 3
UP1 = 0
DOWN1 = UP1 + 2 * KF
IN = DOWN1 + 3 * KD
OUT = IN + 14
UP2 = OUT + KD
DOWN2 = UP2 + 2 * KF
LAST = DOWN2 + 3 * KD
END = LAST + KD + 2
DOWN_K = (8, 8, 6)

IN_ORDER = ("k", "v", "g0", "q0", "g1", "q1", "g2", "g3", "q2", "q3", "u0", "u1", "u2", "u3")
IN_PAIR = (0, 1, 2, 0, 1, 0, 1, 0, 1, 0, 1, 0, 1, 0)
STAT_BANK = (None, 7, 7, 7, 2)
Y_PAIR = (3, 2, 0, 1, 3)
ITEM_UNIT = (4, 5, 6, 7, 9, 10, 11, 12)
OUT_K = (4, 5, 6, 0, 1, 2, 3, 7)
C_BOUT, C_Q, C_K, C_V, C_U, C_G, C_FIN, N_COLS = 32, 40, 44, 45, 46, 50, 54, 62


def mixer_steps():
    extra = {
        (1, 2): [("stat_sum",)],
        (1, 4): [("cache_turn",)],
        (2, 0): [("stat_spread",), ("evac", 0), ("evac", 1)],
        (3, 1): [("ws_turn",)],
        (3, 5): [("kv_turn",)],
        (9, 6): [("norm_stats",)],
        (10, 3): [("norm", 3), ("norm", 4), ("s_build",)],
        (10, 7): [("norm", 0), ("norm", 1), ("norm", 2)],
        (11, 6): [("s_scores",), ("spatial", 0), ("gm", 0)],
        (11, 7): [("s_softmax",)],
        (12, 7): [("s_probs",), ("spatial", 1), ("gm", 1)],
        (13, 2): [("s_values",), ("spatial", 2)],
        (13, 6): [("gm", 2), ("spatial", 3)],
    }

    def put(u, k, *stages):
        extra[(u, k)] = list(stages) + extra.get((u, k), [])

    for u, name in enumerate(IN_ORDER[:-1]):
        if name[0] == "g":
            put(u + 1, 7, ("g_turn", int(name[1])))
        if name[0] in "ug":
            put(u + 1, 6, ("gelu_end", u))
            put(u + 1, 1, ("gelu_mid", u))
    for i, u in enumerate(ITEM_UNIT):
        put(u, 2, ("scores", i))
        put(u, 5, ("soft", i))
        put(u + 1, 1, ("p_turn", i, 0))
        put(u + 1, 4, ("p_turn", i, 1))
        put(u + 1, 6, ("values", i))
        if u + 2 < 14:
            put(u + 2, 0, ("o_turn", i))
    steps = []
    for u in range(14):
        for k in range(KD):
            steps += extra.pop((u, k), [])
            steps.append(("gemm", u, k))
        if u > 1:
            steps.append(("evac", u))
    assert not extra, extra
    steps += [("out", OUT_K[0]), ("o_turn", 7), ("gelu_mid", 13)]
    steps += [("out", k) for k in OUT_K[1:7]]
    return steps + [("gelu_end", 13), ("gm", 3), ("out", OUT_K[7])]


def hybrid_decoder_layer(nc, a, o):
    steps = mixer_steps()
    with ExitStack() as ctx:
        def sb(name, shape, dt=F32, scope=ctx):
            return scope.enter_context(nc.sbuf_tensor(name, shape, dt))

        def sem(name):
            return ctx.enter_context(nc.semaphore(name))

        x = sb("x", [P, KD, T])
        xg_hi = sb("xg_hi", [P, KD, T], F32R)
        xg_lo = sb("xg_lo", [P, KD, T], F32R)
        w_raw = sb("w_raw", [P, RING, KD * P])
        w_hi = sb("w_hi", [P, RING, KD * P], F32R)
        w_lo = sb("w_lo", [P, RING, KD * P], F32R)
        ta = sb("ta", [P, T])
        tb = sb("tb", [P, T])
        tq = sb("tq", [P, T])
        rstd = sb("rstd", [P, T])
        sq = sb("sq", [P, T])
        ssq = sb("ssq", [P, T])
        diag = sb("diag", [P, T])
        ident = sb("ident", [P, P])
        ones = sb("ones", [P, P])
        p_t = sb("p_t", [P, KP, T])
        cols = sb("cols", [P, 64])
        cols_g = sb("cols_g", [P, 64])
        var = sb("var", [P, 8])
        rs = sb("rs", [P, 8])
        rs_i = sb("rs_i", [P, 8], I32)
        rs_t = sb("rs_t", [P, 8])

        with ExitStack() as s:
            x_rows = sb("x_rows", [P, NB, D], scope=s)
            sq_rows = sb("sq_rows", [P, D], scope=s)
            xs_rows = sb("xs_rows", [P, D], scope=s)
            rows = sb("rows", [64, P], scope=s)
        with ExitStack() as s:
            h1 = sb("h1_hi", [P, KF, T], F32R, s), sb("h1_lo", [P, KF, T], F32R, s)
            p_rows = sb("p_rows", [P, NB, PLE], scope=s)
            ps_rows = sb("ps_rows", [P, PLE], scope=s)
        with ExitStack() as s:
            mix_hi = sb("mix_hi", [P, 8, T], F32R, s)
            mix_lo = sb("mix_lo", [P, 8, T], F32R, s)
            q_t = sb("q_t", [P, GQ, T], scope=s)
            k_t = sb("k_t", [P, T], scope=s)
            v_t = sb("v_t", [P, T], scope=s)
            g_rows = sb("g_rows", [P, NB + 1, GM], scope=s)
            v_rows = sb("v_rows", [P, NB + 1, P], scope=s)
            k_rows = sb("k_rows", [P, 2, P], scope=s)
            ws_t = sb("ws_t", [P, GG, P], scope=s)
            bs_all = sb("bs_all", [P, GG, P], scope=s)
            lng = sb("lng", [P, GM], scope=s)
            lnb = sb("lnb", [P, GM], scope=s)
            probs = sb("probs", [P, 2, NKV, 2, 2 * W], scope=s)
            probs_t = sb("probs_t", [P, 2, NKV, 2, P], scope=s)
            o_rows = sb("o_rows", [P, 2, NKV, HD], scope=s)
            mask = sb("mask", [P, 2, 2 * W], scope=s)
            cache_k_t = sb("cache_k_t", [P, TS, W], scope=s)
            cache_v = sb("cache_v", [P, TS, W], scope=s)
            sink = sb("sink", [P, NQ], scope=s)
            st = sb("st", [P, 32], scope=s)
            bn = sb("bn", [P, NB + 1, 6], scope=s)
            mv = sb("mv", [P, NB + 1, 2], scope=s)
            w00 = sb("w00", [TS, GG], scope=s)
            w00_diag = sb("w00_diag", [TS, GG, TS], scope=s)
            s_sink = sb("s_sink", [64, 1], scope=s)
            s_st = sb("s_st", [64, 8], scope=s)
            q_diag = sb("q_diag", [P, TS, NQ], scope=s)
            qk_new = sb("qk_new", [P, TS, NQ], scope=s)
            s_keys = sb("s_keys", [P, 64], scope=s)
            s_p = sb("s_p", [64, W + 1], scope=s)
            s_new = sb("s_new", [64, 64], scope=s)
            s_pt = sb("s_pt", [P, 64], scope=s)
            s_pv = sb("s_pv", [P, TS, NQ], scope=s)
            s_o = sb("s_o", [P, TS, NQ], scope=s)
            with ExitStack() as early:
                cache_k = sb("cache_k", [P, TS, W], scope=early)
                ws_rows = sb("ws_rows", [P, GG, P], scope=early)
                g_t = sb("g_t", [P, T], scope=early)
            gu = sb("gu", [P, 2, T], scope=s)
            sp = sb("sp", [P, T], scope=s)
        with ExitStack() as s:
            h2 = sb("h2_hi", [P, KF, T], F32R, s), sb("h2_lo", [P, KF, T], F32R, s)
        with ExitStack() as s:
            p_hi = sb("p_hi", [P, KP, T], F32R, s)
            p_lo = sb("p_lo", [P, KP, T], F32R, s)
            pp = sb("pp", [P, KD, T], scope=s)
            xf = sb("xf", [P, KD, T], scope=s)
            y = sb("y", [P, NB + 1, D], scope=s)

        ps = ctx.enter_context(nc.psum_tensor("ps", [P, 8, 512], F32))

        raw_in = [sem(f"raw_in{i}") for i in range(RING)]
        w_hi_ready, w_lo_ready = sem("w_hi_ready"), sem("w_lo_ready")
        unit_done = sem("unit_done")
        x_in = [sem(f"x_in{i}") for i in range(NB + 1)]
        p_in, ps_in = sem("p_in"), sem("ps_in")
        rows_in = sem("rows_in")
        consts_ready = sem("consts_ready")
        cols_turned, cols_ready = sem("cols_turned"), sem("cols_ready")
        x_turned = sem("x_turned")
        x_ready = sem("x_ready")
        xg_hi_ready, xg_lo_ready = sem("xg_hi_ready"), sem("xg_lo_ready")
        p_turned, p_ready = sem("p_turned"), sem("p_ready")
        sq_made = sem("sq_made")
        sq_added = sem("sq_added")
        stat_summed, diag_ready = sem("stat_summed"), sem("diag_ready")
        stat_spread, rstd_ready = sem("stat_spread"), sem("rstd_ready")
        dve_step = sem("dve_step")
        a_ready, tanh_ready = sem("a_ready"), sem("tanh_ready")
        ab_ready, ab_scaled = sem("ab_ready"), sem("ab_scaled")
        h_ready, h_hi_ready, h_lo_ready = sem("h_ready"), sem("h_hi_ready"), sem("h_lo_ready")
        mix_in = sem("mix_in")
        cache_in, ws_in = sem("cache_in"), sem("ws_in")
        mask_ready = sem("mask_ready")
        z_scaled, z_done = sem("z_scaled"), sem("z_done")
        gelu_sq, gelu_arg, gelu_tanh = sem("gelu_sq"), sem("gelu_arg"), sem("gelu_tanh")
        gelu_done = sem("gelu_done")
        cache_turned, cache_taken = sem("cache_turned"), sem("cache_taken")
        ws_turned, ws_taken, ws_ready = sem("ws_turned"), sem("ws_taken"), sem("ws_ready")
        g_turned, g_taken = sem("g_turned"), sem("g_taken")
        kv_turned, kv_taken = sem("kv_turned"), sem("kv_taken")
        g_centred = sem("g_centred")
        g_normed = sem("g_normed"), sem("g_normed_late")
        g_gained = sem("g_gained")
        scored, masked, max_ready = sem("scored"), sem("masked"), sem("max_ready")
        exp_done, sum_ready = sem("exp_done"), sem("sum_ready")
        probs_turned = sem("probs_turned")
        probs_taken = sem("probs_taken")
        o_made, o_taken = sem("o_made"), sem("o_taken")
        o_turned, o_hi, o_lo = sem("o_turned"), sem("o_hi"), sem("o_lo")
        spatial_made, spatial_taken = sem("spatial_made"), sem("spatial_taken")
        gm_ready, gm_hi, gm_lo = sem("gm_ready"), sem("gm_hi"), sem("gm_lo")
        w00_ready = sem("w00_ready")
        s_built, s_scored, s_taken = sem("s_built"), sem("s_scored"), sem("s_taken")
        s_turned, s_max, s_exp, s_normed = sem("s_turned"), sem("s_max"), sem("s_exp"), sem("s_normed")
        s_diag_clear = sem("s_diag_clear")
        s_p_turned, s_p_taken = sem("s_p_turned"), sem("s_p_taken")
        s_valued, s_out, s_hi, s_lo = sem("s_valued"), sem("s_out"), sem("s_hi"), sem("s_lo")
        pple_hi, pple_lo, pp_made, pp_ready = sem("pple_hi"), sem("pple_lo"), sem("pp_made"), sem("pp_ready")
        z_ready, gate_ready, gated = sem("z_ready"), sem("gate_ready"), sem("gated")
        row_sums, rs_ready = sem("row_sums"), sem("rs_ready")
        x_odd, x_even = sem("x_odd"), sem("x_even")
        xf_ready = sem("xf_ready")
        y_turned = sem("y_turned")
        y_ready = [sem(f"y_ready{b}") for b in range(NB + 1)]
        out_done = sem("out_done")

        def pair(i, width=HALF):
            return ps[:, 2 * i:2 * i + 2, 0:width]

        def halves(ap):
            return ap.rearrange("p (h t) -> p h t", h=2)

        def at(n, step, it):
            return n if it is None else it * step + n

        def tile_of(t, m, step, it):
            if it is None:
                return t[:, m, :]
            return t[:, bass.ds(it * step + m, 1), :].rearrange("p a t -> p (a t)")

        def col(c, step=0, it=None):
            return cols[:, c:c + 1] if it is None else cols[:, bass.ds(it * step + c, 1)]

        w_dram = {n: a[n][0].rearrange("(k p) c -> p k c", p=P)
                  for n in ("w1_ffn1", "w3_ffn1", "w2_ffn1", "w_in", "w_out", "w1_ffn2", "w3_ffn2",
                            "w2_ffn2", "w_ple_gate", "w_ple_proj")}
        mix_loads = 6 + TS

        block = ctx.enter_context(nc.Block())

        @block.sync
        def _(sp_):
            def load(n, step, it, src, width=KD * P):
                if n >= RING:
                    sp_.wait_ge(w_lo_ready, at(n - RING + 1, step, it))
                dst = w_raw[:, n % RING, 0:width]
                dst = dst.rearrange("p (k c) -> p k c", k=src.shape[1])
                sp_.dma_start(dst, src).then_inc(raw_in[n % RING], 16)

            def up_step(base, ws, f, it):
                for i, w in enumerate(ws):
                    c = bass.ds(at(f * P, 3 * P, it), P) if it is not None else slice(f * P, f * P + P)
                    load(base + 2 * f + i, 6, it, w_dram[w][:, :, c])

            def down_step(base, w, m, it):
                c = bass.ds(at(m * P, 2 * P, it), P)
                for i, kn in enumerate(DOWN_K):
                    load(base + 3 * m + i, 6, it, w_dram[w][:, 8 * i:8 * i + kn, c], kn * P)

            def ffn(up, down, w1, w3, w2, first=0):
                for f in range(1 if first else 0, 4):
                    up_step(up, (w1, w3), f, None)
                with sp_.Fori(0, (KF - 4) // 3) as it:
                    for r in range(3):
                        up_step(up, (w1, w3), 4 + r, it)
                if first:
                    sp_.wait_ge(x_turned, KD)
                    sp_.dma_start(p_rows[:], a["p_prompt"][0, 0].rearrange("(b p) c -> p b c", p=P)).then_inc(p_in, 16)
                    sp_.dma_start(ps_rows[0:TS, :], a["p_sample"][0].rearrange("b t c -> (b t) c")).then_inc(ps_in, 16)
                with sp_.Fori(0, KD // 2) as it:
                    for r in range(2):
                        down_step(down, w2, r, it)

            for b in range(NB):
                sp_.dma_start(x_rows[:, b, :], a["x_prompt"][0, b * P:(b + 1) * P, :]).then_inc(x_in[b], 16)
            up_step(UP1, ("w1_ffn1", "w3_ffn1"), 0, None)
            ffn(UP1, DOWN1, "w1_ffn1", "w3_ffn1", "w2_ffn1", first=1)

            offset = {"q": 0, "k": 512, "v": 640, "u": 768, "g": 1280}
            for u, name in enumerate(IN_ORDER):
                c0 = offset[name[0]] + (int(name[1]) * P if name[0] in "ug" else 0)
                if name[0] == "q":
                    n, j = IN + u, int(name[1])
                    sp_.wait_ge(w_lo_ready, n - RING + 1)
                    for c in range(NKV):
                        src = w_dram["w_in"][:, :, c * 256 + j * HD:c * 256 + (j + 1) * HD]
                        dst = w_raw[:, n % RING, :].rearrange("p (k c d) -> p k c d", k=KD, c=NKV)[:, :, c, :]
                        sp_.dma_start(dst, src).then_inc(raw_in[n % RING], 16)
                else:
                    load(IN + u, 0, None, w_dram["w_in"][:, :, c0:c0 + P])
            wo = a["w_out"][0]
            for m in range(KD):
                n = OUT + m
                sp_.wait_ge(w_lo_ready, n - RING + 1)
                dst = w_raw[:, n % RING, :].rearrange("p (k c) -> p k c", k=KD)
                for c in range(NKV):
                    sp_.dma_start(dst[c * HD:(c + 1) * HD, 0:4, :],
                                  wo[c * 256:(c + 1) * 256, m * P:(m + 1) * P].rearrange("(j d) c -> d j c", d=HD)
                                  ).then_inc(raw_in[n % RING], 16)
                sp_.dma_start(dst[:, 4:8, :], wo[512:1024, m * P:(m + 1) * P].rearrange("(j d) c -> d j c", d=P)
                              ).then_inc(raw_in[n % RING], 16)

            ffn(UP2, DOWN2, "w1_ffn2", "w3_ffn2", "w2_ffn2")

            load(LAST, 0, None, w_dram["w_ple_gate"][:, :, 0:P])
            for i in range(2):
                load(LAST + 1 + i, 0, None, w_dram["w_ple_proj"][:, :, 512 * i:512 * (i + 1)])
            for m in range(1, KD):
                load(LAST + 2 + m, 0, None, w_dram["w_ple_gate"][:, :, m * P:(m + 1) * P])

            for b in range(NB):
                sp_.wait_ge(y_ready[b], 1)
                sp_.dma_start(o["y_prompt"][0, b * P:(b + 1) * P, :], y[:, b, :]).then_inc(out_done, 16)
            sp_.wait_ge(y_ready[NB], 1)
            sp_.dma_start(o["y_sample"].rearrange("b t d -> (b t) d"), y[0:TS, NB, :]).then_inc(out_done, 16)
            sp_.wait_ge(out_done, 16 * 13)

        def parts(n):
            if IN <= n < OUT and IN_ORDER[n - IN][0] == "q":
                return NKV
            return 3 if OUT <= n < UP2 else 1

        def arrived(n):
            return 16 * sum(parts(m) for m in range(n % RING, n + 1, RING))

        @block.scalar
        def _(act):
            def split_hi(n, step=0, it=None):
                if n >= END:
                    return
                act.wait_ge(raw_in[n % RING], at(arrived(n), 16 * step // RING, it))
                if n >= RING:
                    act.wait_ge(unit_done, at(n - RING + 1, step, it))
                nc.scalar.activation(w_hi[:, n % RING, :], w_raw[:, n % RING, :], ACT.Copy).then_inc(w_hi_ready, 1)

            def x_hi(stat, m, step=0, it=None):
                act.wait_ge(sq_added, at(9 * stat + m - 8, step, it))
                act.wait_ge(x_ready, at(8 * stat + m - 7, step, it))
                nc.scalar.activation(tile_of(xg_hi, m, step, it), tile_of(x, m, step, it), ACT.Copy,
                                     scale=col(8 * stat + m, step, it)).then_inc(xg_hi_ready, 1)
                nc.scalar.activation(sq[:], tile_of(x, m, step, it), ACT.Square).then_inc(sq_made, 1)

            def spread(stat):
                act.wait_ge(stat_spread, stat + 1)
                nc.scalar.activation(rstd[:, 0:TP], ps[:, 6, :], ACT.Copy).then_inc(rstd_ready, 1)
                nc.scalar.activation(rstd[:, TP:T], ps[:, 7, 8:8 + TS], ACT.Copy).then_inc(rstd_ready, 1)

            def up_step(base, f0, h, f, it):
                split_hi(base + 2 * f + 3, 6, it)
                if f0 + f:
                    act.wait_ge(h_ready, at(f0 + f, 3, it))
                act.wait_ge(a_ready, at(f0 + f + 1, 3, it))
                nc.scalar.activation(tb[:], ta[:], ACT.Tanh, scale=0.5).then_inc(tanh_ready, 1)
                split_hi(base + 2 * f + 4, 6, it)
                act.wait_ge(h_ready, at(f0 + f + 1, 3, it))
                nc.scalar.activation(tile_of(h[0], f, 3, it), tq[:], ACT.Copy).then_inc(h_hi_ready, 1)

            def ffn(up, down, f0, h, stat):
                spread(stat)
                up_step(up, f0, h, 0, None)
                with act.Fori(0, (KF - 1) // 3) as it:
                    for r in range(3):
                        up_step(up, f0, h, 1 + r, it)
                with act.Fori(0, KD // 2) as it:
                    for m in range(2):
                        for c in range(3):
                            split_hi(down + 3 * m + 3 + c, 6, it)
                        x_hi(stat + 1, m, 2, it)

            act.dma_start(xs_rows[0:TS, :], a["x_sample"].rearrange("b t d -> (b t) d")).then_inc(x_in[NB], 16)
            r0 = 0
            for name in ("g_ffn1", "g_mix", "g_ffn2", "g_ple", "b_out"):
                act.dma_start(rows[r0:r0 + 8, :], a[name][0].rearrange("(k p) -> k p", p=P)).then_inc(rows_in, 16)
                r0 += 8
            b_in = a["b_in"][0]
            for c in range(NKV):
                act.dma_start(rows[C_Q:C_Q + GQ, c * HD:(c + 1) * HD],
                              b_in[c * GQ * HD:(c + 1) * GQ * HD].rearrange("(j d) -> j d", d=HD)).then_inc(rows_in, 16)
            act.dma_start(rows[C_K:C_FIN, :], b_in[512:1792].rearrange("(k p) -> k p", p=P)).then_inc(rows_in, 16)
            act.dma_start(rows[C_FIN:N_COLS, :], a["g_final"].rearrange("(k p) -> k p", p=P)).then_inc(rows_in, 16)

            act.wait_ge(cols_ready, 1)
            for m in range(KD):
                if m % 2:
                    act.wait_ge(x_turned, m + 1)
                    nc.scalar.activation(x[:, m, 0:TP], ps[:, 2 * (1 + m % 3), :], ACT.Copy)
                    nc.scalar.activation(x[:, m, TP:T], ps[:, 2 * (1 + m % 3) + 1, 0:TS], ACT.Copy).then_inc(x_odd, 1)
                    act.wait_ge(x_odd, m // 2 + 1)
                else:
                    act.wait_ge(x_even, m // 2 + 1)
                nc.scalar.activation(xg_hi[:, m, :], x[:, m, :], ACT.Copy, scale=col(m)).then_inc(xg_hi_ready, 1)
                if m == 1:
                    split_hi(0)
            split_hi(1)
            for b in range(NB + 1):
                n, src = (P, x_rows[:, b, :]) if b < NB else (TS, xs_rows[0:TS, :])
                nc.scalar.activation(sq_rows[0:n, :], src, ACT.Square, accum_out=rs_t[0:n, b:b + 1]).then_inc(row_sums, 1)
                if b < NB:
                    act.wait_ge(row_sums, b + 1)
            split_hi(2)
            ffn(UP1, DOWN1, 0, h1, 0)

            act.wait_ge(unit_done, IN)
            act.dma_start(cache_k[:], a["cache_k_win"][0].rearrange("b w h d -> w b (h d)")).then_inc(cache_in, 16)
            act.dma_start(ws_rows[:], a["gm_w_s"][0].rearrange("g t s -> t g s")).then_inc(ws_in, 16)
            for dst, src in (
                (sink[:], a["attn_sinks"][0].partition_broadcast(P)),
                (cache_v[:], a["cache_v_win"][0].rearrange("b w h d -> w b (h d)")),
                (bs_all[:], a["gm_b_s"][0].partition_broadcast(P)),
                (lng[:], a["gm_ln_g"][0].partition_broadcast(P)),
                (lnb[:], a["gm_ln_b"][0].partition_broadcast(P)),
            ):
                act.dma_start(dst, src).then_inc(mix_in, 16)
            act.dma_start(w00[:], a["gm_w_s"][0, :, 0, 0].partition_broadcast(TS),
                          allow_slow_non_contiguous=True).then_inc(mix_in, 16)
            for r in range(TS):
                act.dma_start(s_sink[r * NQ:(r + 1) * NQ, :],
                              a["attn_sinks"][0].rearrange("(h o) -> h o", o=1)).then_inc(mix_in, 16)
            for dst, src in ((o["k_win_sample"], a["cache_k_win"]), (o["v_win_sample"], a["cache_v_win"])):
                act.dma_start(dst[0, :, 0:W - 1].rearrange("b w h d -> b (w h d)"),
                              src[0, :, 1:W].rearrange("b w h d -> b (w h d)")).then_inc(out_done, 16)

            n_gelu = 0
            for kind, *arg in steps:
                if kind == "gemm" and arg[1] == 0 and arg[0] > 0:
                    split_hi(IN + arg[0] + 2)
                elif kind == "out" and arg[0] == OUT_K[0]:
                    split_hi(OUT + 2)
                elif kind == "stat_spread":
                    spread(1)
                elif kind == "cache_turn":
                    act.wait_ge(cache_turned, 1)
                    nc.scalar.activation(cache_k_t[:], ps[:, 4:6, :].rearrange("p a (b w) -> p (a b) w", w=W),
                                         ACT.Copy).then_inc(cache_taken, 1)
                elif kind == "ws_turn":
                    act.wait_ge(ws_turned, 1)
                    nc.scalar.activation(ws_t[:], ps[:, 6, :].rearrange("p (g s) -> p g s", g=GG),
                                         ACT.Copy).then_inc(ws_taken, 1)
                elif kind == "evac":
                    u, name = arg[0], IN_ORDER[arg[0]]
                    j = int(name[1:] or 0)
                    c = {"q": C_Q, "k": C_K, "v": C_V, "u": C_U, "g": C_G}[name[0]] + j
                    act.wait_ge(z_scaled, u + 1)
                    if name[0] in "ug":
                        if n_gelu:
                            act.wait_ge(gelu_done, n_gelu)
                        n_gelu += 1
                        nc.scalar.activation(tb[:], ta[:], ACT.Square, bias=cols_g[:, c:c + 1],
                                             scale=GELU_K).then_inc(gelu_sq, 1)
                        nc.scalar.activation(tq[:], ta[:], ACT.Identity, bias=col(c)).then_inc(z_done, 1)
                    else:
                        dst = {"q": q_t[:, j, :], "k": k_t[:], "v": v_t[:]}[name[0]]
                        nc.scalar.activation(dst, ta[:], ACT.Identity, bias=col(c)).then_inc(z_done, 1)
                elif kind == "gelu_mid":
                    act.wait_ge(gelu_arg, n_gelu)
                    nc.scalar.activation(tb[:], tb[:], ACT.Tanh, scale=GELU_C).then_inc(gelu_tanh, 1)
                elif kind == "g_turn":
                    g, bank = arg[0], 4
                    act.wait_ge(g_turned, g + 1)
                    nc.scalar.activation(g_rows[:, 0:NB, g * P:(g + 1) * P],
                                         ps[:, bank, :].rearrange("p (b c) -> p b c", c=P), ACT.Copy)
                    nc.scalar.activation(g_rows[0:TS, NB, g * P:(g + 1) * P], ps[0:TS, bank + 1, 0:P],
                                         ACT.Copy).then_inc(g_taken, 1)
                elif kind == "kv_turn":
                    act.wait_ge(kv_turned, 1)
                    nc.scalar.activation(v_rows[:, 0:NB, :], ps[:, 6, :].rearrange("p (b c) -> p b c", c=P),
                                         ACT.Copy).then_inc(kv_taken, 1)
                    nc.scalar.activation(v_rows[0:TS, NB, :], ps[0:TS, 7, 0:P], ACT.Copy).then_inc(kv_taken, 1)
                    nc.scalar.activation(k_rows[:, 0, :], ps[:, 7, P:2 * P], ACT.Copy).then_inc(kv_taken, 1)
                    nc.scalar.activation(k_rows[0:TS, 1, :], ps[0:TS, 7, 2 * P:3 * P], ACT.Copy).then_inc(kv_taken, 1)
                    act.wait_ge(kv_taken, 4)
                    act.dma_start(o["v_win_prompt"][0, 0].rearrange("w h d -> w (h d)"), v_rows[:, NB - 1, :]
                                  ).then_inc(out_done, 16)
                    act.dma_start(o["k_win_prompt"][0, 0].rearrange("w h d -> w (h d)"), k_rows[:, 0, :]
                                  ).then_inc(out_done, 16)
                    act.dma_start(o["v_win_sample"][0, :, W - 1].rearrange("b h d -> b (h d)"), v_rows[0:TS, NB, :]
                                  ).then_inc(out_done, 16)
                    act.dma_start(o["k_win_sample"][0, :, W - 1].rearrange("b h d -> b (h d)"), k_rows[0:TS, 1, :]
                                  ).then_inc(out_done, 16)
                elif kind == "soft":
                    i = arg[0]
                    c0 = 16 * (i % 2)
                    act.wait_ge(max_ready, i + 1)
                    for c in range(4):
                        item = probs[:, i % 2, c // 2, c % 2, :]
                        nc.scalar.activation(item, item, ACT.Exp, bias=st[:, c0 + c:c0 + c + 1],
                                             accum_out=st[:, c0 + 8 + c:c0 + 9 + c]).then_inc(exp_done, 1)
                    nc.scalar.activation(st[:, c0 + 4:c0 + 8], st[:, c0 + 4:c0 + 8], ACT.Exp).then_inc(exp_done, 1)
                elif kind == "p_turn":
                    i, b = arg
                    act.wait_ge(probs_turned, 2 * i + b + 1)
                    nc.scalar.activation(probs_t[:, b].rearrange("p c k q -> p (c k q)"), ps[:, 6, :],
                                         ACT.Copy).then_inc(probs_taken, 1)
                elif kind == "o_turn":
                    i = arg[0]
                    act.wait_ge(o_turned, i + 1)
                    nc.scalar.activation(mix_hi[:, i // 2, 256 * (i % 2):256 * (i % 2) + 256], ps[:, 7, 256:512],
                                         ACT.Copy).then_inc(o_hi, 1)
                elif kind == "spatial" and arg[0] < 2:
                    b = NB - 1 + arg[0]
                    act.wait_ge(g_normed[1], b - NB + 2)
                    if b == NB - 1:
                        act.dma_start(o["gm_v_prompt"][0, 0], g_rows[:, b, :]).then_inc(out_done, 16)
                    else:
                        act.dma_start(o["gm_v_sample"][0].rearrange("b t c -> (b t) c"), g_rows[0:TS, b, :]
                                      ).then_inc(out_done, 16)
                elif kind == "gm":
                    g = arg[0]
                    act.wait_ge(gm_ready, g + 1)
                    nc.scalar.activation(mix_hi[:, 4 + g, :], sp[:], ACT.Copy, scale=0.5).then_inc(gm_hi, 1)
                elif kind == "s_softmax":
                    act.wait_ge(s_max, 1)
                    nc.scalar.activation(s_p[:], s_p[:], ACT.Exp, bias=s_st[:, 0:1],
                                         accum_out=s_st[:, 2:3]).then_inc(s_exp, 1)
                    nc.scalar.activation(s_st[:, 1:2], s_st[:, 1:2], ACT.Exp).then_inc(s_exp, 1)
                elif kind == "s_values":
                    act.wait_ge(s_out, 1)
                    for c in range(NKV):
                        part = slice(c * HD, (c + 1) * HD)
                        nc.scalar.activation(mix_hi[part, 0:4, TP:T],
                                             s_o[part, :, c * GQ:(c + 1) * GQ].rearrange("p s j -> p j s"),
                                             ACT.Copy).then_inc(s_hi, 1)

            for m in range(KD):
                split_hi(OUT + m + 3)
                x_hi(2, m)
            act.wait_ge(out_done, 16 * 8)
            ffn(UP2, DOWN2, KF, h2, 2)

            act.wait_ge(unit_done, LAST)
            nc.scalar.activation(p_hi[:], p_t[:], ACT.Copy).then_inc(pple_hi, 1)
            split_hi(LAST + 3)
            split_hi(LAST + 4)
            split_hi(LAST + 5)
            spread(3)
            for m in range(KD):
                if m:
                    split_hi(LAST + 5 + m)
                    act.wait_ge(gated, m)
                act.wait_ge(z_ready, m + 1)
                nc.scalar.activation(tb[:], ta[:], ACT.Tanh, scale=0.5).then_inc(gate_ready, 1)
                act.wait_ge(sq_added, 28 + m)
                act.wait_ge(x_ready, 24 + m + 1)
                nc.scalar.activation(sq[:], x[:, m, :], ACT.Square).then_inc(sq_made, 1)
            act.wait_ge(rs_ready, 1)
            for b in (1, 3):
                act.wait_ge(y_turned, b + 1)
                nc.scalar.activation(y[:, b, :].rearrange("p (a c) -> p a c", a=2), ps[:, 2 * Y_PAIR[b]:2 * Y_PAIR[b] + 2, :],
                                     ACT.Copy, scale=rs[:, b:b + 1]).then_inc(y_ready[b], 1)

        @block.gpsimd
        def _(pool):
            def split_lo(n, step=0, it=None):
                if n >= END:
                    return
                pool.wait_ge(w_hi_ready, at(n + 1, step, it))
                nc.gpsimd.tensor_tensor(w_lo[:, n % RING, :], w_raw[:, n % RING, :],
                                        w_hi[:, n % RING, :].bitcast(F32), ALU.subtract).then_inc(w_lo_ready, 1)

            def clear_ssq(stat):
                if stat > 1:
                    pool.wait_ge(stat_summed, stat - 1)
                nc.gpsimd.memset(ssq[:], 0.0).then_inc(sq_added, 1)

            def add_square(stat, m, step=0, it=None):
                pool.wait_ge(sq_added, 9 * stat - 8)
                pool.wait_ge(sq_made, at(8 * stat + m - 7, step, it))
                nc.gpsimd.tensor_tensor(ssq[:], ssq[:], sq[:], ALU.add).then_inc(sq_added, 1)

            def ffn(up, down, stat):
                split_lo(up + 3)
                split_lo(up + 4)
                with pool.Fori(0, (KF - 1) // 3) as it:
                    for r in range(3):
                        split_lo(up + 2 * (1 + r) + 3, 6, it)
                        split_lo(up + 2 * (1 + r) + 4, 6, it)
                clear_ssq(stat + 1)
                with pool.Fori(0, KD // 2) as it:
                    for m in range(2):
                        for c in range(3):
                            split_lo(down + 3 * m + 3 + c, 6, it)
                        add_square(stat + 1, m, 2, it)

            nc.gpsimd.memset(ident[:], 0.0).then_inc(consts_ready, 1)
            nc.gpsimd.memset(ones[:], 1.0).then_inc(consts_ready, 1)
            nc.gpsimd.memset(var[:], 1.0).then_inc(consts_ready, 1)
            pool.wait_ge(consts_ready, 3)
            nc.gpsimd.affine_select(out=ident[:], in_=ident[:], compare_op=ALU.not_equal, fill=1.0, base=0,
                                    pattern=[[-1, P]], channel_multiplier=1).then_inc(consts_ready, 1)
            for n in range(RING):
                split_lo(n)
            ffn(UP1, DOWN1, 0)

            clear_ssq(2)
            pool.wait_ge(unit_done, IN)
            nc.gpsimd.memset(mask[:], 0.0).then_inc(mask_ready, 1)
            nc.gpsimd.memset(q_diag[:], 0.0).then_inc(s_diag_clear, 1)
            pool.wait_ge(mask_ready, 1)
            nc.gpsimd.affine_select(out=mask[:, 0, :], in_=mask[:, 0, :], compare_op=ALU.is_ge, fill=NEG, base=0,
                                    pattern=[[-1, 2 * W]], channel_multiplier=1).then_inc(mask_ready, 1)
            nc.gpsimd.affine_select(out=mask[:, 1, :], in_=mask[:, 1, :], compare_op=ALU.is_ge, fill=NEG, base=W,
                                    pattern=[[-1, 2 * W]], channel_multiplier=1).then_inc(mask_ready, 1)
            pool.wait_ge(mask_ready, 3)
            nc.gpsimd.affine_select(out=mask[:, 1, :], in_=mask[:, 1, :], compare_op=ALU.is_ge, fill=NEG, base=0,
                                    pattern=[[1, 2 * W]], channel_multiplier=-1).then_inc(mask_ready, 1)
            for kind, *arg in steps:
                if kind == "gemm" and arg[1] == 0 and arg[0] > 0:
                    split_lo(IN + arg[0] + 2)
                elif kind == "out" and arg[0] == OUT_K[0]:
                    split_lo(OUT + 2)
                elif kind == "norm" and arg[0] >= NB - 1:
                    b = arg[0]
                    n = P if b < NB else TS
                    v = g_rows[0:n, b, :]
                    pool.wait_ge(g_centred, b - NB + 2)
                    nc.gpsimd.tensor_tensor(v, v, lng[0:n, :], ALU.mult).then_inc(g_gained, 1)
                    pool.wait_ge(g_gained, b - NB + 2)
                    nc.gpsimd.tensor_tensor(v, v, lnb[0:n, :], ALU.add).then_inc(g_normed[1], 1)
                elif kind == "ws_turn":
                    pool.wait_ge(ws_taken, 1)
                    nc.gpsimd.affine_select(out=ws_t[:], in_=ws_t[:], compare_op=ALU.is_ge, fill=0.0, base=0,
                                            pattern=[[0, GG], [1, P]], channel_multiplier=-1).then_inc(ws_ready, 1)

            for m in range(KD):
                split_lo(OUT + m + 3)
                add_square(2, m)
            ffn(UP2, DOWN2, 2)
            clear_ssq(4)
            for n in range(LAST + 3, LAST + 6):
                split_lo(n)
            for m in range(KD):
                if m:
                    split_lo(LAST + 5 + m)
                add_square(4, m)

        @block.vector
        def _(dve):
            chain = [0]

            def link(ins):
                chain[0] += 1
                ins.then_inc(dve_step, 1)
                dve.wait_ge(dve_step, chain[0])

            def rsqrt():
                link(nc.vector.tensor_scalar(rs_i[:], var[:].bitcast(I32), 1, None, ALU.logical_shift_right))
                link(nc.vector.tensor_scalar(rs[:].bitcast(I32), rs_i[:], -1.0, RSQRT_SEED, ALU.mult, ALU.add))
                for _ in range(3):
                    link(nc.vector.tensor_tensor(rs_t[:], rs[:], rs[:], ALU.mult))
                    link(nc.vector.tensor_tensor(rs_t[:], rs_t[:], var[:], ALU.mult))
                    link(nc.vector.tensor_scalar(rs_t[:], rs_t[:], -0.5, 1.5, ALU.mult, ALU.add))
                    link(nc.vector.tensor_tensor(rs[:], rs[:], rs_t[:], ALU.mult))

            def stat_rsqrt(stat):
                if stat:
                    dve.wait_ge(stat_summed, stat)
                    sums = ps[:, STAT_BANK[stat], 0:NB + 1]
                else:
                    dve.wait_ge(row_sums, NB + 1)
                    sums = rs_t[:, 0:NB + 1]
                link(nc.vector.tensor_scalar(var[:, 0:NB], sums[:, 0:NB], 1.0 / D, RMS_EPS, ALU.mult, ALU.add))
                link(nc.vector.tensor_scalar(var[0:TS, NB:NB + 1], sums[0:TS, NB:NB + 1], 1.0 / D, RMS_EPS,
                                             ALU.mult, ALU.add))
                rsqrt()

            def stat_diag(stat):
                stat_rsqrt(stat)
                nc.vector.tensor_tensor(diag[:, 0:TP].rearrange("p (b t) -> p b t", t=P),
                                        ident[:].unsqueeze(1).broadcast_to([P, NB, P]),
                                        rs[:, 0:NB].unsqueeze(2).broadcast_to([P, NB, P]),
                                        ALU.mult).then_inc(diag_ready, 1)
                nc.vector.tensor_scalar(diag[0:TS, TP:T], ident[0:TS, 0:TS], rs[0:TS, NB:NB + 1], None,
                                        ALU.mult).then_inc(diag_ready, 1)

            def x_lo(stat, m, step=0, it=None):
                dve.wait_ge(xg_hi_ready, at(8 * stat + m + 1, step, it))
                nc.vector.scalar_tensor_tensor(out=tile_of(xg_lo, m, step, it), in0=tile_of(x, m, step, it),
                                               scalar=col(8 * stat + m, step, it),
                                               in1=tile_of(xg_hi, m, step, it).bitcast(F32),
                                               op0=ALU.mult, op1=ALU.subtract).then_inc(xg_lo_ready, 1)

            def take_turned(dst, p):
                nc.vector.tensor_copy(dst[:, 0:TP], ps[:, 2 * p, :])
                return nc.vector.tensor_copy(dst[:, TP:T], ps[:, 2 * p + 1, 0:TS])

            def up_step(base, f0, h, f, it):
                if f0 + f:
                    dve.wait_ge(tanh_ready, at(f0 + f, 3, it))
                dve.wait_ge(unit_done, at(base + 2 * f + 1, 6, it))
                nc.vector.tensor_tensor(halves(ta[:]), pair(2 * f % 3), halves(rstd[:]), ALU.mult).then_inc(a_ready, 1)
                if f0 + f:
                    dve.wait_ge(h_lo_ready, at(f0 + f, 3, it))
                dve.wait_ge(a_ready, at(f0 + f + 1, 3, it))
                dve.wait_ge(unit_done, at(base + 2 * f + 2, 6, it))
                nc.vector.tensor_tensor(halves(tq[:]), pair((2 * f + 1) % 3), halves(ta[:]),
                                        ALU.mult).then_inc(ab_ready, 1)
                dve.wait_ge(ab_ready, at(f0 + f + 1, 3, it))
                nc.vector.tensor_tensor(tq[:], tq[:], rstd[:], ALU.mult).then_inc(ab_scaled, 1)
                dve.wait_ge(tanh_ready, at(f0 + f + 1, 3, it))
                dve.wait_ge(ab_scaled, at(f0 + f + 1, 3, it))
                nc.vector.scalar_tensor_tensor(out=tq[:], in0=tb[:], scalar=1.0, in1=tq[:], op0=ALU.add,
                                               op1=ALU.mult).then_inc(h_ready, 1)
                dve.wait_ge(h_hi_ready, at(f0 + f + 1, 3, it))
                nc.vector.tensor_tensor(tile_of(h[1], f, 3, it), tq[:], tile_of(h[0], f, 3, it).bitcast(F32),
                                        ALU.subtract).then_inc(h_lo_ready, 1)

            def down_step(base, stat, m, it):
                dve.wait_ge(unit_done, at(base + 3 * m + 3, 6, it))
                nc.vector.scalar_tensor_tensor(out=halves(tile_of(x, m, 2, it)), in0=pair(m % 2), scalar=0.25,
                                               in1=halves(tile_of(x, m, 2, it)), op0=ALU.mult,
                                               op1=ALU.add).then_inc(x_ready, 1)
                x_lo(stat, m, 2, it)

            def ffn(up, down, f0, h, stat):
                dve.wait_ge(rstd_ready, 2 * (stat + 1))
                up_step(up, f0, h, 0, None)
                with dve.Fori(0, (KF - 1) // 3) as it:
                    for r in range(3):
                        up_step(up, f0, h, 1 + r, it)
                if stat == 0:
                    for k in range(KP):
                        dve.wait_ge(p_turned, k + 1)
                        take_turned(p_t[:, k, :], 3 - k).then_inc(p_ready, 1)
                with dve.Fori(0, KD // 2) as it:
                    for m in range(2):
                        down_step(down, stat + 1, m, it)

            dve.wait_ge(cols_turned, 1)
            nc.vector.tensor_copy(cols[:, 0:N_COLS], ps[:, 6, 0:N_COLS]).then_inc(cols_ready, 1)
            dve.wait_ge(cols_ready, 1)
            nc.vector.tensor_scalar(cols_g[:, 0:N_COLS], cols[:, 0:N_COLS], GELU_K, None, ALU.mult)
            for m in range(0, KD, 2):
                dve.wait_ge(x_turned, m + 1)
                take_turned(x[:, m, :], 1 + m % 3).then_inc(x_even, 1)
                if m:
                    x_lo(0, m - 1)
                x_lo(0, m)
            x_lo(0, KD - 1)
            stat_diag(0)
            ffn(UP1, DOWN1, 0, h1, 0)

            n_gelu = 0
            for kind, *arg in steps:
                if kind == "stat_sum":
                    stat_diag(1)
                elif kind == "evac":
                    u, name = arg[0], IN_ORDER[arg[0]]
                    if u == 0:
                        dve.wait_ge(rstd_ready, 4)
                    else:
                        dve.wait_ge(z_done, u)
                    dve.wait_ge(unit_done, IN + u + 1)
                    nc.vector.tensor_tensor(halves(ta[:]), pair(IN_PAIR[u]), halves(rstd[:]),
                                            ALU.mult).then_inc(z_scaled, 1)
                    if name[0] in "ug":
                        n_gelu += 1
                    if name == "k":
                        dve.wait_ge(mix_in, 16 * mix_loads)
                        nc.vector.tensor_tensor(w00_diag[:], ident[0:TS, 0:TS].unsqueeze(1).broadcast_to([TS, GG, TS]),
                                                w00[:].unsqueeze(2).broadcast_to([TS, GG, TS]),
                                                ALU.mult).then_inc(w00_ready, 1)
                elif kind == "gelu_mid":
                    dve.wait_ge(gelu_sq, n_gelu)
                    dve.wait_ge(z_done, arg[0] + 1)
                    nc.vector.scalar_tensor_tensor(out=tb[:], in0=tb[:], scalar=1.0, in1=tq[:], op0=ALU.add,
                                                   op1=ALU.mult).then_inc(gelu_arg, 1)
                elif kind == "gelu_end":
                    name = IN_ORDER[arg[0]]
                    g = int(name[1])
                    if name[0] == "g" and g:
                        dve.wait_ge(g_turned, g)
                    dve.wait_ge(gelu_tanh, n_gelu)
                    nc.vector.scalar_tensor_tensor(out=g_t[:] if name[0] == "g" else gu[:, g % 2, :], in0=tb[:],
                                                   scalar=1.0, in1=tq[:], op0=ALU.add,
                                                   op1=ALU.mult).then_inc(gelu_done, 1)
                elif kind == "soft":
                    i = arg[0]
                    j, bp, c0 = i // 2, i % 2, 16 * (i % 2)
                    dst = probs[:, bp]
                    dve.wait_ge(scored, i + 1)
                    if i == 0:
                        dve.wait_ge(mask_ready, 4)
                    if i >= 2:
                        dve.wait_ge(probs_turned, 2 * (i - 1))
                    for c in range(NKV):
                        for r in range(2):
                            ins = nc.vector.tensor_tensor_reduce(
                                out=dst[:, c, r, :], in0=ps[:, 4 + c, r * 2 * W:(r + 1) * 2 * W],
                                in1=mask[:, 1 if bp else r, :], scale=SCALE, scalar=sink[:, c * GQ + j:c * GQ + j + 1],
                                op0=ALU.add, op1=ALU.max, accum_out=st[:, c0 + 12 + 2 * c + r:c0 + 13 + 2 * c + r])
                    ins.then_inc(masked, 1)
                    dve.wait_ge(masked, i + 1)
                    link(nc.vector.tensor_scalar(st[:, c0:c0 + 4], st[:, c0 + 12:c0 + 16], -1.0, None, ALU.mult))
                    nc.vector.tensor_tensor(st[:, c0 + 4:c0 + 8].rearrange("p (c b) -> p c b", c=NKV),
                                            st[:, c0:c0 + 4].rearrange("p (c b) -> p c b", c=NKV),
                                            sink[:].rearrange("p (c j) -> p c j", c=NKV)[:, :, j:j + 1]
                                            .broadcast_to([P, NKV, 2]), ALU.add).then_inc(max_ready, 1)
                elif kind == "p_turn" and arg[1] == 0:
                    i = arg[0]
                    c0 = 16 * (i % 2)
                    dve.wait_ge(exp_done, 5 * (i + 1))
                    link(nc.vector.tensor_tensor(st[:, c0 + 12:c0 + 16], st[:, c0 + 8:c0 + 12], st[:, c0 + 4:c0 + 8],
                                                 ALU.add))
                    link(nc.vector.reciprocal(st[:, c0 + 12:c0 + 16], st[:, c0 + 12:c0 + 16]))
                elif kind == "values":
                    i = arg[0]
                    c0 = 16 * (i % 2)
                    dve.wait_ge(o_made, i + 1)
                    if i:
                        dve.wait_ge(o_turned, i)
                    nc.vector.tensor_tensor(
                        o_rows[:], ps[:, 7, 0:256].rearrange("p (b c d) -> p b c d", b=2, c=NKV),
                        st[:, c0 + 12:c0 + 16].rearrange("p (c b) -> p b c", c=NKV).unsqueeze(3)
                        .broadcast_to([P, 2, NKV, HD]), ALU.mult).then_inc(o_taken, 1)
                elif kind == "o_turn":
                    i = arg[0]
                    part = slice(256 * (i % 2), 256 * (i % 2) + 256)
                    dve.wait_ge(o_hi, i + 1)
                    nc.vector.tensor_tensor(mix_lo[:, i // 2, part], ps[:, 7, 256:512],
                                            mix_hi[:, i // 2, part].bitcast(F32), ALU.subtract).then_inc(o_lo, 1)
                elif kind == "norm_stats":
                    dve.wait_ge(g_taken, GG)
                    for b in range(NB + 1):
                        n = P if b < NB else TS
                        link(nc.vector.bn_stats(bn[0:n, b, :], g_rows[0:n, b, :]))
                        link(nc.vector.bn_aggr(mv[0:n, b, :], bn[0:n, b, :]))
                        link(nc.vector.tensor_scalar(var[0:n, b:b + 1], mv[0:n, b, 1:2], 4 * LN_EPS, None, ALU.add))
                    rsqrt()
                elif kind == "norm":
                    b = arg[0]
                    n = P if b < NB else TS
                    v = g_rows[0:n, b, :]
                    ins = nc.vector.tensor_scalar(v, v, mv[0:n, b, 0:1], rs[0:n, b:b + 1], ALU.subtract, ALU.mult)
                    if b >= NB - 1:
                        ins.then_inc(g_centred, 1)
                    else:
                        link(ins)
                        link(nc.vector.tensor_tensor(v, v, lng[0:n, :], ALU.mult))
                        nc.vector.tensor_tensor(v, v, lnb[0:n, :], ALU.add).then_inc(g_normed[0], 1)
                elif kind == "spatial":
                    g = arg[0]
                    dve.wait_ge(spatial_made, g + 1)
                    if g:
                        dve.wait_ge(gm_lo, g)
                    nc.vector.tensor_tensor(sp[:, 0:TP].rearrange("p (b t) -> p b t", t=P),
                                            ps[:, 4, :].rearrange("p (b t) -> p b t", t=P),
                                            bs_all[:, g:g + 1, :].broadcast_to([P, NB, P]), ALU.add)
                    nc.vector.tensor_scalar(sp[:, TP:T], ps[:, 5, 384:384 + TS], bs_all[:, g, 0:1], None,
                                            ALU.add).then_inc(spatial_taken, 1)
                elif kind == "gm":
                    g = arg[0]
                    dve.wait_ge(spatial_taken, g + 1)
                    dve.wait_ge(gelu_done, GG + g + 1)
                    nc.vector.tensor_tensor(sp[:], sp[:], gu[:, g % 2, :], ALU.mult).then_inc(gm_ready, 1)
                    dve.wait_ge(gm_hi, g + 1)
                    nc.vector.scalar_tensor_tensor(out=mix_lo[:, 4 + g, :], in0=sp[:], scalar=0.5,
                                                   in1=mix_hi[:, 4 + g, :].bitcast(F32), op0=ALU.mult,
                                                   op1=ALU.subtract).then_inc(gm_lo, 1)
                elif kind == "s_build":
                    dve.wait_ge(s_diag_clear, 1)
                    dve.wait_ge(z_done, IN_ORDER.index("q3") + 1)
                    for c in range(NKV):
                        part = slice(c * HD, (c + 1) * HD)
                        link(nc.vector.tensor_copy(q_diag[part, :, c * GQ:(c + 1) * GQ],
                                                   q_t[part, :, TP:T].rearrange("p j s -> p s j")))
                    nc.vector.tensor_tensor(qk_new[:], q_diag[:], k_t[:, TP:T].unsqueeze(2).broadcast_to([P, TS, NQ]),
                                            ALU.mult).then_inc(s_built, 1)
                elif kind == "s_scores":
                    dve.wait_ge(s_scored, 1)
                    nc.vector.tensor_copy(s_keys[:], ps[:, 5, 0:64]).then_inc(s_taken, 1)
                elif kind == "s_softmax":
                    dve.wait_ge(s_turned, 1)
                    link(nc.vector.tensor_scalar(s_p[:, 0:W], ps[0:64, 5, 128:256], SCALE, None, ALU.mult))
                    link(nc.vector.tensor_scalar(s_p[:, W:W + 1], ps[0:64, 5, 64:65], SCALE, None, ALU.mult))
                    link(nc.vector.tensor_reduce(s_st[:, 3:4], s_p[:], AX_X, ALU.max))
                    link(nc.vector.tensor_tensor(s_st[:, 3:4], s_st[:, 3:4], s_sink[:], ALU.max))
                    link(nc.vector.tensor_scalar(s_st[:, 0:1], s_st[:, 3:4], -1.0, None, ALU.mult))
                    nc.vector.tensor_tensor(s_st[:, 1:2], s_st[:, 0:1], s_sink[:], ALU.add).then_inc(s_max, 1)
                    dve.wait_ge(s_exp, 2)
                    link(nc.vector.tensor_tensor(s_st[:, 4:5], s_st[:, 1:2], s_st[:, 2:3], ALU.add))
                    link(nc.vector.reciprocal(s_st[:, 5:6], s_st[:, 4:5]))
                    link(nc.vector.tensor_scalar(s_p[:], s_p[:], s_st[:, 5:6], None, ALU.mult))
                    nc.vector.tensor_scalar(s_new[:], ident[0:64, 0:64], s_p[:, W:W + 1], None,
                                            ALU.mult).then_inc(s_normed, 1)
                elif kind == "s_probs":
                    dve.wait_ge(s_p_turned, 1)
                    nc.vector.tensor_copy(s_pt[:], ps[:, 5, 0:64]).then_inc(s_p_taken, 1)
                    nc.vector.tensor_tensor(s_pv[:], ps[:, 5, 64:128].rearrange("p (s h) -> p s h", s=TS),
                                            v_t[:, TP:T].unsqueeze(2).broadcast_to([P, TS, NQ]),
                                            ALU.mult).then_inc(s_p_taken, 1)
                elif kind == "s_values":
                    dve.wait_ge(s_valued, 1)
                    dve.wait_ge(s_p_taken, 2)
                    nc.vector.tensor_tensor(s_o[:], ps[:, 5, 256:320].rearrange("p (s h) -> p s h", s=TS), s_pv[:],
                                            ALU.add).then_inc(s_out, 1)
                    for c in range(NKV):
                        part = slice(c * HD, (c + 1) * HD)
                        dve.wait_ge(s_hi, c + 1)
                        nc.vector.tensor_tensor(mix_lo[part, 0:4, TP:T],
                                                s_o[part, :, c * GQ:(c + 1) * GQ].rearrange("p s j -> p j s"),
                                                mix_hi[part, 0:4, TP:T].bitcast(F32), ALU.subtract).then_inc(s_lo, 1)

            for m in range(KD):
                dve.wait_ge(unit_done, OUT + m + 1)
                nc.vector.scalar_tensor_tensor(out=halves(x[:, m, :]), in0=pair((m + 1) % 3), scalar=col(C_BOUT + m),
                                               in1=halves(x[:, m, :]), op0=ALU.add,
                                               op1=ALU.add).then_inc(x_ready, 1)
                x_lo(2, m)
            stat_diag(2)
            ffn(UP2, DOWN2, KF, h2, 2)

            dve.wait_ge(pple_hi, 1)
            nc.vector.tensor_tensor(p_lo[:], p_t[:], p_hi[:].bitcast(F32), ALU.subtract).then_inc(pple_lo, 1)
            for m in range(KD):
                if m % 4 == 3:
                    dve.wait_ge(unit_done, LAST + 2 + m // 4)
                else:
                    dve.wait_ge(pp_made, 3 * (m // 4) + m % 4 + 1)
                nc.vector.tensor_copy(halves(pp[:, m, :]), pair(1 + m % 2)).then_inc(pp_ready, 1)
            stat_diag(3)
            for m in range(KD):
                if m == 0:
                    dve.wait_ge(rstd_ready, 8)
                else:
                    dve.wait_ge(gate_ready, m)
                dve.wait_ge(unit_done, LAST + 1 if m == 0 else LAST + 3 + m)
                nc.vector.tensor_tensor(halves(ta[:]), pair(m % 3), halves(rstd[:]), ALU.mult).then_inc(z_ready, 1)
                dve.wait_ge(gate_ready, m + 1)
                nc.vector.scalar_tensor_tensor(out=tq[:], in0=tb[:], scalar=1.0, in1=pp[:, m, :], op0=ALU.add,
                                               op1=ALU.mult).then_inc(gated, 1)
                dve.wait_ge(gated, m + 1)
                nc.vector.scalar_tensor_tensor(out=x[:, m, :], in0=tq[:], scalar=0.5, in1=x[:, m, :], op0=ALU.mult,
                                               op1=ALU.add).then_inc(x_ready, 1)
                dve.wait_ge(x_ready, 24 + m + 1)
                nc.vector.tensor_scalar(xf[:, m, :], x[:, m, :], col(C_FIN + m), None, ALU.mult).then_inc(xf_ready, 1)

            stat_rsqrt(4)
            nc.vector.tensor_copy(rs_t[:], rs[:]).then_inc(rs_ready, 1)
            for b in (0, 2, 4):
                n = P if b < NB else TS
                dve.wait_ge(y_turned, b + 1)
                nc.vector.tensor_scalar(y[0:n, b, :].rearrange("p (a c) -> p a c", a=2),
                                        ps[0:n, 2 * Y_PAIR[b]:2 * Y_PAIR[b] + 2, :], rs[0:n, b:b + 1], None,
                                        ALU.mult).then_inc(y_ready[b], 1)

        @block.tensor
        def _(pe):
            def k_step(n, k, src, sk, p, first, last):
                for i, (w, m_) in enumerate(((w_hi, src[0]), (w_hi, src[1]), (w_lo, src[0]))):
                    for h in range(2):
                        ins = pe.matmul(ps[:, 2 * p + h, 0:HALF], w[:, n % RING, k * P:(k + 1) * P],
                                        m_[:, sk, h * HALF:(h + 1) * HALF],
                                        start=(first and i == 0), stop=(last and i == 2))
                return ins

            def unit(n, src, p, sk0=0, kn=KD, first=True, last=True, step=0, it=None, ready=None,
                     between=()):
                pe.wait_ge(w_lo_ready, at(n + 1, step, it))
                for k in range(kn):
                    if ready:
                        pe.wait_ge(ready[0], ready[1] + k + 1)
                    for k_, stage in between:
                        if k_ == k:
                            stage()
                    ins = k_step(n, k, src, sk0 + k, p, first and k == 0, last and k == kn - 1)
                ins.then_inc(unit_done, 1)

            def stat_sum(stat):
                pe.wait_ge(sq_added, 9 * stat)
                bank = STAT_BANK[stat]
                for b in range(NB + 1):
                    n = P if b < NB else TS
                    ins = pe.matmul(ps[0:n, bank, b:b + 1], ssq[:, b * P:b * P + n], ones[:, 0:1], start=True, stop=True)
                ins.then_inc(stat_summed, 1)

            def stat_out(stat):
                pe.wait_ge(diag_ready, 2 * (stat + 1))
                pe.matmul(ps[:, 6, :], ones[:], diag[:, 0:TP], start=True, stop=True)
                pe.matmul(ps[:, 7, 8:8 + TS], ones[0:TS, :], diag[0:TS, TP:T], start=True,
                          stop=True).then_inc(stat_spread, 1)

            def turn(dst, src, n=P):
                return pe.transpose(dst, src, ident[0:n, 0:n])

            def turn_tile(rows_, s_rows, c, p):
                for b in range(NB):
                    turn(ps[:, 2 * p, b * P:(b + 1) * P], rows_[:, b, c * P:(c + 1) * P])
                return turn(ps[:, 2 * p + 1, 0:TS], s_rows[0:TS, c * P:(c + 1) * P], TS)

            def up_step(base, f0, f, it, src):
                pe.wait_ge(a_ready, at(f0 + f, 3, it))
                unit(base + 2 * f, src, 2 * f % 3, step=6, it=it)
                unit(base + 2 * f + 1, src, (2 * f + 1) % 3, step=6, it=it)

            def down_step(base, f0, stat, h, m, it):
                pe.wait_ge(xg_lo_ready, at(8 * stat + m - 1, 2, it))
                for c, kn in enumerate(DOWN_K):
                    pe.wait_ge(h_lo_ready, f0 + 8 * c + kn)
                    unit(base + 3 * m + c, h, m % 2, 8 * c, kn, c == 0, c == 2, 6, it)

            def ffn(up, down, f0, h, stat, src):
                with pe.Fori(0, (KF - 1) // 3) as it:
                    for r in range(3):
                        up_step(up, f0, 1 + r, it, src)
                if stat == 0:
                    pe.wait_ge(p_in, 16)
                    pe.wait_ge(ps_in, 16)
                    turn_tile(p_rows, ps_rows, 0, 3).then_inc(p_turned, 1)
                    pe.wait_ge(a_ready, KF)
                    turn_tile(p_rows, ps_rows, 1, 2).then_inc(p_turned, 1)
                pe.wait_ge(a_ready, f0 + KF)
                with pe.Fori(0, KD // 2) as it:
                    for m in range(2):
                        down_step(down, f0, stat + 1, h, m, it)

            xg = xg_hi, xg_lo

            pe.wait_ge(consts_ready, 4)
            pe.wait_ge(rows_in, 16 * 9)
            pe.transpose(ps[:, 6, 0:N_COLS], rows[0:N_COLS, :], ident[0:N_COLS, 0:N_COLS]).then_inc(cols_turned, 1)
            for s_ in x_in:
                pe.wait_ge(s_, 16)
            for m in range(KD):
                if m >= 3:
                    pe.wait_ge((x_odd, x_even)[m % 2], (m - 3) // 2 + 1)
                elif m == 2:
                    pe.wait_ge(cols_ready, 1)
                turn_tile(x_rows, xs_rows, m, 1 + m % 3).then_inc(x_turned, 1)

            unit(UP1, xg, 0, ready=(xg_lo_ready, 0))
            unit(UP1 + 1, xg, 1)
            stat_out(0)
            ffn(UP1, DOWN1, 0, h1, 0, xg)

            for kind, *arg in steps:
                if kind == "gemm":
                    u, k = arg
                    n = IN + u
                    if k == 0:
                        if u < 2:
                            pe.wait_ge(x_ready, 7 + u)
                        if u == 2:
                            pe.wait_ge(cache_taken, 1)
                        if u >= 3:
                            pe.wait_ge(z_scaled, u - 1 if u > 3 else 1)
                        pe.wait_ge(w_lo_ready, n + 1)
                    if u == 0:
                        pe.wait_ge(xg_lo_ready, 8 + k + 1)
                    ins = k_step(n, k, xg, k, IN_PAIR[u], k == 0, k == KD - 1)
                    if k == KD - 1:
                        ins.then_inc(unit_done, 1)
                elif kind == "out":
                    k = arg[0]
                    if k == OUT_K[0]:
                        pe.wait_ge(w_lo_ready, OUT + 1)
                        pe.wait_ge(z_scaled, 13)
                    if k >= 4:
                        pe.wait_ge(gm_lo, k - 3)
                    elif k == 0:
                        pe.wait_ge(s_lo, 2)
                    elif k == 3:
                        pe.wait_ge(o_lo, 8)
                    ins = k_step(OUT, k, (mix_hi, mix_lo), k, 1, k == OUT_K[0], k == OUT_K[7])
                    if k == OUT_K[7]:
                        ins.then_inc(unit_done, 1)
                elif kind == "stat_sum":
                    stat_sum(1)
                elif kind == "stat_spread":
                    stat_out(1)
                elif kind == "cache_turn":
                    pe.wait_ge(cache_in, 16)
                    for b in range(TS):
                        ins = turn(ps[:, 4 + b // 4, (b % 4) * W:(b % 4 + 1) * W], cache_k[:, b, :])
                    ins.then_inc(cache_turned, 1)
                elif kind == "ws_turn":
                    pe.wait_ge(ws_in, 16)
                    pe.wait_ge(rstd_ready, 4)
                    for g in range(GG):
                        ins = turn(ps[:, 6, g * P:(g + 1) * P], ws_rows[:, g, :])
                    ins.then_inc(ws_turned, 1)
                elif kind == "g_turn":
                    g = arg[0]
                    bank = 4
                    pe.wait_ge(gelu_done, g + 1)
                    pe.wait_ge(masked, sum(1 for u in ITEM_UNIT if u <= IN_ORDER.index(f"g{g}") + 1))
                    for b in range(NB):
                        turn(ps[:, bank, b * P:(b + 1) * P], g_t[:, b * P:(b + 1) * P])
                    pe.transpose(ps[0:TS, bank + 1, 0:P], g_t[:, TP:T], ident[:]).then_inc(g_turned, 1)
                elif kind == "kv_turn":
                    pe.wait_ge(z_done, 2)
                    pe.wait_ge(ws_taken, 1)
                    for b in range(NB):
                        turn(ps[:, 6, b * P:(b + 1) * P], v_t[:, b * P:(b + 1) * P])
                    pe.transpose(ps[0:TS, 7, 0:P], v_t[:, TP:T], ident[:])
                    turn(ps[:, 7, P:2 * P], k_t[:, TP - P:TP])
                    pe.transpose(ps[0:TS, 7, 2 * P:3 * P], k_t[:, TP:T], ident[:]).then_inc(kv_turned, 1)
                elif kind == "scores":
                    i = arg[0]
                    j, bp = i // 2, i % 2
                    pe.wait_ge(z_done, IN_ORDER.index(f"q{j}") + 1)
                    if i == 0:
                        pe.wait_ge(z_scaled, 3)
                    turned = sum(1 for u, name in enumerate(IN_ORDER) if name[0] == "g" and u + 1 < ITEM_UNIT[i])
                    if turned:
                        pe.wait_ge(g_taken, turned)
                    if i:
                        pe.wait_ge(masked, i)
                    if i == 7:
                        pe.wait_ge(spatial_taken, 1)
                        pe.wait_ge(s_max, 1)
                    for c in range(NKV):
                        part = slice(c * HD, (c + 1) * HD)
                        for r in range(2):
                            b = 2 * bp + r
                            k0 = max(b - 1, 0) * W
                            ins = pe.matmul(ps[:, 4 + c, r * 2 * W:(r + 1) * 2 * W], q_t[part, j, b * P:(b + 1) * P],
                                            k_t[part, k0:k0 + 2 * W], start=True, stop=True)
                    ins.then_inc(scored, 1)
                elif kind == "p_turn":
                    i, r = arg
                    pe.wait_ge(exp_done, 5 * (i + 1))
                    if 2 * i + r == 0:
                        pe.wait_ge(kv_taken, 4)
                    else:
                        pe.wait_ge(probs_taken, 2 * i + r)
                    for c in range(NKV):
                        for k in range(2):
                            ins = turn(ps[:, 6, (2 * c + k) * P:(2 * c + k + 1) * P],
                                       probs[:, i % 2, c, r, k * W:(k + 1) * W])
                    ins.then_inc(probs_turned, 1)
                elif kind == "values":
                    i = arg[0]
                    bp = i % 2
                    pe.wait_ge(probs_taken, 2 * i + 2)
                    if i:
                        pe.wait_ge(o_lo, i)
                    for r in range(2):
                        b = 2 * bp + r
                        ks = (0,) if b == 0 else (0, 1)
                        for c in range(NKV):
                            for k in ks:
                                ins = pe.matmul(ps[:, 7, r * P + c * HD:r * P + (c + 1) * HD], probs_t[:, r, c, k, :],
                                                v_rows[:, max(b - 1, 0) + k, c * HD:(c + 1) * HD],
                                                start=(k == 0), stop=(k == ks[-1]))
                    ins.then_inc(o_made, 1)
                elif kind == "o_turn":
                    i = arg[0]
                    pe.wait_ge(o_taken, i + 1)
                    for r in range(2):
                        ins = turn(ps[:, 7, (2 + r) * P:(3 + r) * P], o_rows[:, r].rearrange("p c d -> p (c d)"))
                    ins.then_inc(o_turned, 1)
                elif kind == "spatial":
                    g = arg[0]
                    pe.wait_ge(g_normed[0], NB - 1)
                    pe.wait_ge(g_normed[1], 2)
                    pe.wait_ge(ws_ready, 1)
                    pe.wait_ge(w00_ready, 1)
                    if g:
                        pe.wait_ge(spatial_taken, g)
                    if g == 0:
                        pe.wait_ge(s_taken, 1)
                    elif g == 1:
                        pe.wait_ge(s_p_taken, 2)
                    else:
                        pe.wait_ge(s_out, 1)
                    pe.wait_ge(masked, 7 if g == 0 else 8)
                    for b in range(NB):
                        pe.matmul(ps[:, 4, b * P:(b + 1) * P], g_rows[:, b, g * P:(g + 1) * P], ws_t[:, g, :],
                                  start=True, stop=True)
                    pe.matmul(ps[:, 5, 384:384 + TS], g_rows[0:TS, NB, g * P:(g + 1) * P], w00_diag[:, g, :],
                              start=True, stop=True).then_inc(spatial_made, 1)
                elif kind == "s_scores":
                    pe.wait_ge(s_built, 1)
                    pe.wait_ge(masked, 7)
                    for b in range(TS):
                        pe.matmul(ps[:, 5, b * NQ:(b + 1) * NQ], cache_k_t[:, b, :], q_diag[:, b, :],
                                  start=True, stop=True)
                    pe.matmul(ps[0:64, 5, 64:65], qk_new[:].rearrange("p s h -> p (s h)"), ones[:, 0:1],
                              start=True, stop=True).then_inc(s_scored, 1)
                elif kind == "s_softmax":
                    pe.wait_ge(s_taken, 1)
                    pe.wait_ge(spatial_taken, 1)
                    pe.transpose(ps[0:64, 5, 128:256], s_keys[:], ident[:]).then_inc(s_turned, 1)
                elif kind == "s_probs":
                    pe.wait_ge(s_normed, 1)
                    pe.wait_ge(masked, 8)
                    pe.transpose(ps[:, 5, 0:64], s_p[:, 0:W], ident[0:64, 0:64])
                    pe.matmul(ps[:, 5, 64:128], ones[0:64, :], s_new[:], start=True, stop=True).then_inc(s_p_turned, 1)
                elif kind == "s_values":
                    pe.wait_ge(s_p_taken, 2)
                    pe.wait_ge(spatial_taken, 2)
                    for b in range(TS):
                        ins = pe.matmul(ps[:, 5, 256 + b * NQ:256 + (b + 1) * NQ], cache_v[:, b, :],
                                        s_pt[:, b * NQ:(b + 1) * NQ], start=True, stop=True)
                    ins.then_inc(s_valued, 1)

            for m in range(1, KD):
                n = OUT + m
                pe.wait_ge(w_lo_ready, n + 1)
                if m == 1:
                    pe.wait_ge(spatial_taken, GG)
                elif m == 2:
                    pe.wait_ge(z_scaled, 14)
                else:
                    pe.wait_ge(x_ready, 8 + m - 2)
                for k in range(KD):
                    ins = k_step(n, k, (mix_hi, mix_lo), k, (m + 1) % 3, k == 0, k == KD - 1)
                ins.then_inc(unit_done, 1)

            pe.wait_ge(x_ready, 8 + 6)
            unit(UP2, xg, 0, ready=(xg_lo_ready, 16))
            pe.wait_ge(x_ready, 8 + 7)
            unit(UP2 + 1, xg, 1, between=[(2, lambda: stat_sum(2))])
            stat_out(2)
            pe.wait_ge(x_ready, 8 + 8)
            ffn(UP2, DOWN2, KF, h2, 2, xg)

            pe.wait_ge(x_ready, 16 + 7)
            unit(LAST, xg, 0, ready=(xg_lo_ready, 24))
            pe.wait_ge(pple_lo, 1)
            for i in range(2):
                n = LAST + 1 + i
                pe.wait_ge(w_lo_ready, n + 1)
                for q in range(4):
                    m = 4 * i + q
                    if m >= 2:
                        pe.wait_ge(pp_ready, m - 1)
                    for k in range(KP):
                        ins = k_step(n, 4 * k + q, (p_hi, p_lo), k, 1 + m % 2, k == 0, k == KP - 1)
                    ins.then_inc(unit_done if q == 3 else pp_made, 1)
            stat_sum(3)
            for m in range(1, KD):
                if m < 3:
                    pe.wait_ge(pp_ready, KD - 2 + m)
                else:
                    pe.wait_ge(z_ready, m - 2)
                unit(LAST + 2 + m, xg, m % 3, between=[(6, lambda: stat_out(3))] if m == 1 else ())

            def turn_back(b, ks):
                n = P if b < NB else TS
                for k in ks:
                    ins = pe.transpose(ps[0:n, 2 * Y_PAIR[b] + k // 4, (k % 4) * P:(k % 4 + 1) * P],
                                       xf[:, k, b * P:b * P + n], ident[:])
                return ins

            pe.wait_ge(rstd_ready, 8)
            pe.wait_ge(xf_ready, KD - 1)
            pe.wait_ge(z_ready, KD - 1)
            for b in range(3):
                turn_back(b, range(KD - 1))
            pe.wait_ge(xf_ready, KD)
            for b in range(3):
                turn_back(b, (KD - 1,)).then_inc(y_turned, 1)
            stat_sum(4)
            pe.wait_ge(rs_ready, 1)
            turn_back(3, range(KD)).then_inc(y_turned, 1)
            pe.wait_ge(y_ready[0], 1)
            turn_back(4, range(KD)).then_inc(y_turned, 1)


_INS = ["x_prompt", "x_sample", "cache_k_win", "cache_v_win", "p_prompt", "p_sample", "g_ffn1", "w1_ffn1", "w3_ffn1",
        "w2_ffn1", "g_mix", "w_in", "b_in", "attn_sinks", "gm_ln_g", "gm_ln_b", "gm_w_s", "gm_b_s", "w_out", "b_out",
        "g_ffn2", "w1_ffn2", "w3_ffn2", "w2_ffn2", "g_ple", "w_ple_gate", "w_ple_proj", "g_final"]
_OUTS = [("y_prompt", (1, TP, D)), ("y_sample", (TS, 1, D)), ("k_win_prompt", (1, 1, W, NKV, HD)),
         ("v_win_prompt", (1, 1, W, NKV, HD)), ("k_win_sample", (1, TS, W, NKV, HD)),
         ("v_win_sample", (1, TS, W, NKV, HD)), ("gm_v_prompt", (1, 1, W, GM)), ("gm_v_sample", (1, TS, 1, GM))]


def kernel(**inputs):
    import numpy as _np
    import concourse.bacc as _bacc
    from concourse import mybir as _mybir
    from concourse.bass_utils import run_bass_kernel_spmd as _run

    nc = _bacc.Bacc("TRN2", target_bir_lowering=False, num_devices=1)
    arrays, ins, outs = {}, {}, {}
    for name in _INS:
        arr = _np.ascontiguousarray(inputs[name])
        arrays[f"in_{name}_dram"] = arr
        ins[name] = nc.dram_tensor(f"in_{name}_dram", arr.shape, _mybir.dt.from_np(arr.dtype),
                                   kind="ExternalInput").ap()
    for name, shape in _OUTS:
        outs[name] = nc.dram_tensor(f"out_{name}_dram", shape, _mybir.dt.float32, kind="ExternalOutput").ap()
    hybrid_decoder_layer(nc, ins, outs)
    r = _run(nc, [arrays], core_ids=[0])
    return tuple(r.results[0][f"out_{name}_dram"] for name, _ in _OUTS)
```

```python
from contextlib import ExitStack

import concourse.bass as bass
from concourse import mybir

F32 = mybir.dt.float32
F32R = mybir.dt.float32r
I32 = mybir.dt.int32
ALU = mybir.AluOpType
ACT = mybir.ActivationFunctionType
AX_X = mybir.AxisListType.X

P = 128
D, FF, PLE = 1024, 2816, 256
TP, TS = 512, 8
T = TP + TS
HALF = T // 2
NB = TP // P
KD, KF, KP = D // P, FF // P, PLE // P
HD, NQ, NKV, GQ = 64, 8, 2, 4
GM, GG = 512, 4
W = 128
RMS_EPS, LN_EPS = 1e-6, 1e-5
SCALE = HD ** -0.5
NEG = -1.0e30
GELU_C = 0.7978845608028654
GELU_K = 0.044715 ** 0.5
RSQRT_SEED = 1597463007.0

RING = 3
UP1 = 0
DOWN1 = UP1 + 2 * KF
IN = DOWN1 + 3 * KD
OUT = IN + 14
UP2 = OUT + KD
DOWN2 = UP2 + 2 * KF
LAST = DOWN2 + 3 * KD
END = LAST + KD + 2
DOWN_K = (8, 8, 6)

IN_ORDER = ("k", "v", "g0", "q0", "g1", "q1", "g2", "q2", "g3", "q3", "u0", "u1", "u2", "u3")
IN_PAIR = (0, 1, 2, 0, 1, 0, 1, 0, 1, 0, 1, 0, 1, 0)
STAT_BANK = (None, 7, 7, 7, 0)
Y_PAIR = (3, 2, 0, 1, 1)
ITEM_UNIT = (4, 5, 6, 7, 8, 9, 10, 11)
C_BOUT, C_Q, C_K, C_V, C_U, C_G, C_FIN, C_LNG, C_LNB, N_COLS = 32, 40, 44, 45, 46, 50, 54, 62, 66, 70


def mixer_steps():
    extra = {
        (1, 2): [("stat_sum",)],
        (1, 4): [("cache_turn",)],
        (2, 0): [("stat_spread",), ("evac", 0), ("evac", 1)],
        (3, 1): [("ws_turn",)],
        (3, 5): [("kv_turn",)],
        (8, 7): [("ws_sum",)],
        (10, 1): [("norm_stats", 3), ("norm_stats", 4)],
        (10, 2): [("s_build",)],
        (10, 5): [("norm_stats", 0)],
        (10, 7): [("s_scores",)],
        (11, 0): [("s_softmax",)],
        (11, 1): [("norm_stats", 1)],
        (11, 5): [("norm_stats", 2)],
        (11, 7): [("s_probs",)],
        (12, 0): [("norm_rsqrt",)],
        (12, 1): [("norm", 3), ("norm", 4), ("norm", 0), ("norm", 1), ("norm", 2)],
        (12, 4): [("s_values",)],
        (12, 6): [("spatial", 0), ("gm", 0)],
        (13, 0): [("gm_lo", 0)],
        (13, 1): [("spatial", 1), ("gm", 1)],
        (13, 4): [("gm_lo", 1), ("spatial", 2)],
        (13, 7): [("gm", 2)],
    }

    def put(u, k, *stages):
        extra[(u, k)] = list(stages) + extra.get((u, k), [])

    for u, name in enumerate(IN_ORDER[:-1]):
        if name[0] == "g":
            put(u + 2, 0, ("g_turn", int(name[1])))
        if name[0] in "ug":
            put(u + 1, 6, ("gelu_end", u))
            put(u + 1, 3, ("gelu_mid", u))
    for i, u in enumerate(ITEM_UNIT):
        put(u, 3, ("scores", i))
        put(u, 4, ("soft", i))
        put(u + 1, 1, ("p_turn", i, 0))
        put(u + 1, 3, ("p_turn", i, 1))
        put(u + 1, 5, ("values", i))
        put(u + 2, 1, ("o_turn", i))
    steps = []
    for u in range(14):
        for k in range(KD):
            steps += extra.pop((u, k), [])
            steps.append(("gemm", u, k))
        if u > 1:
            steps.append(("evac", u))
    assert not extra, extra
    steps += [("out", 0, 0), ("gm_lo", 2), ("spatial", 3), ("out", 0, 1), ("gelu_mid", 13)]
    steps += [("out", 0, k) for k in range(2, 7)] + [("out", 1, k) for k in range(7)]
    return steps + [("gelu_end", 13), ("gm", 3), ("gm_lo", 3), ("out", 0, 7), ("out", 1, 7)]


def hybrid_decoder_layer(nc, a, o):
    steps = mixer_steps()
    with ExitStack() as ctx:
        def sb(name, shape, dt=F32, scope=ctx):
            return scope.enter_context(nc.sbuf_tensor(name, shape, dt))

        def sem(name):
            return ctx.enter_context(nc.semaphore(name))

        x = sb("x", [P, KD, T])
        xg_hi = sb("xg_hi", [P, KD, T], F32R)
        xg_lo = sb("xg_lo", [P, KD, T], F32R)
        w_raw = sb("w_raw", [P, RING, KD * P])
        w_hi = sb("w_hi", [P, RING, KD * P], F32R)
        w_lo = sb("w_lo", [P, RING, KD * P], F32R)
        ta = sb("ta", [P, T])
        tb = sb("tb", [P, T])
        tq = sb("tq", [P, T])
        rstd = sb("rstd", [P, T])
        sq = sb("sq", [P, T])
        ssq = sb("ssq", [P, T])
        diag = sb("diag", [P, T])
        ident = sb("ident", [P, P])
        ones = sb("ones", [P, P])
        p_t = sb("p_t", [P, KP, T])
        cols = sb("cols", [P, N_COLS])
        cols_g = sb("cols_g", [P, N_COLS])
        var = sb("var", [P, 8])
        rs = sb("rs", [P, 8])
        rs_i = sb("rs_i", [P, 8], I32)
        rs_t = sb("rs_t", [P, 8])

        with ExitStack() as s:
            x_rows = sb("x_rows", [P, NB, D], scope=s)
            sq_rows = sb("sq_rows", [P, 2, D], scope=s)
            xs_rows = sb("xs_rows", [P, D], scope=s)
            rows = sb("rows", [N_COLS, P], scope=s)
        with ExitStack() as s:
            h1 = sb("h1_hi", [P, KF, T], F32R, s), sb("h1_lo", [P, KF, T], F32R, s)
            p_rows = sb("p_rows", [P, NB, PLE], scope=s)
            ps_rows = sb("ps_rows", [P, PLE], scope=s)
        with ExitStack() as s:
            mix_hi = sb("mix_hi", [P, 8, T], F32R, s)
            mix_lo = sb("mix_lo", [P, 8, T], F32R, s)
            q_t = sb("q_t", [P, GQ, T], scope=s)
            k_t = sb("k_t", [P, T], scope=s)
            v_t = sb("v_t", [P, T], scope=s)
            g_rows = sb("g_rows", [P, NB + 1, GM], scope=s)
            v_rows = sb("v_rows", [P, NB + 1, P], scope=s)
            k_rows = sb("k_rows", [P, 2, P], scope=s)
            ws_t = sb("ws_t", [P, GG, P], scope=s)
            bs_all = sb("bs_all", [P, GG, P], scope=s)
            lng = sb("lng", [P, GM], scope=s)
            lnb = sb("lnb", [P, GM], scope=s)
            probs = sb("probs", [P, 2, NKV, 2, 2 * W], scope=s)
            probs_t = sb("probs_t", [P, 2, NKV, 2, P], scope=s)
            o_rows = sb("o_rows", [P, 2, NKV, HD], scope=s)
            mask = sb("mask", [P, 2, 2 * W], scope=s)
            cache_k_t = sb("cache_k_t", [P, TS, W], scope=s)
            cache_v = sb("cache_v", [P, TS, W], scope=s)
            sink = sb("sink", [P, NQ], scope=s)
            st = sb("st", [P, 32], scope=s)
            bn = sb("bn", [P, NB + 1, 6], scope=s)
            mv = sb("mv", [P, NB + 1, 2], scope=s)
            w00 = sb("w00", [TS, GG], scope=s)
            w00_diag = sb("w00_diag", [TS, GG, TS], scope=s)
            s_sink = sb("s_sink", [64, 1], scope=s)
            s_st = sb("s_st", [64, 8], scope=s)
            q_diag = sb("q_diag", [P, TS, NQ], scope=s)
            qk_new = sb("qk_new", [P, TS, NQ], scope=s)
            s_keys = sb("s_keys", [P, 64], scope=s)
            s_p = sb("s_p", [64, W + 1], scope=s)
            s_new = sb("s_new", [64, 64], scope=s)
            s_pt = sb("s_pt", [P, 64], scope=s)
            s_pv = sb("s_pv", [P, TS, NQ], scope=s)
            s_o = sb("s_o", [P, TS, NQ], scope=s)
            with ExitStack() as early:
                cache_k = sb("cache_k", [P, TS, W], scope=early)
                ws_rows = sb("ws_rows", [P, GG, P], scope=early)
                g_t = sb("g_t", [P, T], scope=early)
            gu = sb("gu", [P, 2, T], scope=s)
            sp = sb("sp", [P, T], scope=s)
            gv_rows = sb("gv_rows", [P, 2, GM], scope=s)
        with ExitStack() as s:
            h2 = sb("h2_hi", [P, KF, T], F32R, s), sb("h2_lo", [P, KF, T], F32R, s)
        with ExitStack() as s:
            p_hi = sb("p_hi", [P, KP, T], F32R, s)
            p_lo = sb("p_lo", [P, KP, T], F32R, s)
            pp = sb("pp", [P, KD, T], scope=s)
            xf = sb("xf", [P, KD, T], scope=s)
            y = sb("y", [P, NB + 1, D], scope=s)
            xf_rows = sb("xf_rows", [P, D], scope=s)

        ps = ctx.enter_context(nc.psum_tensor("ps", [P, 8, 512], F32))

        raw_in = [sem(f"raw_in{i}") for i in range(RING)]
        w_hi_ready, w_lo_ready = sem("w_hi_ready"), sem("w_lo_ready")
        unit_done = sem("unit_done")
        x_in = [sem(f"x_in{i}") for i in range(NB + 1)]
        p_in, ps_in = sem("p_in"), sem("ps_in")
        gain_in, rows_in = sem("gain_in"), sem("rows_in")
        consts_ready = sem("consts_ready")
        cols_turned, cols_ready = sem("cols_turned"), sem("cols_ready")
        x_turned = sem("x_turned")
        x_ready = sem("x_ready")
        xg_hi_ready, xg_lo_ready = sem("xg_hi_ready"), sem("xg_lo_ready")
        p_turned = sem("p_turned")
        sq_made = sem("sq_made")
        sq_added = sem("sq_added")
        stat_summed, diag_ready = sem("stat_summed"), sem("diag_ready")
        stat_spread, rstd_ready = sem("stat_spread"), sem("rstd_ready")
        dve_step = sem("dve_step")
        a_ready, tanh_ready = sem("a_ready"), sem("tanh_ready")
        ab_ready, ab_scaled = sem("ab_ready"), sem("ab_scaled")
        h_ready, h_hi_ready, h_lo_ready = sem("h_ready"), sem("h_hi_ready"), sem("h_lo_ready")
        mix_in = sem("mix_in")
        cache_in, ws_in = sem("cache_in"), sem("ws_in")
        mask_ready = sem("mask_ready")
        z_scaled, z_done = sem("z_scaled"), sem("z_done")
        gelu_sq, gelu_arg, gelu_tanh = sem("gelu_sq"), sem("gelu_arg"), sem("gelu_tanh")
        gelu_done = sem("gelu_done")
        cache_turned, cache_taken = sem("cache_turned"), sem("cache_taken")
        ws_turned, ws_taken, ws_ready = sem("ws_turned"), sem("ws_taken"), sem("ws_ready")
        g_turned, g_taken = sem("g_turned"), sem("g_taken")
        kv_turned, kv_taken = sem("kv_turned"), sem("kv_taken")
        ws_summed, bs_ready = sem("ws_summed"), sem("bs_ready")
        g_centred, g_gained, g_normed = sem("g_centred"), sem("g_gained"), sem("g_normed")
        scored, masked, max_ready = sem("scored"), sem("masked"), sem("max_ready")
        exp_done = sem("exp_done")
        probs_turned = sem("probs_turned")
        probs_taken = sem("probs_taken")
        o_made, o_taken = sem("o_made"), sem("o_taken")
        o_turned, o_hi, o_lo = sem("o_turned"), sem("o_hi"), sem("o_lo")
        spatial_made, spatial_taken = sem("spatial_made"), sem("spatial_taken")
        gm_ready, gm_hi, gm_lo = sem("gm_ready"), sem("gm_hi"), sem("gm_lo")
        w00_ready = sem("w00_ready")
        s_built, s_scored, s_taken = sem("s_built"), sem("s_scored"), sem("s_taken")
        s_turned, s_max, s_exp, s_normed = sem("s_turned"), sem("s_max"), sem("s_exp"), sem("s_normed")
        s_diag_clear = sem("s_diag_clear")
        s_p_turned, s_p_taken = sem("s_p_turned"), sem("s_p_taken")
        s_valued, s_out, s_hi, s_lo = sem("s_valued"), sem("s_out"), sem("s_hi"), sem("s_lo")
        pple_hi, pple_lo, pp_made, pp_ready = sem("pple_hi"), sem("pple_lo"), sem("pp_made"), sem("pp_ready")
        z_ready, gate_ready, gated = sem("z_ready"), sem("gate_ready"), sem("gated")
        row_sums, rs_ready = sem("row_sums"), sem("rs_ready")
        sums_taken, ys_taken = sem("sums_taken"), sem("ys_taken")
        x_odd, x_even = sem("x_odd"), sem("x_even")
        xf_ready = sem("xf_ready")
        y_turned = sem("y_turned")
        y_ready = [sem(f"y_ready{b}") for b in range(NB + 1)]
        out_done = sem("out_done")

        def pair(i, width=HALF):
            return ps[:, 2 * i:2 * i + 2, 0:width]

        def keys(bp, r):
            return 2 * W if bp or r else W

        def halves(ap):
            return ap.rearrange("p (h t) -> p h t", h=2)

        def at(n, step, it):
            return n if it is None else it * step + n

        def tile_of(t, m, step, it):
            if it is None:
                return t[:, m, :]
            return t[:, bass.ds(it * step + m, 1), :].rearrange("p a t -> p (a t)")

        def col(c, step=0, it=None):
            return cols[:, c:c + 1] if it is None else cols[:, bass.ds(it * step + c, 1)]

        w_dram = {n: a[n][0].rearrange("(k p) c -> p k c", p=P)
                  for n in ("w1_ffn1", "w3_ffn1", "w2_ffn1", "w_in", "w_out", "w1_ffn2", "w3_ffn2",
                            "w2_ffn2", "w_ple_gate", "w_ple_proj")}
        mix_loads = 6 + TS

        block = ctx.enter_context(nc.Block())

        @block.sync
        def _(sp_):
            def load(n, step, it, src, width=KD * P):
                if n >= RING:
                    sp_.wait_ge(w_lo_ready, at(n - RING + 1, step, it))
                dst = w_raw[:, n % RING, 0:width]
                dst = dst.rearrange("p (k c) -> p k c", k=src.shape[1])
                sp_.dma_start(dst, src).then_inc(raw_in[n % RING], 16)

            def up_step(base, ws, f, it):
                for i, w in enumerate(ws):
                    c = bass.ds(at(f * P, 3 * P, it), P) if it is not None else slice(f * P, f * P + P)
                    load(base + 2 * f + i, 6, it, w_dram[w][:, :, c])

            def down_step(base, w, m, it):
                c = bass.ds(at(m * P, 2 * P, it), P)
                for i, kn in enumerate(DOWN_K):
                    load(base + 3 * m + i, 6, it, w_dram[w][:, 8 * i:8 * i + kn, c], kn * P)

            def ffn(up, down, w1, w3, w2, first=0):
                for f in range(1 if first else 0, 4):
                    up_step(up, (w1, w3), f, None)
                with sp_.Fori(0, (KF - 4) // 3) as it:
                    for r in range(3):
                        up_step(up, (w1, w3), 4 + r, it)
                if first:
                    sp_.wait_ge(x_turned, KD)
                    sp_.dma_start(p_rows[:], a["p_prompt"][0, 0].rearrange("(b p) c -> p b c", p=P)).then_inc(p_in, 16)
                    sp_.dma_start(ps_rows[0:TS, :], a["p_sample"][0].rearrange("b t c -> (b t) c")).then_inc(ps_in, 16)
                with sp_.Fori(0, KD // 2) as it:
                    for r in range(2):
                        down_step(down, w2, r, it)

            for b in range(NB):
                sp_.dma_start(x_rows[:, b, :], a["x_prompt"][0, b * P:(b + 1) * P, :]).then_inc(x_in[b], 16)
            up_step(UP1, ("w1_ffn1", "w3_ffn1"), 0, None)
            ffn(UP1, DOWN1, "w1_ffn1", "w3_ffn1", "w2_ffn1", first=1)

            offset = {"q": 0, "k": 512, "v": 640, "u": 768, "g": 1280}
            for u, name in enumerate(IN_ORDER):
                c0 = offset[name[0]] + (int(name[1]) * P if name[0] in "ug" else 0)
                if name[0] == "q":
                    n, j = IN + u, int(name[1])
                    sp_.wait_ge(w_lo_ready, n - RING + 1)
                    for c in range(NKV):
                        src = w_dram["w_in"][:, :, c * 256 + j * HD:c * 256 + (j + 1) * HD]
                        dst = w_raw[:, n % RING, :].rearrange("p (k c d) -> p k c d", k=KD, c=NKV)[:, :, c, :]
                        sp_.dma_start(dst, src).then_inc(raw_in[n % RING], 16)
                else:
                    load(IN + u, 0, None, w_dram["w_in"][:, :, c0:c0 + P])
            wo = a["w_out"][0]
            for m in range(KD):
                n = OUT + m
                sp_.wait_ge(w_lo_ready, n - RING + 1)
                dst = w_raw[:, n % RING, :].rearrange("p (k c) -> p k c", k=KD)
                for c in range(NKV):
                    sp_.dma_start(dst[c * HD:(c + 1) * HD, 0:4, :],
                                  wo[c * 256:(c + 1) * 256, m * P:(m + 1) * P].rearrange("(j d) c -> d j c", d=HD)
                                  ).then_inc(raw_in[n % RING], 16)
                sp_.dma_start(dst[:, 4:8, :], wo[512:1024, m * P:(m + 1) * P].rearrange("(j d) c -> d j c", d=P)
                              ).then_inc(raw_in[n % RING], 16)

            ffn(UP2, DOWN2, "w1_ffn2", "w3_ffn2", "w2_ffn2")

            load(LAST, 0, None, w_dram["w_ple_gate"][:, :, 0:P])
            for i in range(2):
                load(LAST + 1 + i, 0, None, w_dram["w_ple_proj"][:, :, 512 * i:512 * (i + 1)])
            for m in range(1, KD):
                load(LAST + 2 + m, 0, None, w_dram["w_ple_gate"][:, :, m * P:(m + 1) * P])

            for blocks in ((1, 0), (3, 2)):
                for h in range(2):
                    for b in blocks:
                        sp_.wait_ge(y_ready[b], h + 1)
                        sp_.dma_start(o["y_prompt"][0, b * P:(b + 1) * P, h * 512:(h + 1) * 512],
                                      y[:, b, h * 512:(h + 1) * 512]).then_inc(out_done, 16)
            sp_.wait_ge(y_ready[NB], 1)
            sp_.dma_start(o["y_sample"].rearrange("b t d -> (b t) d"), y[0:TS, NB, :]).then_inc(out_done, 16)
            sp_.wait_ge(out_done, 16 * 17)

        def parts(n):
            if IN <= n < OUT and IN_ORDER[n - IN][0] == "q":
                return NKV
            return 3 if OUT <= n < UP2 else 1

        def arrived(n):
            return 16 * sum(parts(m) for m in range(n % RING, n + 1, RING))

        @block.scalar
        def _(act):
            def split_hi(n, step=0, it=None):
                if n >= END:
                    return
                act.wait_ge(raw_in[n % RING], at(arrived(n), 16 * step // RING, it))
                if n >= RING:
                    act.wait_ge(unit_done, at(n - RING + 1, step, it))
                nc.scalar.activation(w_hi[:, n % RING, :], w_raw[:, n % RING, :], ACT.Copy).then_inc(w_hi_ready, 1)

            def x_hi(stat, m, step=0, it=None):
                act.wait_ge(sq_added, at(9 * stat + m - 8, step, it))
                act.wait_ge(x_ready, at(8 * stat + m - 7, step, it))
                nc.scalar.activation(tile_of(xg_hi, m, step, it), tile_of(x, m, step, it), ACT.Copy,
                                     scale=col(8 * stat + m, step, it)).then_inc(xg_hi_ready, 1)
                nc.scalar.activation(sq[:], tile_of(x, m, step, it), ACT.Square).then_inc(sq_made, 1)

            def spread(stat):
                act.wait_ge(stat_spread, stat + 1)
                nc.scalar.activation(rstd[:, 0:TP], ps[:, 6, :], ACT.Copy).then_inc(rstd_ready, 1)
                nc.scalar.activation(rstd[:, TP:T], ps[:, 7, 8:8 + TS], ACT.Copy).then_inc(rstd_ready, 1)

            def up_step(base, f0, h, f, it):
                if f:
                    split_hi(base + 2 * f + 3, 6, it)
                if f0 + f:
                    act.wait_ge(h_ready, at(f0 + f, 3, it))
                act.wait_ge(a_ready, at(f0 + f + 1, 3, it))
                nc.scalar.activation(tb[:], ta[:], ACT.Tanh, scale=0.5).then_inc(tanh_ready, 1)
                split_hi(base + 2 * f + 4, 6, it)
                act.wait_ge(h_ready, at(f0 + f + 1, 3, it))
                nc.scalar.activation(tile_of(h[0], f, 3, it), tq[:], ACT.Copy).then_inc(h_hi_ready, 1)

            def ffn(up, down, f0, h, stat):
                split_hi(up + 3)
                spread(stat)
                up_step(up, f0, h, 0, None)
                with act.Fori(0, (KF - 1) // 3) as it:
                    for r in range(3):
                        up_step(up, f0, h, 1 + r, it)
                with act.Fori(0, KD // 2) as it:
                    for m in range(2):
                        for c in range(3):
                            split_hi(down + 3 * m + 3 + c, 6, it)
                        x_hi(stat + 1, m, 2, it)

            act.dma_start(rows[0:KD, :], a["g_ffn1"][0].rearrange("(k p) -> k p", p=P)).then_inc(gain_in, 16)
            act.dma_start(xs_rows[0:TS, :], a["x_sample"].rearrange("b t d -> (b t) d")).then_inc(x_in[NB], 16)
            r0 = KD
            for name in ("g_mix", "g_ffn2", "g_ple", "b_out"):
                act.dma_start(rows[r0:r0 + 8, :], a[name][0].rearrange("(k p) -> k p", p=P)).then_inc(rows_in, 16)
                r0 += 8
            b_in = a["b_in"][0]
            for c in range(NKV):
                act.dma_start(rows[C_Q:C_Q + GQ, c * HD:(c + 1) * HD],
                              b_in[c * GQ * HD:(c + 1) * GQ * HD].rearrange("(j d) -> j d", d=HD)).then_inc(rows_in, 16)
            act.dma_start(rows[C_K:C_FIN, :], b_in[512:1792].rearrange("(k p) -> k p", p=P)).then_inc(rows_in, 16)
            act.dma_start(rows[C_FIN:C_LNG, :], a["g_final"].rearrange("(k p) -> k p", p=P)).then_inc(rows_in, 16)
            for r0, name in ((C_LNG, "gm_ln_g"), (C_LNB, "gm_ln_b")):
                act.dma_start(rows[r0:r0 + GG, :], a[name][0].rearrange("(k p) -> k p", p=P)).then_inc(rows_in, 16)

            act.wait_ge(consts_ready, 2)
            nc.scalar.activation(tb[:, 0:P], ones[:], ACT.Copy)
            act.wait_ge(cols_ready, 1)
            for m in range(KD):
                if m % 2:
                    act.wait_ge(x_turned, m + 1)
                    nc.scalar.activation(x[:, m, 0:TP], ps[:, 2 * (1 + m % 3), :], ACT.Copy)
                    nc.scalar.activation(x[:, m, TP:T], ps[:, 2 * (1 + m % 3) + 1, 0:TS], ACT.Copy).then_inc(x_odd, 1)
                    act.wait_ge(x_odd, m // 2 + 1)
                else:
                    act.wait_ge(x_even, m // 2 + 1)
                nc.scalar.activation(xg_hi[:, m, :], x[:, m, :], ACT.Copy, scale=col(m)).then_inc(xg_hi_ready, 1)
                if m == 1:
                    split_hi(0)
                elif m == 5:
                    split_hi(1)
            nc.scalar.activation(sq_rows[:, 0, :], x_rows[:, NB - 1, :], ACT.Square,
                                 accum_out=rs_t[:, NB - 1:NB]).then_inc(row_sums, 1)
            nc.scalar.activation(sq_rows[0:TS, 1, :], xs_rows[0:TS, :], ACT.Square,
                                 accum_out=rs_t[0:TS, NB:NB + 1]).then_inc(row_sums, 1)
            split_hi(2)
            ffn(UP1, DOWN1, 0, h1, 0)

            act.wait_ge(unit_done, IN)
            act.dma_start(cache_k[:], a["cache_k_win"][0].rearrange("b w h d -> w b (h d)")).then_inc(cache_in, 16)
            act.dma_start(ws_rows[:], a["gm_w_s"][0].rearrange("g t s -> t g s")).then_inc(ws_in, 16)
            for dst, src in (
                (sink[:], a["attn_sinks"][0].partition_broadcast(P)),
                (cache_v[:], a["cache_v_win"][0].rearrange("b w h d -> w b (h d)")),
                (bs_all[:], a["gm_b_s"][0].partition_broadcast(P)),
                (lng[:], a["gm_ln_g"][0].partition_broadcast(P)),
                (lnb[:], a["gm_ln_b"][0].partition_broadcast(P)),
            ):
                act.dma_start(dst, src).then_inc(mix_in, 16)
            act.dma_start(w00[:], a["gm_w_s"][0, :, 0, 0].partition_broadcast(TS),
                          allow_slow_non_contiguous=True).then_inc(mix_in, 16)
            for r in range(TS):
                act.dma_start(s_sink[r * NQ:(r + 1) * NQ, :],
                              a["attn_sinks"][0].rearrange("(h o) -> h o", o=1)).then_inc(mix_in, 16)
            for dst, src in ((o["k_win_sample"], a["cache_k_win"]), (o["v_win_sample"], a["cache_v_win"])):
                act.dma_start(dst[0, :, 0:W - 1].rearrange("b w h d -> b (w h d)"),
                              src[0, :, 1:W].rearrange("b w h d -> b (w h d)")).then_inc(out_done, 16)

            n_gelu = 0
            for kind, *arg in steps:
                if kind == "gemm" and arg[1] == 4 and arg[0] > 0:
                    split_hi(IN + arg[0] + 2)
                elif kind == "out" and arg == [0, 4]:
                    split_hi(OUT + 2)
                elif kind == "stat_spread":
                    spread(1)
                elif kind == "cache_turn":
                    act.wait_ge(cache_turned, 1)
                    nc.scalar.activation(cache_k_t[:], ps[:, 4:6, :].rearrange("p a (b w) -> p (a b) w", w=W),
                                         ACT.Copy).then_inc(cache_taken, 1)
                elif kind == "ws_turn":
                    act.wait_ge(ws_turned, 1)
                    nc.scalar.activation(ws_t[:], ps[:, 6, :].rearrange("p (g s) -> p g s", g=GG),
                                         ACT.Copy).then_inc(ws_taken, 1)
                elif kind == "evac":
                    u, name = arg[0], IN_ORDER[arg[0]]
                    j = int(name[1:] or 0)
                    c = {"q": C_Q, "k": C_K, "v": C_V, "u": C_U, "g": C_G}[name[0]] + j
                    act.wait_ge(z_scaled, u + 1)
                    if name[0] in "ug":
                        if n_gelu:
                            act.wait_ge(gelu_done, n_gelu)
                        n_gelu += 1
                        nc.scalar.activation(tb[:], ta[:], ACT.Square, bias=cols_g[:, c:c + 1],
                                             scale=GELU_K).then_inc(gelu_sq, 1)
                        nc.scalar.activation(tq[:], ta[:], ACT.Identity, bias=col(c)).then_inc(z_done, 1)
                    else:
                        dst = {"q": q_t[:, j, :], "k": k_t[:], "v": v_t[:]}[name[0]]
                        nc.scalar.activation(dst, ta[:], ACT.Identity, bias=col(c)).then_inc(z_done, 1)
                elif kind == "gelu_mid":
                    act.wait_ge(gelu_arg, n_gelu)
                    nc.scalar.activation(tb[:], tb[:], ACT.Tanh, scale=GELU_C).then_inc(gelu_tanh, 1)
                elif kind == "g_turn":
                    g = arg[0]
                    act.wait_ge(g_turned, g + 1)
                    nc.scalar.activation(g_rows[:, 0:NB, g * P:(g + 1) * P],
                                         ps[:, 4, :].rearrange("p (b c) -> p b c", c=P), ACT.Copy)
                    nc.scalar.activation(g_rows[0:TS, NB, g * P:(g + 1) * P], ps[0:TS, 5, 0:P],
                                         ACT.Copy).then_inc(g_taken, 1)
                elif kind == "kv_turn":
                    act.wait_ge(kv_turned, 1)
                    nc.scalar.activation(v_rows[:, 0:NB, :], ps[:, 6, :].rearrange("p (b c) -> p b c", c=P),
                                         ACT.Copy).then_inc(kv_taken, 1)
                    nc.scalar.activation(v_rows[0:TS, NB, :], ps[0:TS, 7, 0:P], ACT.Copy).then_inc(kv_taken, 1)
                    nc.scalar.activation(k_rows[:, 0, :], ps[:, 7, P:2 * P], ACT.Copy).then_inc(kv_taken, 1)
                    nc.scalar.activation(k_rows[0:TS, 1, :], ps[0:TS, 7, 2 * P:3 * P], ACT.Copy).then_inc(kv_taken, 1)
                    act.wait_ge(kv_taken, 4)
                    act.dma_start(o["v_win_prompt"][0, 0].rearrange("w h d -> w (h d)"), v_rows[:, NB - 1, :]
                                  ).then_inc(out_done, 16)
                    act.dma_start(o["k_win_prompt"][0, 0].rearrange("w h d -> w (h d)"), k_rows[:, 0, :]
                                  ).then_inc(out_done, 16)
                    act.dma_start(o["v_win_sample"][0, :, W - 1].rearrange("b h d -> b (h d)"), v_rows[0:TS, NB, :]
                                  ).then_inc(out_done, 16)
                    act.dma_start(o["k_win_sample"][0, :, W - 1].rearrange("b h d -> b (h d)"), k_rows[0:TS, 1, :]
                                  ).then_inc(out_done, 16)
                elif kind == "soft":
                    i = arg[0]
                    c0 = 16 * (i % 2)
                    act.wait_ge(max_ready, i + 1)
                    for c in range(4):
                        item = probs[:, i % 2, c // 2, c % 2, 0:keys(i % 2, c % 2)]
                        nc.scalar.activation(item, item, ACT.Exp, bias=st[:, c0 + c:c0 + c + 1],
                                             accum_out=st[:, c0 + 8 + c:c0 + 9 + c]).then_inc(exp_done, 1)
                    nc.scalar.activation(st[:, c0 + 4:c0 + 8], st[:, c0 + 4:c0 + 8], ACT.Exp).then_inc(exp_done, 1)
                elif kind == "p_turn":
                    i, b = arg
                    act.wait_ge(probs_turned, 2 * i + b + 1)
                    kn = keys(i % 2, b) // W
                    nc.scalar.activation(probs_t[:, b, :, 0:kn, :],
                                         ps[:, 6, :].rearrange("p (c k q) -> p c k q", c=NKV, k=2)[:, :, 0:kn, :],
                                         ACT.Copy).then_inc(probs_taken, 1)
                elif kind == "o_turn":
                    i = arg[0]
                    act.wait_ge(o_turned, i + 1)
                    nc.scalar.activation(mix_hi[:, i // 2, 256 * (i % 2):256 * (i % 2) + 256], ps[:, 7, 256:512],
                                         ACT.Copy).then_inc(o_hi, 1)
                elif kind == "spatial" and arg[0] >= 2:
                    b = arg[0] - 2
                    act.wait_ge(g_normed, b + 1)
                    if b == 0:
                        act.dma_start(o["gm_v_prompt"][0, 0], gv_rows[:, b, :]).then_inc(out_done, 16)
                    else:
                        act.dma_start(o["gm_v_sample"][0].rearrange("b t c -> (b t) c"), gv_rows[0:TS, b, :]
                                      ).then_inc(out_done, 16)
                elif kind == "gm":
                    g = arg[0]
                    act.wait_ge(gm_ready, g + 1)
                    nc.scalar.activation(mix_hi[:, 4 + g, :], sp[:], ACT.Copy, scale=0.5).then_inc(gm_hi, 1)
                elif kind == "s_softmax":
                    act.wait_ge(s_max, 1)
                    nc.scalar.activation(s_p[:], s_p[:], ACT.Exp, bias=s_st[:, 0:1],
                                         accum_out=s_st[:, 2:3]).then_inc(s_exp, 1)
                    nc.scalar.activation(s_st[:, 1:2], s_st[:, 1:2], ACT.Exp).then_inc(s_exp, 1)
                elif kind == "s_values":
                    act.wait_ge(s_out, 1)
                    for c in range(NKV):
                        part = slice(c * HD, (c + 1) * HD)
                        nc.scalar.activation(mix_hi[part, 0:4, TP:T],
                                             s_o[part, :, c * GQ:(c + 1) * GQ].rearrange("p s j -> p j s"),
                                             ACT.Copy).then_inc(s_hi, 1)

            for m in range(KD):
                split_hi(OUT + m + 3)
                x_hi(2, m)
            act.wait_ge(out_done, 16 * 8)
            ffn(UP2, DOWN2, KF, h2, 2)

            act.wait_ge(unit_done, LAST)
            nc.scalar.activation(p_hi[:], p_t[:], ACT.Copy).then_inc(pple_hi, 1)
            split_hi(LAST + 3)
            split_hi(LAST + 4)
            split_hi(LAST + 5)
            spread(3)
            for m in range(KD):
                if m:
                    split_hi(LAST + 5 + m)
                    act.wait_ge(gated, m)
                act.wait_ge(z_ready, m + 1)
                nc.scalar.activation(tb[:], ta[:], ACT.Tanh, scale=0.5).then_inc(gate_ready, 1)
                act.wait_ge(sq_added, 28 + m)
                act.wait_ge(x_ready, 24 + m + 1)
                nc.scalar.activation(sq[:], x[:, m, :], ACT.Square).then_inc(sq_made, 1)
            act.wait_ge(y_turned, 1)
            nc.scalar.activation(xf_rows[0:TS, :].rearrange("p (a c) -> p a c", a=2),
                                 ps[0:TS, 2 * Y_PAIR[NB]:2 * Y_PAIR[NB] + 2, :], ACT.Copy).then_inc(ys_taken, 1)
            act.wait_ge(rs_ready, 1)
            for b in (1, 3):
                act.wait_ge(y_turned, b + 2)
                for h in range(2):
                    nc.scalar.activation(y[:, b, h * 512:(h + 1) * 512], ps[:, 2 * Y_PAIR[b] + h, :],
                                         ACT.Copy, scale=rs[:, b:b + 1]).then_inc(y_ready[b], 1)

        @block.gpsimd
        def _(pool):
            def split_lo(n, step=0, it=None):
                if n >= END:
                    return
                pool.wait_ge(w_hi_ready, at(n + 1, step, it))
                nc.gpsimd.tensor_tensor(w_lo[:, n % RING, :], w_raw[:, n % RING, :],
                                        w_hi[:, n % RING, :].bitcast(F32), ALU.subtract).then_inc(w_lo_ready, 1)

            def clear_ssq(stat):
                if stat > 1:
                    pool.wait_ge(stat_summed, stat - 1)
                nc.gpsimd.memset(ssq[:], 0.0).then_inc(sq_added, 1)

            def add_square(stat, m, step=0, it=None):
                pool.wait_ge(sq_added, 9 * stat - 8)
                pool.wait_ge(sq_made, at(8 * stat + m - 7, step, it))
                nc.gpsimd.tensor_tensor(ssq[:], ssq[:], sq[:], ALU.add).then_inc(sq_added, 1)

            def ffn(up, down, stat):
                split_lo(up + 3)
                split_lo(up + 4)
                with pool.Fori(0, (KF - 1) // 3) as it:
                    for r in range(3):
                        split_lo(up + 2 * (1 + r) + 3, 6, it)
                        split_lo(up + 2 * (1 + r) + 4, 6, it)
                clear_ssq(stat + 1)
                with pool.Fori(0, KD // 2) as it:
                    for m in range(2):
                        for c in range(3):
                            split_lo(down + 3 * m + 3 + c, 6, it)
                        add_square(stat + 1, m, 2, it)

            nc.gpsimd.memset(ident[:], 0.0).then_inc(consts_ready, 1)
            nc.gpsimd.memset(ones[:], 1.0).then_inc(consts_ready, 1)
            nc.gpsimd.memset(var[:], 1.0).then_inc(consts_ready, 1)
            pool.wait_ge(consts_ready, 3)
            nc.gpsimd.affine_select(out=ident[:], in_=ident[:], compare_op=ALU.not_equal, fill=1.0, base=0,
                                    pattern=[[-1, P]], channel_multiplier=1).then_inc(consts_ready, 1)
            for n in range(RING):
                split_lo(n)
            ffn(UP1, DOWN1, 0)

            clear_ssq(2)
            pool.wait_ge(unit_done, IN)
            nc.gpsimd.memset(mask[:], 0.0).then_inc(mask_ready, 1)
            nc.gpsimd.memset(q_diag[:], 0.0).then_inc(s_diag_clear, 1)
            pool.wait_ge(mask_ready, 1)
            nc.gpsimd.affine_select(out=mask[:, 0, :], in_=mask[:, 0, :], compare_op=ALU.is_ge, fill=NEG, base=0,
                                    pattern=[[-1, 2 * W]], channel_multiplier=1).then_inc(mask_ready, 1)
            nc.gpsimd.affine_select(out=mask[:, 1, :], in_=mask[:, 1, :], compare_op=ALU.is_ge, fill=NEG, base=W,
                                    pattern=[[-1, 2 * W]], channel_multiplier=1).then_inc(mask_ready, 1)
            pool.wait_ge(mask_ready, 3)
            nc.gpsimd.affine_select(out=mask[:, 1, :], in_=mask[:, 1, :], compare_op=ALU.is_ge, fill=NEG, base=0,
                                    pattern=[[1, 2 * W]], channel_multiplier=-1).then_inc(mask_ready, 1)
            for kind, *arg in steps:
                if kind == "gemm" and arg[1] == 4 and arg[0] > 0:
                    split_lo(IN + arg[0] + 2)
                elif kind == "out" and arg == [0, 4]:
                    split_lo(OUT + 2)
                elif kind == "norm" and arg[0] >= NB - 1:
                    b = arg[0]
                    i, n = b - NB + 1, P if b < NB else TS
                    v = gv_rows[0:n, i, :]
                    pool.wait_ge(g_centred, i + 1)
                    nc.gpsimd.tensor_tensor(v, g_rows[0:n, b, :], lng[0:n, :], ALU.mult).then_inc(g_gained, 1)
                    pool.wait_ge(g_gained, i + 1)
                    nc.gpsimd.tensor_tensor(v, v, lnb[0:n, :], ALU.add).then_inc(g_normed, 1)
                elif kind == "ws_turn":
                    pool.wait_ge(ws_taken, 1)
                    nc.gpsimd.affine_select(out=ws_t[:], in_=ws_t[:], compare_op=ALU.is_ge, fill=0.0, base=0,
                                            pattern=[[0, GG], [1, P]], channel_multiplier=-1).then_inc(ws_ready, 1)

            for m in range(KD):
                split_lo(OUT + m + 3)
                add_square(2, m)
            ffn(UP2, DOWN2, 2)
            for n in range(LAST + 3, LAST + 6):
                split_lo(n)
            clear_ssq(4)
            for m in range(KD):
                if m:
                    split_lo(LAST + 5 + m)
                if m < KD - 1:
                    add_square(4, m)

        @block.vector
        def _(dve):
            chain = [0]

            def link(ins):
                chain[0] += 1
                ins.then_inc(dve_step, 1)
                dve.wait_ge(dve_step, chain[0])

            def rsqrt():
                link(nc.vector.tensor_scalar(rs_i[:], var[:].bitcast(I32), 1, None, ALU.logical_shift_right))
                link(nc.vector.tensor_scalar(rs[:].bitcast(I32), rs_i[:], -1.0, RSQRT_SEED, ALU.mult, ALU.add))
                for _ in range(3):
                    link(nc.vector.scalar_tensor_tensor(out=rs_t[:], in0=rs[:], scalar=-0.5, in1=rs[:], op0=ALU.mult,
                                                        op1=ALU.mult))
                    link(nc.vector.tensor_tensor(rs_t[:], rs_t[:], var[:], ALU.mult))
                    link(nc.vector.scalar_tensor_tensor(out=rs[:], in0=rs_t[:], scalar=1.5, in1=rs[:], op0=ALU.add,
                                                        op1=ALU.mult))

            def stat_rsqrt(stat):
                if stat:
                    dve.wait_ge(stat_summed, stat)
                    sums = ps[:, STAT_BANK[stat], 0:NB + 1]
                else:
                    dve.wait_ge(row_sums, 2)
                    sums = rs_t[:, 0:NB + 1]
                link(nc.vector.tensor_scalar(var[:, 0:NB], sums[:, 0:NB], 1.0 / D, RMS_EPS, ALU.mult, ALU.add))
                link(nc.vector.tensor_scalar(var[0:TS, NB:NB + 1], sums[0:TS, NB:NB + 1], 1.0 / D, RMS_EPS,
                                             ALU.mult, ALU.add))
                if stat == 4:
                    nc.vector.tensor_copy(rs_t[:], var[:]).then_inc(sums_taken, 1)
                rsqrt()

            def stat_diag(stat):
                stat_rsqrt(stat)
                nc.vector.tensor_tensor(diag[:, 0:TP].rearrange("p (b t) -> p b t", t=P),
                                        ident[:].unsqueeze(1).broadcast_to([P, NB, P]),
                                        rs[:, 0:NB].unsqueeze(2).broadcast_to([P, NB, P]),
                                        ALU.mult).then_inc(diag_ready, 1)
                nc.vector.tensor_scalar(diag[0:TS, TP:T], ident[0:TS, 0:TS], rs[0:TS, NB:NB + 1], None,
                                        ALU.mult).then_inc(diag_ready, 1)

            def x_lo(stat, m, step=0, it=None):
                dve.wait_ge(xg_hi_ready, at(8 * stat + m + 1, step, it))
                nc.vector.scalar_tensor_tensor(out=tile_of(xg_lo, m, step, it), in0=tile_of(x, m, step, it),
                                               scalar=col(8 * stat + m, step, it),
                                               in1=tile_of(xg_hi, m, step, it).bitcast(F32),
                                               op0=ALU.mult, op1=ALU.subtract).then_inc(xg_lo_ready, 1)

            def take_turned(dst, p):
                nc.vector.tensor_copy(dst[:, 0:TP], ps[:, 2 * p, :])
                return nc.vector.tensor_copy(dst[:, TP:T], ps[:, 2 * p + 1, 0:TS])

            def up_step(base, f0, h, f, it):
                if f0 + f:
                    dve.wait_ge(tanh_ready, at(f0 + f, 3, it))
                dve.wait_ge(unit_done, at(base + 2 * f + 1, 6, it))
                nc.vector.tensor_tensor(halves(ta[:]), pair(2 * f % 3), halves(rstd[:]), ALU.mult).then_inc(a_ready, 1)
                if f0 + f:
                    dve.wait_ge(h_lo_ready, at(f0 + f, 3, it))
                dve.wait_ge(a_ready, at(f0 + f + 1, 3, it))
                dve.wait_ge(unit_done, at(base + 2 * f + 2, 6, it))
                nc.vector.tensor_tensor(halves(tq[:]), pair((2 * f + 1) % 3), halves(ta[:]),
                                        ALU.mult).then_inc(ab_ready, 1)
                dve.wait_ge(ab_ready, at(f0 + f + 1, 3, it))
                nc.vector.tensor_tensor(tq[:], tq[:], rstd[:], ALU.mult).then_inc(ab_scaled, 1)
                dve.wait_ge(tanh_ready, at(f0 + f + 1, 3, it))
                dve.wait_ge(ab_scaled, at(f0 + f + 1, 3, it))
                nc.vector.scalar_tensor_tensor(out=tq[:], in0=tb[:], scalar=1.0, in1=tq[:], op0=ALU.add,
                                               op1=ALU.mult).then_inc(h_ready, 1)
                dve.wait_ge(h_hi_ready, at(f0 + f + 1, 3, it))
                nc.vector.tensor_tensor(tile_of(h[1], f, 3, it), tq[:], tile_of(h[0], f, 3, it).bitcast(F32),
                                        ALU.subtract).then_inc(h_lo_ready, 1)

            def down_step(base, stat, m, it):
                dve.wait_ge(unit_done, at(base + 3 * m + 3, 6, it))
                nc.vector.scalar_tensor_tensor(out=halves(tile_of(x, m, 2, it)), in0=pair(m % 2), scalar=0.25,
                                               in1=halves(tile_of(x, m, 2, it)), op0=ALU.mult,
                                               op1=ALU.add).then_inc(x_ready, 1)
                x_lo(stat, m, 2, it)

            def ffn(up, down, f0, h, stat):
                dve.wait_ge(rstd_ready, 2 * (stat + 1))
                up_step(up, f0, h, 0, None)
                with dve.Fori(0, (KF - 1) // 3) as it:
                    for r in range(3):
                        up_step(up, f0, h, 1 + r, it)
                if stat == 0:
                    for k in range(KP):
                        dve.wait_ge(p_turned, k + 1)
                        take_turned(p_t[:, k, :], 3 - k)
                with dve.Fori(0, KD // 2) as it:
                    for m in range(2):
                        down_step(down, stat + 1, m, it)

            for b in range(NB - 1):
                dve.wait_ge(x_in[b], 16)
                link(nc.vector.tensor_tensor_reduce(out=sq_rows[:, b % 2, :], in0=x_rows[:, b, :], in1=x_rows[:, b, :],
                                                    scale=1.0, scalar=0.0, op0=ALU.mult, op1=ALU.add,
                                                    accum_out=rs_t[:, b:b + 1]))
            dve.wait_ge(cols_turned, 1)
            nc.vector.tensor_copy(cols[:, 0:KD], ps[:, 6, 0:KD]).then_inc(cols_ready, 1)
            dve.wait_ge(cols_ready, 1)
            for m in range(0, KD, 2):
                dve.wait_ge(x_turned, m + 1)
                take_turned(x[:, m, :], 1 + m % 3).then_inc(x_even, 1)
                if m:
                    x_lo(0, m - 1)
                x_lo(0, m)
            x_lo(0, KD - 1)
            stat_diag(0)
            dve.wait_ge(cols_turned, 2)
            nc.vector.tensor_copy(cols[:, KD:N_COLS], ps[:, 7, KD:N_COLS]).then_inc(cols_ready, 1)
            dve.wait_ge(cols_ready, 2)
            link(nc.vector.tensor_scalar(cols_g[:, KD:N_COLS], cols[:, KD:N_COLS], GELU_K, None, ALU.mult))
            ffn(UP1, DOWN1, 0, h1, 0)

            n_gelu = 0
            for kind, *arg in steps:
                if kind == "stat_sum":
                    stat_diag(1)
                elif kind == "evac":
                    u, name = arg[0], IN_ORDER[arg[0]]
                    if u == 0:
                        dve.wait_ge(rstd_ready, 4)
                    else:
                        dve.wait_ge(z_done, u)
                    dve.wait_ge(unit_done, IN + u + 1)
                    nc.vector.tensor_tensor(halves(ta[:]), pair(IN_PAIR[u]), halves(rstd[:]),
                                            ALU.mult).then_inc(z_scaled, 1)
                    if name[0] in "ug":
                        n_gelu += 1
                elif kind == "gelu_mid":
                    dve.wait_ge(gelu_sq, n_gelu)
                    dve.wait_ge(z_done, arg[0] + 1)
                    nc.vector.scalar_tensor_tensor(out=tb[:], in0=tb[:], scalar=1.0, in1=tq[:], op0=ALU.add,
                                                   op1=ALU.mult).then_inc(gelu_arg, 1)
                elif kind == "gelu_end":
                    name = IN_ORDER[arg[0]]
                    g = int(name[1])
                    if name[0] == "g" and g:
                        dve.wait_ge(g_turned, g)
                    dve.wait_ge(gelu_tanh, n_gelu)
                    nc.vector.scalar_tensor_tensor(out=g_t[:] if name[0] == "g" else gu[:, g % 2, :], in0=tb[:],
                                                   scalar=1.0, in1=tq[:], op0=ALU.add,
                                                   op1=ALU.mult).then_inc(gelu_done, 1)
                elif kind == "soft":
                    i = arg[0]
                    j, bp, c0 = i // 2, i % 2, 16 * (i % 2)
                    dst = probs[:, bp]
                    dve.wait_ge(scored, i + 1)
                    if i == 0:
                        dve.wait_ge(mask_ready, 4)
                        dve.wait_ge(mix_in, 16 * mix_loads)
                    if i >= 2:
                        dve.wait_ge(probs_turned, 2 * (i - 1))
                    for c in range(NKV):
                        for r in range(2):
                            n = keys(bp, r)
                            ins = nc.vector.tensor_tensor_reduce(
                                out=dst[:, c, r, 0:n], in0=ps[:, 4 + c, r * 2 * W:r * 2 * W + n],
                                in1=mask[:, 1 if bp else r, 0:n], scale=SCALE, scalar=sink[:, c * GQ + j:c * GQ + j + 1],
                                op0=ALU.add, op1=ALU.max, accum_out=st[:, c0 + 12 + 2 * c + r:c0 + 13 + 2 * c + r])
                    ins.then_inc(masked, 1)
                    dve.wait_ge(masked, i + 1)
                    link(nc.vector.tensor_scalar(st[:, c0:c0 + 4], st[:, c0 + 12:c0 + 16], -1.0, None, ALU.mult))
                    nc.vector.tensor_tensor(st[:, c0 + 4:c0 + 8].rearrange("p (c b) -> p c b", c=NKV),
                                            st[:, c0:c0 + 4].rearrange("p (c b) -> p c b", c=NKV),
                                            sink[:].rearrange("p (c j) -> p c j", c=NKV)[:, :, j:j + 1]
                                            .broadcast_to([P, NKV, 2]), ALU.add).then_inc(max_ready, 1)
                elif kind == "p_turn" and arg[1] == 0:
                    i = arg[0]
                    c0 = 16 * (i % 2)
                    dve.wait_ge(exp_done, 5 * (i + 1))
                    link(nc.vector.tensor_tensor(st[:, c0 + 12:c0 + 16], st[:, c0 + 8:c0 + 12], st[:, c0 + 4:c0 + 8],
                                                 ALU.add))
                    link(nc.vector.reciprocal(st[:, c0 + 12:c0 + 16], st[:, c0 + 12:c0 + 16]))
                elif kind == "values":
                    i = arg[0]
                    c0 = 16 * (i % 2)
                    dve.wait_ge(o_made, i + 1)
                    if i:
                        dve.wait_ge(o_turned, i)
                    nc.vector.tensor_tensor(
                        o_rows[:], ps[:, 7, 0:256].rearrange("p (b c d) -> p b c d", b=2, c=NKV),
                        st[:, c0 + 12:c0 + 16].rearrange("p (c b) -> p b c", c=NKV).unsqueeze(3)
                        .broadcast_to([P, 2, NKV, HD]), ALU.mult).then_inc(o_taken, 1)
                elif kind == "o_turn":
                    i = arg[0]
                    part = slice(256 * (i % 2), 256 * (i % 2) + 256)
                    dve.wait_ge(o_hi, i + 1)
                    nc.vector.tensor_tensor(mix_lo[:, i // 2, part], ps[:, 7, 256:512],
                                            mix_hi[:, i // 2, part].bitcast(F32), ALU.subtract).then_inc(o_lo, 1)
                elif kind == "norm_stats":
                    b = arg[0]
                    n = P if b < NB else TS
                    dve.wait_ge(g_taken, GG)
                    link(nc.vector.bn_stats(bn[0:n, b, :], g_rows[0:n, b, :]))
                    link(nc.vector.bn_aggr(mv[0:n, b, :], bn[0:n, b, :]))
                    link(nc.vector.tensor_scalar(var[0:n, b:b + 1], mv[0:n, b, 1:2], 4 * LN_EPS, None, ALU.add))
                elif kind == "norm_rsqrt":
                    rsqrt()
                elif kind == "norm":
                    b = arg[0]
                    n = P if b < NB else TS
                    v = g_rows[0:n, b, :]
                    nc.vector.tensor_scalar(v, v, mv[0:n, b, 0:1], rs[0:n, b:b + 1], ALU.subtract,
                                            ALU.mult).then_inc(g_centred, 1)
                elif kind == "ws_sum":
                    dve.wait_ge(ws_summed, 1)
                    for g in range(GG):
                        nc.vector.scalar_tensor_tensor(out=bs_all[:, g, :], in0=ps[:, 4, g * P:(g + 1) * P],
                                                       scalar=col(C_LNB + g), in1=bs_all[:, g, :], op0=ALU.mult,
                                                       op1=ALU.add).then_inc(bs_ready, 1)
                elif kind == "spatial":
                    g = arg[0]
                    dve.wait_ge(spatial_made, g + 1)
                    if g:
                        dve.wait_ge(gm_lo, g)
                    dve.wait_ge(bs_ready, GG)
                    nc.vector.scalar_tensor_tensor(out=sp[:, 0:TP].rearrange("p (b t) -> p b t", t=P),
                                                   in0=ps[:, 4, :].rearrange("p (b t) -> p b t", t=P),
                                                   scalar=col(C_LNG + g),
                                                   in1=bs_all[:, g:g + 1, :].broadcast_to([P, NB, P]),
                                                   op0=ALU.mult, op1=ALU.add)
                    nc.vector.tensor_scalar(sp[:, TP:T], ps[:, 5, 384:384 + TS], col(C_LNG + g), bs_all[:, g, 0:1],
                                            ALU.mult, ALU.add).then_inc(spatial_taken, 1)
                elif kind == "gm":
                    g = arg[0]
                    dve.wait_ge(spatial_taken, g + 1)
                    dve.wait_ge(gelu_done, GG + g + 1)
                    nc.vector.tensor_tensor(sp[:], sp[:], gu[:, g % 2, :], ALU.mult).then_inc(gm_ready, 1)
                elif kind == "gm_lo":
                    g = arg[0]
                    dve.wait_ge(gm_hi, g + 1)
                    nc.vector.scalar_tensor_tensor(out=mix_lo[:, 4 + g, :], in0=sp[:], scalar=0.5,
                                                   in1=mix_hi[:, 4 + g, :].bitcast(F32), op0=ALU.mult,
                                                   op1=ALU.subtract).then_inc(gm_lo, 1)
                elif kind == "s_build":
                    nc.vector.tensor_tensor(w00_diag[:], ident[0:TS, 0:TS].unsqueeze(1).broadcast_to([TS, GG, TS]),
                                            w00[:].unsqueeze(2).broadcast_to([TS, GG, TS]),
                                            ALU.mult).then_inc(w00_ready, 1)
                    dve.wait_ge(s_diag_clear, 1)
                    dve.wait_ge(z_done, IN_ORDER.index("q3") + 1)
                    for c in range(NKV):
                        part = slice(c * HD, (c + 1) * HD)
                        link(nc.vector.tensor_copy(q_diag[part, :, c * GQ:(c + 1) * GQ],
                                                   q_t[part, :, TP:T].rearrange("p j s -> p s j")))
                    nc.vector.tensor_tensor(qk_new[:], q_diag[:], k_t[:, TP:T].unsqueeze(2).broadcast_to([P, TS, NQ]),
                                            ALU.mult).then_inc(s_built, 1)
                elif kind == "s_scores":
                    dve.wait_ge(s_scored, 1)
                    nc.vector.tensor_copy(s_keys[:], ps[:, 5, 0:64]).then_inc(s_taken, 1)
                elif kind == "s_softmax":
                    dve.wait_ge(s_turned, 1)
                    link(nc.vector.tensor_scalar(s_p[:, 0:W], ps[0:64, 5, 128:256], SCALE, None, ALU.mult))
                    link(nc.vector.tensor_scalar(s_p[:, W:W + 1], ps[0:64, 5, 64:65], SCALE, None, ALU.mult))
                    link(nc.vector.tensor_reduce(s_st[:, 3:4], s_p[:], AX_X, ALU.max))
                    link(nc.vector.tensor_tensor(s_st[:, 3:4], s_st[:, 3:4], s_sink[:], ALU.max))
                    link(nc.vector.tensor_scalar(s_st[:, 0:1], s_st[:, 3:4], -1.0, None, ALU.mult))
                    nc.vector.tensor_tensor(s_st[:, 1:2], s_st[:, 0:1], s_sink[:], ALU.add).then_inc(s_max, 1)
                    dve.wait_ge(s_exp, 2)
                    link(nc.vector.tensor_tensor(s_st[:, 4:5], s_st[:, 1:2], s_st[:, 2:3], ALU.add))
                    link(nc.vector.reciprocal(s_st[:, 5:6], s_st[:, 4:5]))
                    link(nc.vector.tensor_scalar(s_p[:], s_p[:], s_st[:, 5:6], None, ALU.mult))
                    nc.vector.tensor_scalar(s_new[:], ident[0:64, 0:64], s_p[:, W:W + 1], None,
                                            ALU.mult).then_inc(s_normed, 1)
                elif kind == "s_probs":
                    dve.wait_ge(s_p_turned, 1)
                    nc.vector.tensor_copy(s_pt[:], ps[:, 5, 0:64]).then_inc(s_p_taken, 1)
                    nc.vector.tensor_tensor(s_pv[:], ps[:, 5, 64:128].rearrange("p (s h) -> p s h", s=TS),
                                            v_t[:, TP:T].unsqueeze(2).broadcast_to([P, TS, NQ]),
                                            ALU.mult).then_inc(s_p_taken, 1)
                elif kind == "s_values":
                    dve.wait_ge(s_valued, 1)
                    dve.wait_ge(s_p_taken, 2)
                    nc.vector.tensor_tensor(s_o[:], ps[:, 5, 256:320].rearrange("p (s h) -> p s h", s=TS), s_pv[:],
                                            ALU.add).then_inc(s_out, 1)
                    for c in range(NKV):
                        part = slice(c * HD, (c + 1) * HD)
                        dve.wait_ge(s_hi, c + 1)
                        nc.vector.tensor_tensor(mix_lo[part, 0:4, TP:T],
                                                s_o[part, :, c * GQ:(c + 1) * GQ].rearrange("p s j -> p j s"),
                                                mix_hi[part, 0:4, TP:T].bitcast(F32), ALU.subtract).then_inc(s_lo, 1)

            for m in range(KD):
                dve.wait_ge(unit_done, OUT + m + 1)
                nc.vector.scalar_tensor_tensor(out=halves(x[:, m, :]), in0=pair((m + 1) % 3), scalar=col(C_BOUT + m),
                                               in1=halves(x[:, m, :]), op0=ALU.add,
                                               op1=ALU.add).then_inc(x_ready, 1)
                x_lo(2, m)
            stat_diag(2)
            ffn(UP2, DOWN2, KF, h2, 2)

            dve.wait_ge(pple_hi, 1)
            nc.vector.tensor_tensor(p_lo[:], p_t[:], p_hi[:].bitcast(F32), ALU.subtract).then_inc(pple_lo, 1)
            for m in range(KD):
                if m % 4 == 3:
                    dve.wait_ge(unit_done, LAST + 2 + m // 4)
                else:
                    dve.wait_ge(pp_made, 3 * (m // 4) + m % 4 + 1)
                nc.vector.tensor_copy(halves(pp[:, m, :]), pair(1 + m % 2)).then_inc(pp_ready, 1)
            stat_diag(3)
            for m in range(KD):
                if m == 0:
                    dve.wait_ge(rstd_ready, 8)
                else:
                    dve.wait_ge(gate_ready, m)
                dve.wait_ge(unit_done, LAST + 1 if m == 0 else LAST + 3 + m)
                nc.vector.tensor_tensor(halves(ta[:]), pair(m % 3), halves(rstd[:]), ALU.mult).then_inc(z_ready, 1)
                dve.wait_ge(gate_ready, m + 1)
                nc.vector.scalar_tensor_tensor(out=tq[:], in0=tb[:], scalar=1.0, in1=pp[:, m, :], op0=ALU.add,
                                               op1=ALU.mult).then_inc(gated, 1)
                dve.wait_ge(gated, m + 1)
                nc.vector.scalar_tensor_tensor(out=x[:, m, :], in0=tq[:], scalar=0.5, in1=x[:, m, :], op0=ALU.mult,
                                               op1=ALU.add).then_inc(x_ready, 1)
                dve.wait_ge(x_ready, 24 + m + 1)
                nc.vector.tensor_scalar(xf[:, m, :], x[:, m, :], col(C_FIN + m), None, ALU.mult).then_inc(xf_ready, 1)

            stat_rsqrt(4)
            nc.vector.tensor_copy(rs_t[:], rs[:]).then_inc(rs_ready, 1)
            for b in (0, 2):
                dve.wait_ge(y_turned, b + 2)
                for h in range(2):
                    nc.vector.tensor_scalar(y[:, b, h * 512:(h + 1) * 512], ps[:, 2 * Y_PAIR[b] + h, :],
                                            rs[:, b:b + 1], None, ALU.mult).then_inc(y_ready[b], 1)
                if b == 2:
                    dve.wait_ge(ys_taken, 1)
                    nc.vector.tensor_scalar(y[0:TS, NB, :], xf_rows[0:TS, :], rs[0:TS, NB:NB + 1], None,
                                            ALU.mult).then_inc(y_ready[NB], 1)

        @block.tensor
        def _(pe):
            def k_step(n, k, src, sk, p, first, last):
                for i, (w, m_) in enumerate(((w_hi, src[0]), (w_hi, src[1]), (w_lo, src[0]))):
                    for h in range(2):
                        ins = pe.matmul(ps[:, 2 * p + h, 0:HALF], w[:, n % RING, k * P:(k + 1) * P],
                                        m_[:, sk, h * HALF:(h + 1) * HALF],
                                        start=(first and i == 0), stop=(last and i == 2))
                return ins

            def unit(n, src, p, sk0=0, kn=KD, first=True, last=True, step=0, it=None, ready=None,
                     between=()):
                pe.wait_ge(w_lo_ready, at(n + 1, step, it))
                for k in range(kn):
                    if ready:
                        pe.wait_ge(ready[0], ready[1] + k + 1)
                    for k_, stage in between:
                        if k_ == k:
                            stage()
                    ins = k_step(n, k, src, sk0 + k, p, first and k == 0, last and k == kn - 1)
                ins.then_inc(unit_done, 1)

            def stat_sum(stat):
                pe.wait_ge(sq_added, 9 * stat)
                bank = STAT_BANK[stat]
                for b in range(NB + 1):
                    n = P if b < NB else TS
                    ins = pe.matmul(ps[0:n, bank, b:b + 1], ssq[:, b * P:b * P + n], ones[:, 0:1], start=True, stop=True)
                ins.then_inc(stat_summed, 1)

            def stat_out(stat):
                pe.wait_ge(diag_ready, 2 * (stat + 1))
                pe.matmul(ps[:, 6, :], ones[:], diag[:, 0:TP], start=True, stop=True)
                pe.matmul(ps[:, 7, 8:8 + TS], ones[0:TS, :], diag[0:TS, TP:T], start=True,
                          stop=True).then_inc(stat_spread, 1)

            def turn(dst, src, n=P):
                return pe.transpose(dst, src, ident[0:n, 0:n])

            def turn_tile(rows_, s_rows, c, p):
                for b in range(NB):
                    turn(ps[:, 2 * p, b * P:(b + 1) * P], rows_[:, b, c * P:(c + 1) * P])
                return turn(ps[:, 2 * p + 1, 0:TS], s_rows[0:TS, c * P:(c + 1) * P], TS)

            def up_a(base, f0, f, it, src, between=()):
                if f0 + f > 1:
                    pe.wait_ge(ab_ready, at(f0 + f - 1, 3, it))
                unit(base + 2 * f, src, 2 * f % 3, step=6, it=it, between=between)

            def up_b(base, f0, f, it, src):
                pe.wait_ge(a_ready, at(f0 + f, 3, it))
                unit(base + 2 * f + 1, src, (2 * f + 1) % 3, step=6, it=it)

            def down_step(base, f0, stat, h, m, it):
                pe.wait_ge(xg_lo_ready, at(8 * stat + m - 1, 2, it))
                for c, kn in enumerate(DOWN_K):
                    pe.wait_ge(h_lo_ready, f0 + 8 * c + kn)
                    unit(base + 3 * m + c, h, m % 2, 8 * c, kn, c == 0, c == 2, 6, it)

            def ffn(up, down, f0, h, stat, src):
                up_a(up, f0, 1, None, src, between=[(1, lambda: stat_out(stat))])
                with pe.Fori(0, (KF - 1) // 3 - 1) as it:
                    for f in range(1, 4):
                        up_b(up, f0, f, it, src)
                        up_a(up, f0, f + 1, it, src)
                for f in range(KF - 3, KF):
                    up_b(up, f0, f, None, src)
                    if f < KF - 1:
                        up_a(up, f0, f + 1, None, src)
                if stat == 0:
                    pe.wait_ge(p_in, 16)
                    pe.wait_ge(ps_in, 16)
                    turn_tile(p_rows, ps_rows, 0, 3).then_inc(p_turned, 1)
                    pe.wait_ge(a_ready, KF)
                    turn_tile(p_rows, ps_rows, 1, 2).then_inc(p_turned, 1)
                pe.wait_ge(a_ready, f0 + KF)
                with pe.Fori(0, KD // 2) as it:
                    for m in range(2):
                        down_step(down, f0, stat + 1, h, m, it)

            xg = xg_hi, xg_lo

            pe.wait_ge(consts_ready, 4)
            pe.wait_ge(gain_in, 16)
            pe.transpose(ps[:, 6, 0:KD], rows[0:KD, :], ident[0:KD, 0:KD]).then_inc(cols_turned, 1)
            for s_ in x_in:
                pe.wait_ge(s_, 16)
            for m in range(KD):
                if m >= 3:
                    pe.wait_ge((x_odd, x_even)[m % 2], (m - 3) // 2 + 1)
                elif m == 2:
                    pe.wait_ge(cols_ready, 1)
                turn_tile(x_rows, xs_rows, m, 1 + m % 3).then_inc(x_turned, 1)

            def turn_vectors():
                pe.wait_ge(rows_in, 16 * 10)
                pe.wait_ge(x_odd, 3)
                pe.transpose(ps[:, 7, 0:N_COLS], rows[0:N_COLS, :], ident[0:N_COLS, 0:N_COLS]).then_inc(cols_turned, 1)

            unit(UP1, xg, 0, ready=(xg_lo_ready, 0))
            unit(UP1 + 1, xg, 1, between=[(1, turn_vectors)])
            pe.wait_ge(cols_ready, 2)
            ffn(UP1, DOWN1, 0, h1, 0, xg)

            for kind, *arg in steps:
                if kind == "gemm":
                    u, k = arg
                    n = IN + u
                    if k == 0:
                        if u < 2:
                            pe.wait_ge(x_ready, 7 + u)
                        if u == 2:
                            pe.wait_ge(cache_taken, 1)
                        if u >= 3:
                            pe.wait_ge(z_scaled, u - 1 if u > 3 else 1)
                        pe.wait_ge(w_lo_ready, n + 1)
                    if u == 0:
                        pe.wait_ge(xg_lo_ready, 8 + k + 1)
                    ins = k_step(n, k, xg, k, IN_PAIR[u], k == 0, k == KD - 1)
                    if k == KD - 1:
                        ins.then_inc(unit_done, 1)
                elif kind == "out":
                    m, k = arg
                    n = OUT + m
                    if k == 0:
                        pe.wait_ge(w_lo_ready, n + 1)
                        if m == 0:
                            pe.wait_ge(z_scaled, 13)
                            pe.wait_ge(s_lo, 2)
                        else:
                            pe.wait_ge(spatial_taken, GG)
                    if m == 0 and k >= 4:
                        pe.wait_ge(gm_lo, k - 3)
                    elif m == 0 and k == 3:
                        pe.wait_ge(o_lo, 8)
                    ins = k_step(n, k, (mix_hi, mix_lo), k, m + 1, k == 0, k == KD - 1)
                    if k == KD - 1:
                        ins.then_inc(unit_done, 1)
                elif kind == "stat_sum":
                    stat_sum(1)
                elif kind == "stat_spread":
                    stat_out(1)
                elif kind == "cache_turn":
                    pe.wait_ge(cache_in, 16)
                    for b in range(TS):
                        ins = turn(ps[:, 4 + b // 4, (b % 4) * W:(b % 4 + 1) * W], cache_k[:, b, :])
                    ins.then_inc(cache_turned, 1)
                elif kind == "ws_turn":
                    pe.wait_ge(ws_in, 16)
                    pe.wait_ge(rstd_ready, 4)
                    for g in range(GG):
                        ins = turn(ps[:, 6, g * P:(g + 1) * P], ws_rows[:, g, :])
                    ins.then_inc(ws_turned, 1)
                elif kind == "g_turn":
                    g = arg[0]
                    pe.wait_ge(gelu_done, g + 1)
                    pe.wait_ge(masked, sum(1 for u in ITEM_UNIT if u <= IN_ORDER.index(f"g{g}") + 1))
                    for b in range(NB):
                        turn(ps[:, 4, b * P:(b + 1) * P], g_t[:, b * P:(b + 1) * P])
                    pe.transpose(ps[0:TS, 5, 0:P], g_t[:, TP:T], ident[:]).then_inc(g_turned, 1)
                elif kind == "ws_sum":
                    pe.wait_ge(ws_ready, 1)
                    pe.wait_ge(masked, sum(1 for u in ITEM_UNIT if u <= 8))
                    pe.matmul(ps[:, 4, :], ones[:], ws_t[:].rearrange("p g t -> p (g t)"), start=True,
                              stop=True).then_inc(ws_summed, 1)
                elif kind == "kv_turn":
                    pe.wait_ge(z_done, 2)
                    pe.wait_ge(ws_taken, 1)
                    for b in range(NB):
                        turn(ps[:, 6, b * P:(b + 1) * P], v_t[:, b * P:(b + 1) * P])
                    pe.transpose(ps[0:TS, 7, 0:P], v_t[:, TP:T], ident[:])
                    turn(ps[:, 7, P:2 * P], k_t[:, TP - P:TP])
                    pe.transpose(ps[0:TS, 7, 2 * P:3 * P], k_t[:, TP:T], ident[:]).then_inc(kv_turned, 1)
                elif kind == "scores":
                    i = arg[0]
                    j, bp = i // 2, i % 2
                    pe.wait_ge(z_done, IN_ORDER.index(f"q{j}") + 1)
                    if i == 0:
                        pe.wait_ge(z_scaled, 3)
                    turned = sum(1 for u, name in enumerate(IN_ORDER) if name[0] == "g" and u + 1 < ITEM_UNIT[i])
                    if turned:
                        pe.wait_ge(g_taken, turned)
                    if i:
                        pe.wait_ge(masked, i)
                    if i == 5:
                        pe.wait_ge(bs_ready, GG)
                    if i == 7:
                        pe.wait_ge(s_max, 1)
                    for c in range(NKV):
                        part = slice(c * HD, (c + 1) * HD)
                        for r in range(2):
                            b = 2 * bp + r
                            k0 = max(b - 1, 0) * W
                            n = keys(bp, r)
                            ins = pe.matmul(ps[:, 4 + c, r * 2 * W:r * 2 * W + n], q_t[part, j, b * P:(b + 1) * P],
                                            k_t[part, k0:k0 + n], start=True, stop=True)
                    ins.then_inc(scored, 1)
                elif kind == "p_turn":
                    i, r = arg
                    pe.wait_ge(exp_done, 5 * (i + 1))
                    if 2 * i + r == 0:
                        pe.wait_ge(kv_taken, 4)
                    else:
                        pe.wait_ge(probs_taken, 2 * i + r)
                    for c in range(NKV):
                        for k in range(keys(i % 2, r) // W):
                            ins = turn(ps[:, 6, (2 * c + k) * P:(2 * c + k + 1) * P],
                                       probs[:, i % 2, c, r, k * W:(k + 1) * W])
                    ins.then_inc(probs_turned, 1)
                elif kind == "values":
                    i = arg[0]
                    bp = i % 2
                    pe.wait_ge(probs_taken, 2 * i + 2)
                    if i:
                        pe.wait_ge(o_lo, i)
                    for r in range(2):
                        b = 2 * bp + r
                        ks = (0,) if b == 0 else (0, 1)
                        for c in range(NKV):
                            for k in ks:
                                ins = pe.matmul(ps[:, 7, r * P + c * HD:r * P + (c + 1) * HD], probs_t[:, r, c, k, :],
                                                v_rows[:, max(b - 1, 0) + k, c * HD:(c + 1) * HD],
                                                start=(k == 0), stop=(k == ks[-1]))
                    ins.then_inc(o_made, 1)
                elif kind == "o_turn":
                    i = arg[0]
                    pe.wait_ge(o_taken, i + 1)
                    for r in range(2):
                        ins = turn(ps[:, 7, (2 + r) * P:(3 + r) * P], o_rows[:, r].rearrange("p c d -> p (c d)"))
                    ins.then_inc(o_turned, 1)
                elif kind == "spatial":
                    g = arg[0]
                    pe.wait_ge(g_centred, NB + 1)
                    pe.wait_ge(ws_ready, 1)
                    pe.wait_ge(w00_ready, 1)
                    if g:
                        pe.wait_ge(spatial_taken, g)
                    else:
                        pe.wait_ge(s_out, 1)
                    for b in range(NB):
                        pe.matmul(ps[:, 4, b * P:(b + 1) * P], g_rows[:, b, g * P:(g + 1) * P], ws_t[:, g, :],
                                  start=True, stop=True)
                    pe.matmul(ps[:, 5, 384:384 + TS], g_rows[0:TS, NB, g * P:(g + 1) * P], w00_diag[:, g, :],
                              start=True, stop=True).then_inc(spatial_made, 1)
                elif kind == "s_scores":
                    pe.wait_ge(s_built, 1)
                    pe.wait_ge(masked, 7)
                    for b in range(TS):
                        pe.matmul(ps[:, 5, b * NQ:(b + 1) * NQ], cache_k_t[:, b, :], q_diag[:, b, :],
                                  start=True, stop=True)
                    pe.matmul(ps[0:64, 5, 64:65], qk_new[:].rearrange("p s h -> p (s h)"), ones[:, 0:1],
                              start=True, stop=True).then_inc(s_scored, 1)
                elif kind == "s_softmax":
                    pe.wait_ge(s_taken, 1)
                    pe.transpose(ps[0:64, 5, 128:256], s_keys[:], ident[:]).then_inc(s_turned, 1)
                elif kind == "s_probs":
                    pe.wait_ge(s_normed, 1)
                    pe.wait_ge(masked, 8)
                    pe.transpose(ps[:, 5, 0:64], s_p[:, 0:W], ident[0:64, 0:64])
                    pe.matmul(ps[:, 5, 64:128], ones[0:64, :], s_new[:], start=True, stop=True).then_inc(s_p_turned, 1)
                elif kind == "s_values":
                    pe.wait_ge(s_p_taken, 2)
                    for b in range(TS):
                        ins = pe.matmul(ps[:, 5, 256 + b * NQ:256 + (b + 1) * NQ], cache_v[:, b, :],
                                        s_pt[:, b * NQ:(b + 1) * NQ], start=True, stop=True)
                    ins.then_inc(s_valued, 1)

            for m in range(2, KD):
                n = OUT + m
                pe.wait_ge(w_lo_ready, n + 1)
                if m == 2:
                    pe.wait_ge(z_scaled, 14)
                else:
                    pe.wait_ge(x_ready, 8 + m - 2)
                for k in range(KD):
                    ins = k_step(n, k, (mix_hi, mix_lo), k, (m + 1) % 3, k == 0, k == KD - 1)
                ins.then_inc(unit_done, 1)

            pe.wait_ge(x_ready, 8 + 6)
            unit(UP2, xg, 0, ready=(xg_lo_ready, 16))
            pe.wait_ge(x_ready, 8 + 7)
            unit(UP2 + 1, xg, 1, between=[(2, lambda: stat_sum(2))])
            pe.wait_ge(x_ready, 8 + 8)
            ffn(UP2, DOWN2, KF, h2, 2, xg)

            pe.wait_ge(x_ready, 16 + 7)
            unit(LAST, xg, 0, ready=(xg_lo_ready, 24))
            pe.wait_ge(pple_lo, 1)
            for i in range(2):
                n = LAST + 1 + i
                pe.wait_ge(w_lo_ready, n + 1)
                for q in range(4):
                    m = 4 * i + q
                    if m >= 2:
                        pe.wait_ge(pp_ready, m - 1)
                    for k in range(KP):
                        ins = k_step(n, 4 * k + q, (p_hi, p_lo), k, 1 + m % 2, k == 0, k == KP - 1)
                    ins.then_inc(unit_done if q == 3 else pp_made, 1)
            stat_sum(3)
            for m in range(1, KD):
                if m < 3:
                    pe.wait_ge(pp_ready, KD - 2 + m)
                else:
                    pe.wait_ge(z_ready, m - 2)
                unit(LAST + 2 + m, xg, m % 3, between=[(6, lambda: stat_out(3))] if m == 1 else ())

            def turn_back(b, ks):
                n = P if b < NB else TS
                for k in ks:
                    ins = pe.transpose(ps[0:n, 2 * Y_PAIR[b] + k // 4, (k % 4) * P:(k % 4 + 1) * P],
                                       xf[:, k, b * P:b * P + n], ident[:])
                return ins

            pe.wait_ge(rstd_ready, 8)
            pe.wait_ge(xf_ready, KD - 1)
            pe.wait_ge(z_ready, KD - 1)
            for b in (0, 1):
                turn_back(b, range(KD - 1))
            pe.wait_ge(z_ready, KD)
            turn_back(NB, range(KD - 1))
            pe.wait_ge(xf_ready, KD)
            for b in (NB, 0, 1):
                turn_back(b, (KD - 1,)).then_inc(y_turned, 1)
            pe.wait_ge(sq_added, 9 * 4 - 1)
            pe.wait_ge(sq_made, 8 * 4)
            for b in range(NB + 1):
                n = P if b < NB else TS
                for i, src in enumerate((ssq, sq)):
                    ins = pe.matmul(ps[0:n, STAT_BANK[4], b:b + 1], src[:, b * P:b * P + n], ones[:, 0:1],
                                    start=i == 0, stop=i == 1)
            ins.then_inc(stat_summed, 1)
            pe.wait_ge(sums_taken, 1)
            turn_back(2, range(KD)).then_inc(y_turned, 1)
            pe.wait_ge(ys_taken, 1)
            turn_back(3, range(KD)).then_inc(y_turned, 1)


_INS = ["x_prompt", "x_sample", "cache_k_win", "cache_v_win", "p_prompt", "p_sample", "g_ffn1", "w1_ffn1", "w3_ffn1",
        "w2_ffn1", "g_mix", "w_in", "b_in", "attn_sinks", "gm_ln_g", "gm_ln_b", "gm_w_s", "gm_b_s", "w_out", "b_out",
        "g_ffn2", "w1_ffn2", "w3_ffn2", "w2_ffn2", "g_ple", "w_ple_gate", "w_ple_proj", "g_final"]
_OUTS = [("y_prompt", (1, TP, D)), ("y_sample", (TS, 1, D)), ("k_win_prompt", (1, 1, W, NKV, HD)),
         ("v_win_prompt", (1, 1, W, NKV, HD)), ("k_win_sample", (1, TS, W, NKV, HD)),
         ("v_win_sample", (1, TS, W, NKV, HD)), ("gm_v_prompt", (1, 1, W, GM)), ("gm_v_sample", (1, TS, 1, GM))]


def kernel(**inputs):
    import numpy as _np
    import concourse.bacc as _bacc
    from concourse import mybir as _mybir
    from concourse.bass_utils import run_bass_kernel_spmd as _run

    nc = _bacc.Bacc("TRN2", target_bir_lowering=False, num_devices=1)
    arrays, ins, outs = {}, {}, {}
    for name in _INS:
        arr = _np.ascontiguousarray(inputs[name])
        arrays[f"in_{name}_dram"] = arr
        ins[name] = nc.dram_tensor(f"in_{name}_dram", arr.shape, _mybir.dt.from_np(arr.dtype),
                                   kind="ExternalInput").ap()
    for name, shape in _OUTS:
        outs[name] = nc.dram_tensor(f"out_{name}_dram", shape, _mybir.dt.float32, kind="ExternalOutput").ap()
    hybrid_decoder_layer(nc, ins, outs)
    r = _run(nc, [arrays], core_ids=[0])
    return tuple(r.results[0][f"out_{name}_dram"] for name, _ in _OUTS)
```
